# Optimizing a Trainium2 kernel written in Bass

```python
import jax, jax.numpy as jnp
from jax import lax
import numpy as np

D_MODEL = 1024
BATCH = 1
SEQ = 512
DEPTH = 2
DEC_BATCH = 8
DEC_SEQ = 8
PAST_LEN = 4096
PAGE_SIZE = 128

N_A_LAYERS = DEPTH // 2
N_B_LAYERS = DEPTH - N_A_LAYERS
D_RNN = D_MODEL
RG_BLOCKS = 8
RG_BLOCK_W = D_RNN // RG_BLOCKS
CONV_W = 4
RG_C = 8.0
HEAD_DIM = 64
N_HEADS = D_MODEL // HEAD_DIM
N_KV_HEADS = 4
GROUP = N_HEADS // N_KV_HEADS
WINDOW = 128
ROPE_THETA = 10000.0
N_KEYS = 128
N_EXPERTS = N_KEYS * N_KEYS
PEER_HEADS = 8
PEER_TOPK = 16
D_KEY = 256
PEER_CHUNK = 128
EPS = 1e-6

kernel_name = 'yoco_rglru_swa_sink_peer_step'

def rmsnorm(x, g):
    xf = x.astype(jnp.float32)
    y = xf * lax.rsqrt(jnp.mean(xf * xf, axis=-1, keepdims=True) + EPS)
    return (y * g.astype(jnp.float32)).astype(x.dtype)

def rope(x, pos):
    half = HEAD_DIM // 2
    inv = ROPE_THETA ** (-jnp.arange(half, dtype=jnp.float32) / half)
    ang = pos.astype(jnp.float32)[:, None] * inv[None, :]
    cos = jnp.cos(ang)[:, None, :]
    sin = jnp.sin(ang)[:, None, :]
    xf = x.astype(jnp.float32)
    x1, x2 = xf[..., :half], xf[..., half:]
    return jnp.concatenate([x1 * cos - x2 * sin, x2 * cos + x1 * sin], axis=-1).astype(x.dtype)

def causal_conv(x, buf, w, b):
    xp = jnp.concatenate([buf.astype(x.dtype), x], axis=1)
    t = x.shape[1]
    y = b
    for k in range(CONV_W):
        y = y + w[k] * xp[:, k:k + t]
    return y, xp[:, -(CONV_W - 1):]

def block_diag(x, w, b):
    xb = x.reshape(x.shape[:-1] + (RG_BLOCKS, RG_BLOCK_W))
    return jnp.einsum('btnc,ncd->btnd', xb, w).reshape(x.shape) + b

def rg_lru(x, h0, wa, ba, wx, bx, lam):
    f32 = jnp.float32
    r = jax.nn.sigmoid(block_diag(x, wa, ba).astype(f32))
    i = jax.nn.sigmoid(block_diag(x, wx, bx).astype(f32))
    log_a = -RG_C * r * jax.nn.softplus(-lam.astype(f32))
    a = jnp.exp(log_a)
    mult = jnp.sqrt(-jnp.expm1(2.0 * log_a))
    bterm = mult * i * x.astype(f32)
    bterm = bterm.at[:, 0].add(a[:, 0] * h0.astype(f32))

    def comb(lhs, rhs):
        a1, b1 = lhs
        a2, b2 = rhs
        return a1 * a2, a2 * b1 + b2

    _, h = lax.associative_scan(comb, (a, bterm), axis=1)
    return h.astype(x.dtype), h[:, -1].astype(x.dtype)

def recurrent_block(xn, conv_buf, h0, w_in, conv_w, conv_b, wa, ba, wx, bx, lam, w_out):
    proj = xn @ w_in
    gate = jax.nn.gelu(proj[..., :D_RNN], approximate=True)
    xc, new_buf = causal_conv(proj[..., D_RNN:], conv_buf, conv_w, conv_b)
    h, h_last = rg_lru(xc, h0, wa, ba, wx, bx, lam)
    return (h * gate) @ w_out, new_buf, h_last

def sink_softmax(s, mask, sink):
    s = jnp.where(mask, s, -jnp.inf)
    m = jnp.maximum(jnp.max(s, axis=-1, keepdims=True), sink)
    p = jnp.exp(s - m)
    return p / (jnp.sum(p, axis=-1, keepdims=True) + jnp.exp(sink - m))

def swa_prompt(q, k, v, sinks):
    b, t = q.shape[:2]
    c = WINDOW
    nb = t // c
    scale = HEAD_DIM ** -0.5
    qb = q.reshape(b, nb, c, N_KV_HEADS, GROUP, HEAD_DIM)
    pad = jnp.zeros((b, c, N_KV_HEADS, HEAD_DIM), k.dtype)
    kblk = jnp.concatenate([pad, k], axis=1).reshape(b, nb + 1, c, N_KV_HEADS, HEAD_DIM)
    vblk = jnp.concatenate([pad, v], axis=1).reshape(b, nb + 1, c, N_KV_HEADS, HEAD_DIM)
    kb = jnp.concatenate([kblk[:, :-1], kblk[:, 1:]], axis=2)
    vb = jnp.concatenate([vblk[:, :-1], vblk[:, 1:]], axis=2)
    blk = jnp.arange(nb)[:, None, None]
    qpos = blk * c + jnp.arange(c)[None, :, None]
    kpos = (blk - 1) * c + jnp.arange(2 * c)[None, None, :]
    mask = (kpos >= 0) & (kpos <= qpos) & (qpos - kpos < WINDOW)
    s = jnp.einsum('bnqkgd,bnskd->bnkgqs', qb, kb).astype(jnp.float32) * scale
    sink = sinks.astype(jnp.float32).reshape(N_KV_HEADS, GROUP, 1, 1)
    p = sink_softmax(s, mask[None, :, None, None], sink)
    o = jnp.einsum('bnkgqs,bnskd->bnqkgd', p.astype(v.dtype), vb)
    return o.reshape(b, t, N_HEADS * HEAD_DIM)

def swa_sample(q, kall, vall, qpos, kpos, sinks):
    b, nq = q.shape[:2]
    scale = HEAD_DIM ** -0.5
    qg = q.reshape(b, nq, N_KV_HEADS, GROUP, HEAD_DIM)
    mask = (kpos[None, :] <= qpos[:, None]) & (qpos[:, None] - kpos[None, :] < WINDOW)
    s = jnp.einsum('bqkgd,bskd->bkgqs', qg, kall).astype(jnp.float32) * scale
    sink = sinks.astype(jnp.float32).reshape(N_KV_HEADS, GROUP, 1, 1)
    p = sink_softmax(s, mask, sink)
    o = jnp.einsum('bkgqs,bskd->bqkgd', p.astype(vall.dtype), vall)
    return o.reshape(b, nq, N_HEADS * HEAD_DIM)

def peer(xn, wq, subkeys, u, v):
    shp = xn.shape
    xt = xn.reshape(-1, D_MODEL)
    t = xt.shape[0]
    q = (xt @ wq).reshape(t, PEER_HEADS, 2, D_KEY // 2)
    s = jnp.einsum('thpc,pnc->thpn', q, subkeys).astype(jnp.float32)
    sv, si = lax.top_k(s, PEER_TOPK)
    cand = sv[:, :, 0, :, None] + sv[:, :, 1, None, :]
    cv, ci = lax.top_k(cand.reshape(t, PEER_HEADS, PEER_TOPK * PEER_TOPK), PEER_TOPK)
    ia = jnp.take_along_axis(si[:, :, 0], ci // PEER_TOPK, axis=-1)
    ib = jnp.take_along_axis(si[:, :, 1], ci % PEER_TOPK, axis=-1)
    eidx = ia * N_KEYS + ib
    gate = jax.nn.softmax(cv, axis=-1).astype(xt.dtype)
    npad = (-t) % PEER_CHUNK
    nc = (t + npad) // PEER_CHUNK
    xp = jnp.pad(xt, ((0, npad), (0, 0))).reshape(nc, PEER_CHUNK, D_MODEL)
    ep = jnp.pad(eidx, ((0, npad), (0, 0), (0, 0))).reshape(nc, PEER_CHUNK, PEER_HEADS, PEER_TOPK)
    gp = jnp.pad(gate, ((0, npad), (0, 0), (0, 0))).reshape(nc, PEER_CHUNK, PEER_HEADS, PEER_TOPK)

    def chunk(args):
        xc, ec, gc = args
        hc = jax.nn.gelu(jnp.einsum('chkd,cd->chk', u[ec], xc), approximate=False)
        return jnp.einsum('chk,chkd->cd', hc * gc, v[ec])

    out = lax.map(chunk, (xp, ep, gp))
    return out.reshape(-1, D_MODEL)[:t].reshape(shp)

def trunk(x, pos, is_prompt, conv_states, h_states, kbuf, vbuf, w):
    b, t = x.shape[:2]
    new_conv, new_h = [], []
    k_new = v_new = None
    kall = vall = kpos = None
    for layer in range(DEPTH):
        if layer < N_A_LAYERS:
            a = layer
            if is_prompt:
                cb = jnp.zeros((b, CONV_W - 1, D_RNN), x.dtype)
                h0 = jnp.zeros((b, D_RNN), x.dtype)
            else:
                cb = conv_states[a]
                h0 = h_states[a]
            y, cb_new, h_last = recurrent_block(
                rmsnorm(x, w['rg_norm'][a]), cb, h0, w['rg_w_in'][a], w['rg_conv_w'][a],
                w['rg_conv_b'][a], w['rg_wa'][a], w['rg_ba'][a], w['rg_wx'][a], w['rg_bx'][a],
                w['rg_lambda'][a], w['rg_w_out'][a])
            x = x + y
            new_conv.append(cb_new)
            new_h.append(h_last)
        else:
            bi = layer - N_A_LAYERS
            if bi == 0:
                kv = (rmsnorm(x, w['kv_norm']) @ w['w_kv']).reshape(b, t, 2, N_KV_HEADS, HEAD_DIM)
                k = rope(kv[:, :, 0], pos)
                v = kv[:, :, 1]
                if is_prompt:
                    k_new, v_new = k[:, -WINDOW:], v[:, -WINDOW:]
                else:
                    kall = jnp.concatenate([kbuf.astype(k.dtype), k], axis=1)
                    vall = jnp.concatenate([vbuf.astype(v.dtype), v], axis=1)
                    kpos = jnp.concatenate([PAST_LEN - WINDOW + jnp.arange(WINDOW), pos])
                    k_new, v_new = kall[:, -WINDOW:], vall[:, -WINDOW:]
            q = rope((rmsnorm(x, w['attn_norm'][bi]) @ w['w_q'][bi]).reshape(b, t, N_HEADS, HEAD_DIM), pos)
            if is_prompt:
                o = swa_prompt(q, k, v, w['sinks'][bi])
            else:
                o = swa_sample(q, kall, vall, pos, kpos, w['sinks'][bi])
            x = x + o @ w['w_o'][bi]
        x = x + peer(rmsnorm(x, w['ffn_norm'][layer]), w['peer_wq'][layer], w['peer_subkeys'][layer],
                     w['peer_u'][layer], w['peer_v'][layer])
    return rmsnorm(x, w['final_norm']), jnp.stack(new_conv), jnp.stack(new_h), k_new, v_new

def setup_inputs(seed: int = 0) -> dict:
    key = jax.random.key(seed)
    ks = jax.random.split(key, 32)
    f32 = jnp.float32

    def nrm(k, shape, scale):
        return jax.random.normal(k, shape, f32) * scale

    def gain(k, shape):
        return 1.0 + 0.02 * jax.random.normal(k, shape, f32)

    na, nb = N_A_LAYERS, N_B_LAYERS
    a0 = jax.random.uniform(ks[10], (na, D_RNN), f32, 0.9, 0.999)
    return {
        'x_prompt': nrm(ks[0], (BATCH, SEQ, D_MODEL), 1.0),
        'x_sample': nrm(ks[1], (DEC_BATCH, DEC_SEQ, D_MODEL), 1.0),
        'state_conv': nrm(ks[2], (na, DEC_BATCH, CONV_W - 1, D_RNN), 1.0),
        'state_h': nrm(ks[3], (na, DEC_BATCH, D_RNN), 0.5),
        'cache_k': nrm(ks[4], (DEC_BATCH, WINDOW, N_KV_HEADS, HEAD_DIM), 1.0),
        'cache_v': nrm(ks[5], (DEC_BATCH, WINDOW, N_KV_HEADS, HEAD_DIM), 1.0),
        'rg_norm': gain(ks[6], (na, D_MODEL)),
        'rg_w_in': nrm(ks[7], (na, D_MODEL, 2 * D_RNN), D_MODEL ** -0.5),
        'rg_conv_w': nrm(ks[8], (na, CONV_W, D_RNN), CONV_W ** -0.5),
        'rg_conv_b': nrm(ks[9], (na, D_RNN), 0.02),
        'rg_wa': nrm(ks[11], (na, RG_BLOCKS, RG_BLOCK_W, RG_BLOCK_W), RG_BLOCK_W ** -0.5),
        'rg_ba': nrm(ks[12], (na, D_RNN), 0.02),
        'rg_wx': nrm(ks[13], (na, RG_BLOCKS, RG_BLOCK_W, RG_BLOCK_W), RG_BLOCK_W ** -0.5),
        'rg_bx': nrm(ks[14], (na, D_RNN), 0.02),
        'rg_lambda': jnp.log(a0) - jnp.log1p(-a0),
        'rg_w_out': nrm(ks[15], (na, D_RNN, D_MODEL), D_RNN ** -0.5),
        'kv_norm': gain(ks[16], (D_MODEL,)),
        'w_kv': nrm(ks[17], (D_MODEL, 2 * N_KV_HEADS * HEAD_DIM), D_MODEL ** -0.5),
        'attn_norm': gain(ks[18], (nb, D_MODEL)),
        'w_q': nrm(ks[19], (nb, D_MODEL, N_HEADS * HEAD_DIM), D_MODEL ** -0.5),
        'sinks': nrm(ks[20], (nb, N_HEADS), 1.0),
        'w_o': nrm(ks[21], (nb, N_HEADS * HEAD_DIM, D_MODEL), (N_HEADS * HEAD_DIM) ** -0.5),
        'ffn_norm': gain(ks[22], (DEPTH, D_MODEL)),
        'peer_wq': nrm(ks[23], (DEPTH, D_MODEL, PEER_HEADS * D_KEY), D_MODEL ** -0.5),
        'peer_subkeys': nrm(ks[24], (DEPTH, 2, N_KEYS, D_KEY // 2), (D_KEY // 2) ** -0.5),
        'peer_u': nrm(ks[25], (DEPTH, N_EXPERTS, D_MODEL), D_MODEL ** -0.5),
        'peer_v': nrm(ks[26], (DEPTH, N_EXPERTS, D_MODEL), 0.1),
        'final_norm': gain(ks[27], (D_MODEL,)),
    }

def reference(x_prompt, x_sample, state_conv, state_h, cache_k, cache_v,
              rg_norm, rg_w_in, rg_conv_w, rg_conv_b, rg_wa, rg_ba, rg_wx, rg_bx, rg_lambda, rg_w_out,
              kv_norm, w_kv, attn_norm, w_q, sinks, w_o,
              ffn_norm, peer_wq, peer_subkeys, peer_u, peer_v, final_norm):
    w = dict(rg_norm=rg_norm, rg_w_in=rg_w_in, rg_conv_w=rg_conv_w, rg_conv_b=rg_conv_b,
             rg_wa=rg_wa, rg_ba=rg_ba, rg_wx=rg_wx, rg_bx=rg_bx, rg_lambda=rg_lambda,
             rg_w_out=rg_w_out, kv_norm=kv_norm, w_kv=w_kv, attn_norm=attn_norm, w_q=w_q,
             sinks=sinks, w_o=w_o, ffn_norm=ffn_norm, peer_wq=peer_wq,
             peer_subkeys=peer_subkeys, peer_u=peer_u, peer_v=peer_v, final_norm=final_norm)
    pos_p = jnp.arange(x_prompt.shape[1])
    y_prompt, conv_p, h_p, k_p, v_p = trunk(x_prompt, pos_p, True, None, None, None, None, w)
    pos_s = PAST_LEN + jnp.arange(x_sample.shape[1])
    y_sample, conv_s, h_s, k_s, v_s = trunk(x_sample, pos_s, False, state_conv, state_h,
                                            cache_k, cache_v, w)
    return (y_prompt, y_sample, conv_p, h_p, k_p, v_p, conv_s, h_s, k_s, v_s)


_drawn_inputs = setup_inputs


def setup_inputs(seed=0):
    import zlib

    import numpy as np

    out = dict(_drawn_inputs(seed))
    spreads = {}
    factors = {'rg_ba': 8.0,
     'rg_bx': 7.859,
     'kv_norm': 2.856,
     'attn_norm': 8.0,
     'sinks': 12.006,
     'ffn_norm': 5.47,
     'final_norm': 9.624}
    for name, (base, spread) in spreads.items():
        noise = np.random.default_rng([zlib.crc32(name.encode()), seed]).standard_normal(out[name].shape)
        drawn = base * np.exp(spread * noise) if base else spread * noise
        out[name] = __import__('jax').numpy.asarray(drawn.astype(out[name].dtype))
    for name, factor in factors.items():
        out[name] = (out[name] * factor).astype(out[name].dtype)
    return out
```

```python
from contextlib import ExitStack

import concourse.bass as bass
from concourse import mybir

F32 = mybir.dt.float32
F32R = mybir.dt.float32r
U32 = mybir.dt.uint32
ALU = mybir.AluOpType
ACT = mybir.ActivationFunctionType
X = mybir.AxisListType.X

P = 128
D = 1024
NC = D // P
TP, NB, TS = 512, 8, 8
T = TP + NB * TS
H2 = T // 2
TT = -(-T // P)
TPAD = TT * P
CW = 4
NH, NKV, HD = 16, 4, 64
GRP = NH // NKV
WIN = 128
NQB = TP // WIN
PH, TOPK = 8, 16
NS = PH * TOPK
KEYS = 128
RING = 4
GB = 96
NGB = T // GB
EPS = 1e-6
BIG = -3.0e38

C_ID, C_IOTA, C_COS = 0, P, 2 * P
C_SIN = C_COS + T
C_MP = C_SIN + T
C_MS = C_MP + 2 * WIN
C_N = C_MS + WIN + TS
(N_RG, N_F0, N_KV, N_AT, N_F1, N_FIN) = (NC * i for i in range(6))
P_CW = 6 * NC
P_CB = P_CW + CW * NC
P_BA = P_CB + NC
P_BX = P_BA + NC
P_LAM = P_BX + NC
P_H0 = P_LAM + NC
P_SINK = P_H0 + NC * NB
P_SKS = P_SINK + NH
P_SK = P_SKS + 1
P_N = P_SK + 4 * KEYS

W_IN, W_A, W_X, W_OUT, W_PQ0, W_K, W_Q, W_O, W_PQ1, W_N = 0, 16, 17, 18, 26, 42, 44, 52, 60, 76
D_IN, D_A, D_X, D_OUT, D_PQ0, D_K, D_Q, D_O, D_PQ1, D_N = 0, 16, 24, 32, 40, 56, 58, 66, 74, 90


def tiles_made(w):
    if w < W_A:
        return w + 1
    if w in (W_A, W_X):
        return D_A + NC * (w - W_A + 1)
    return w + 1 + 2 * (NC - 1)


class Chain:

    def __init__(self, eng, sem):
        self.eng, self.sem, self.n = eng, sem, 0

    def did(self, ins):
        ins.then_inc(self.sem, 1)
        self.n += 1

    def settle(self):
        self.eng.wait_ge(self.sem, self.n)


def decoder(nc, xin, consts, params, wts, wv, stconv, kcT, kc, vc, uT, v,
            yT, convP, hOut, kNew, vNewP, vNewS, kKeep, vKeep, convS, gate_dram):
    with ExitStack() as ctx:
        def sb(name, shape, dt=F32, st=ctx):
            return st.enter_context(nc.sbuf_tensor(name, shape, dt))

        sems = {}

        def sem(name):
            if name not in sems:
                sems[name] = ctx.enter_context(nc.semaphore(name))
            return sems[name]

        ps = ctx.enter_context(nc.psum_tensor("ps", [P, 8, 512], F32))

        xT = sb("xT", [P, NC, T])
        xn = sb("xn", [P, NC, T])
        cst = sb("cst", [P, C_N])
        prm = sb("prm", [P, P_N])
        wring = sb("wring", [P, RING, NC, P])
        rinv = sb("rinv", [P, T])
        ones = sb("ones", [P, P])
        slotT = sb("slotT", [P, 3, TPAD])
        ident = cst[:, C_ID:C_ID + P]
        iota = cst[:, C_IOTA:C_IOTA + P]

        with ExitStack() as st:
            gate = sb("gate", [P, NC, T], st=st)
            xpre = sb("xpre", [P, NC, TP + CW - 1], st=st)
            xpreS = sb("xpreS", [P, NC, NB, TS + CW - 1], st=st)
            xc = sb("xc", [P, NC, T], st=st)
            rg = sb("rg", [P, NC, T], st=st)
            ig = sb("ig", [P, NC, T], st=st)
            dec = sb("dec", [P, NC, T], st=st)
            sp = sb("sp", [P, 4, NC], st=st)
            ah0 = sb("ah0", [P, NC, NB], st=st)
            hlast = sb("hlast", [P, NC, 1 + NB], st=st)
        with ExitStack() as st:
            qT = sb("qT", [P, 2 * PH, TPAD], st=st)
            sc = sb("sc", [P, 2 * PH, KEYS], st=st)
            sc2 = sb("sc2", [P, 2 * PH, KEYS], st=st)
            sv = sb("sv", [P, 2 * PH, TOPK], st=st)
            si = sb("si", [P, 2 * PH, TOPK], U32, st=st)
            sif = sb("sif", [P, 2 * PH, TOPK], st=st)
            cand = sb("cand", [P, PH, TOPK * TOPK], st=st)
            cand2 = sb("cand2", [P, PH, TOPK * TOPK], st=st)
            cv = sb("cv", [P, PH, TOPK], st=st)
            ci = sb("ci", [P, PH, TOPK], U32, st=st)
            cab = sb("cab", [P, 2, PH, TOPK], U32, st=st)
            cabf = sb("cabf", [P, 2, PH, TOPK], st=st)
            ex = sb("ex", [P, PH, TOPK], st=st)
            exs = sb("exs", [P, 2, PH], st=st)
            slot = sb("slot", [P, 3, NS], st=st)
        with ExitStack() as st:
            hotA = sb("hotA", [P, 16, KEYS], st=st)
            hotB = sb("hotB", [P, 16, KEYS], st=st)
            gblk = sb("gblk", [P, 2, KEYS, GB], st=st)
        with ExitStack() as st:
            xh = sb("xh", [P, NC, T], F32R, st=st)
            xl = sb("xl", [P, NC, T], F32R, st=st)
            uraw = sb("uraw", [P, 2, NC, P], st=st)
            uh = sb("uh", [P, 2, NC, P], F32R, st=st)
            ul = sb("ul", [P, 2, NC, P], F32R, st=st)
            vraw = sb("vraw", [P, 2, D], st=st)
            vh = sb("vh", [P, 4, D], F32R, st=st)
            vl = sb("vl", [P, 4, D], F32R, st=st)
            gt = sb("gt", [P, 2, NGB, 2, GB], st=st)
            hg = sb("hg", [P, 2, T], st=st)
            hh = sb("hh", [P, 4, T], F32R, st=st)
            hl = sb("hl", [P, 4, T], F32R, st=st)
        with ExitStack() as st:
            qR = sb("qR", [HD, NH, T], st=st)
            kR = sb("kR", [HD, NKV, T], st=st)
            qS = sb("qS", [HD, NB, NH, TS], st=st)
            rot = sb("rot", [P, 2, T], st=st)
            rc = sb("rc", [P, 2, T], st=st)
            wv_sb = sb("wv_sb", [P, NC, NKV * HD], st=st)
            vtok = sb("vtok", [P, TT, NKV * HD], st=st)
            vnew = sb("vnew", [TS, NB, NKV * HD], st=st)
            kc_sb = sb("kc_sb", [HD, NB, NKV, WIN], st=st)
            vc_sb = sb("vc_sb", [P, NB, NKV * HD], st=st)
            pr = sb("pr", [P, GRP, 2 * WIN], st=st)
            prT = sb("prT", [P, 2 * GRP, P], st=st)
            pss = sb("pss", [P, NB, WIN + TS], st=st)
            pssT = sb("pssT", [P, NB, P], st=st)
            pssN = sb("pssN", [TS, NB, P], st=st)
            sm = sb("sm", [P, 6, NB], st=st)

        def halves(lo):
            return ps[:, lo:lo + 2, 0:H2]

        def two(ap):
            return ap.rearrange("p (h t) -> p h t", h=2)

        def dbank(d):
            return 2 * (d % 2)

        block = ctx.enter_context(nc.Block())

        @block.sync
        def _(spq):
            spq.dma_start(xT[:, :, :], xin).then_inc(sem("x_loaded"), 16)
            spq.dma_start(cst[:, :], consts).then_inc(sem("consts_loaded"), 16)
            spq.dma_start(prm[:, :], params).then_inc(sem("consts_loaded"), 16)

            def load_weights(lo, hi):
                for w in range(lo, hi):
                    if w >= RING:
                        spq.wait_ge(sem("tile_done"), tiles_made(w - RING))
                    spq.dma_start(wring[:, w % RING], wts[w]).then_inc(sem(f"w_loaded{w % RING}"), 16)

            def store_gates(l):
                for b in range(NGB):
                    spq.wait_ge(sem(f"g_copied{l}"), GB // 4 * (b + 1))
                    spq.dma_start(gate_dram[l, b], gblk[:, b % 2]).then_inc(sem(f"g_stored{l}_{b % 2}"), 16)
                for h in range(2):
                    spq.wait_ge(sem(f"g_stored{l}_{h}"), 16 * NGB // 2)

            def load_experts(l):
                def pair(it, first):
                    for j in range(2):
                        g = 2 * it + j
                        for i in range(2):
                            n = 2 * g + i
                            if not (first and j == 0):
                                spq.wait_ge(sem(f"u_split{l}"), n - 1)
                            spq.dma_start(uraw[:, i], tile_of(uT[l], n)).then_inc(sem(f"u_loaded{l}_{i}"), 16)
                        if not first:
                            spq.wait_ge(sem(f"h_mul{l}"), 2 * g - 2)
                        spq.dma_start(gt[:, j].rearrange("p b a t -> p b (a t)"),
                                      gates_of(l, g)).then_inc(sem(f"gt_loaded{l}_{j}"), 16)
                        for i in range(2):
                            n = 2 * g + i
                            if not (first and j == 0):
                                spq.wait_ge(sem(f"v_split{l}"), n - 1)
                            spq.dma_start(vraw[:, i], tile_of(v[l], n)).then_inc(sem(f"v_loaded{l}_{i}"), 16)

                pair(0, True)
                with spq.Fori(1, KEYS // 4) as it:
                    pair(it, False)

            def tile_of(ap, n):
                if isinstance(n, int):
                    return ap[n]
                return ap[bass.ds(n, 1)].rearrange("o p n -> (o p) n")

            def gates_of(l, g):
                src = gate_dram[l].rearrange("b p (g n) -> p b g n", n=2 * GB)
                if isinstance(g, int):
                    return src[:, :, g]
                return src[:, :, bass.ds(g, 1)].rearrange("p b o n -> p b (o n)")

            load_weights(0, W_PQ0)
            spq.wait_ge(sem("pre_copied"), NC)
            spq.wait_ge(sem("d_free"), D_A)
            spq.dma_start(convP, xpre[:, :, TP:TP + CW - 1]).then_inc(sem("states_out"), 16)
            spq.dma_start(convS, xpreS[:, :, :, TS:TS + CW - 1].rearrange("p c b k -> p (c b) k")
                          ).then_inc(sem("states_out"), 16)
            spq.wait_ge(sem("hlast_ready"), 1)
            spq.dma_start(hOut, hlast[:, :, :]).then_inc(sem("states_out"), 16)
            load_weights(W_PQ0, W_K)
            store_gates(0)
            load_experts(0)
            spq.wait_ge(sem("x_ready"), 2)
            spq.dma_start(wv_sb[:, :, :], wv).then_inc(sem("wv_loaded"), 16)
            spq.dma_start(kc_sb[:, :, :, :], kcT).then_inc(sem("kc_loaded"), 16)
            spq.dma_start(vc_sb[:, :, :], vc).then_inc(sem("vc_loaded"), 16)
            load_weights(W_K, W_Q)
            spq.wait_ge(sem("v_ready"), 1)
            spq.dma_start(vNewP, vtok[:, NQB - 1]).then_inc(sem("out_done"), 16)
            spq.dma_start(vNewS, vtok[0:NB * TS, NQB]).then_inc(sem("out_done"), 16)
            for b in range(NB):
                spq.dma_start(vnew[:, b], vtok[b * TS:(b + 1) * TS, NQB]).then_inc(sem("vnew_loaded"), 16)
            spq.wait_ge(sem("k_ready"), 2)
            spq.dma_start(kNew, kR[:, :, TP - WIN:T]).then_inc(sem("out_done"), 16)
            load_weights(W_Q, W_N)
            store_gates(1)
            load_experts(1)
            spq.wait_ge(sem("xn_ready"), 6)
            spq.dma_start(yT, xn[:, :, :]).then_inc(sem("out_done"), 16)
            spq.wait_ge(sem("states_out"), 48)
            spq.wait_ge(sem("out_done"), 16 * 4)

        @block.gpsimd
        def _(pool):
            pool.memset(ones[:, :], 1.0).then_inc(sem("ones_ready"), 1)
            pool.memset(xpre[:, :, 0:CW - 1], 0.0).then_inc(sem("pad_ready"), 1)
            pool.dma_start(xpreS[:, :, :, 0:CW - 1].rearrange("p c b k -> p (c b) k"), stconv
                           ).then_inc(sem("st_loaded"), 16)
            pool.dma_start(kKeep, kc[:, TS:WIN]).then_inc(sem("kept"), 16)
            pool.dma_start(vKeep, vc.rearrange("p b n -> b p n")[:, TS:WIN]).then_inc(sem("kept"), 16)
            pool.wait_ge(sem("kept"), 32)

        @block.scalar
        def _(act):
            chain = Chain(act, sem("act_chain"))

            def square(s):
                act.wait_ge(sem("x_ready" if s else "x_loaded"), s if s else 16)
                if s:
                    act.wait_ge(sem("tile_done"), (0, D_PQ0, D_K, D_PQ1, D_N)[s])
                for c in range(NC):
                    act.activation(xn[:, c], xT[:, c], ACT.Square).then_inc(sem("sq_ready"), 1)
                act.wait_ge(sem("ms_ready"), s + 1)
                act.activation(rinv[:, :], rinv[:, :], ACT.Sqrt).then_inc(sem("rms_ready"), 1)

            def split_x(l):
                act.wait_ge(sem("xn_ready"), (2, 5)[l])
                act.wait_ge(sem(f"g_stored{l}_0"), 16 * NGB // 2)
                act.wait_ge(sem(f"g_stored{l}_1"), 16 * NGB // 2)
                for c in range(NC):
                    act.activation(xh[:, c], xn[:, c], ACT.Copy).then_inc(sem(f"xh_ready{l}"), 1)

            def rg_lru():
                act.wait_ge(sem("consts_loaded"), 32)
                act.activation(sp[:, 0], prm[:, P_LAM:P_LAM + NC], ACT.Exp, scale=-1.0
                               ).then_inc(sem("lam_exp"), 1)
                act.wait_ge(sem("lam_one"), 1)
                act.activation(sp[:, 2], sp[:, 1], ACT.Ln).then_inc(sem("lam_ln"), 1)
                square(0)
                for f in range(NC):
                    act.wait_ge(sem("tile_done"), D_IN + f + 1)
                    act.activation(two(gate[:, f]), halves(dbank(f)), ACT.Gelu_apprx_tanh
                                   ).then_inc(sem("d_free"), 1)
                act.wait_ge(sem("pad_ready"), 1)
                act.wait_ge(sem("st_loaded"), 16)
                for f in range(NC):
                    d = D_IN + NC + f
                    b = dbank(d)
                    act.wait_ge(sem("tile_done"), d + 1)
                    act.activation(xpre[:, f, CW - 1:CW - 1 + H2], ps[:, b, 0:H2], ACT.Copy)
                    act.activation(xpre[:, f, CW - 1 + H2:CW - 1 + TP], ps[:, b + 1, 0:TP - H2], ACT.Copy
                                   ).then_inc(sem("pre_copied"), 1)
                    act.activation(xpreS[:, f, :, CW - 1:],
                                   ps[:, b + 1, TP - H2:H2].rearrange("p (b s) -> p b s", b=NB),
                                   ACT.Copy).then_inc(sem("d_free"), 1)
                for k, (d0, dst, bias) in enumerate(((D_A, rg, P_BA), (D_X, ig, P_BX))):
                    for f in range(NC):
                        act.wait_ge(sem("tile_done"), d0 + f + 1)
                        act.activation(two(dst[:, f]), halves(dbank(d0 + f)), ACT.Sigmoid,
                                       bias=prm[:, bias + f:bias + f + 1]).then_inc(sem("d_free"), 1)
                act.wait_ge(sem("d_free"), D_OUT)
                act.wait_ge(sem("sp_ready"), 1)
                for f in range(NC):
                    act.activation(dec[:, f], rg[:, f], ACT.Exp, scale=sp[:, 3, f:f + 1]
                                   ).then_inc(sem("dec_ready"), 1)
                act.wait_ge(sem("dec_ready"), NC)
                for f in range(NC):
                    act.activation(rg[:, f], rg[:, f], ACT.Tanh, scale=sp[:, 3, f:f + 1]
                                   ).then_inc(sem("tanh_ready"), 1)
                for f in range(NC):
                    act.wait_ge(sem("m2_ready"), f + 1)
                    act.activation(rg[:, f], rg[:, f], ACT.Sqrt).then_inc(sem("mult_ready"), 1)

            def copy_queries(d0):
                for f in range(2 * PH):
                    act.wait_ge(sem("tile_done"), d0 + f + 1)
                    act.activation(two(qT[:, f, 0:T]), halves(dbank(d0 + f)), ACT.Copy
                                   ).then_inc(sem("d_free"), 1)

            def topk(l):
                def copy_scores(t):
                    act.wait_ge(sem(f"sc_done{l}"), t + 1)
                    if t:
                        act.wait_ge(sem(f"sc_read{l}"), t)
                    act.activation(sc[:, :, :].rearrange("p (b j) k -> p b (j k)", b=4), ps[:, 4:8, :],
                                   ACT.Copy).then_inc(sem(f"sc_copied{l}"), 1)

                copy_scores(0)
                for t in range(TT):
                    if t + 1 < TT:
                        copy_scores(t + 1)
                    act.wait_ge(sem(f"ex_in{l}"), t + 1)
                    act.activation(ex[:, :, :], ex[:, :, :], ACT.Exp).then_inc(sem(f"ex_out{l}"), 1)
                    act.wait_ge(sem(f"turned{l}"), t + 1)
                    act.activation(slotT[:, :, t * P:(t + 1) * P],
                                   ps[:, 0, 0:3 * P].rearrange("p (a t) -> p a t", a=3),
                                   ACT.Copy).then_inc(sem(f"slot_ready{l}"), 1)

            def copy_gates(l):
                for b in range(NGB):
                    if b >= 2:
                        act.wait_ge(sem(f"g_stored{l}_{b % 2}"), 16 * (b // 2))
                    with act.Fori(0, GB // 16) as it:
                        for q in range(4):
                            act.wait_ge(sem(f"g_done{l}"), it * 4 + (b * (GB // 4) + q + 1))
                            act.activation(
                                gblk[:, b % 2, :, bass.ds(it * 16 + 4 * q, 4)],
                                ps[:, q, :].rearrange("p (t k) -> p k t", t=4),
                                ACT.Copy).then_inc(sem(f"g_copied{l}"), 1)

            def experts(l):
                def step(it, j, first, last):
                    g = 2 * it + j
                    if not last:
                        for i in range(2):
                            n = 2 * g + 2 + i
                            act.wait_ge(sem(f"u_loaded{l}_{i}"), 16 * g + 32)
                            act.wait_ge(sem(f"s_full{l}"), n - 1)
                            act.activation(uh[:, i], uraw[:, i], ACT.Copy).then_inc(sem(f"uh_ready{l}"), 1)
                    for i in range(2):
                        n = 2 * g + i
                        act.wait_ge(sem(f"s_full{l}"), n + 1)
                        if not first or j:
                            act.wait_ge(sem(f"h_split{l}"), n - 1)
                        act.activation(two(hg[:, i]), halves(2 * i), ACT.Gelu).then_inc(sem(f"s_free{l}"), 1)
                    for i in range(2):
                        act.wait_ge(sem(f"v_loaded{l}_{i}"), 16 * g + 16)
                        if not first:
                            act.wait_ge(sem(f"o_full{l}"), 8 * g - 8)
                        act.activation(vh[:, 2 * j + i], vraw[:, i], ACT.Copy).then_inc(sem(f"vh_ready{l}"), 1)
                    for i in range(2):
                        n = 2 * g + i
                        act.wait_ge(sem(f"h_mul{l}"), n + 1)
                        act.activation(hh[:, 2 * j + i], hg[:, i], ACT.Copy).then_inc(sem(f"hh_ready{l}"), 1)

                for i in range(2):
                    act.wait_ge(sem(f"u_loaded{l}_{i}"), 16)
                    act.activation(uh[:, i], uraw[:, i], ACT.Copy).then_inc(sem(f"uh_ready{l}"), 1)
                for j in range(2):
                    step(0, j, True, False)
                with act.Fori(1, KEYS // 4 - 1) as it:
                    for j in range(2):
                        step(it, j, False, False)
                for j in range(2):
                    step(KEYS // 4 - 1, j, False, j == 1)

            def rope_shift(first_tile, n):
                for f in range(n):
                    d = first_tile + f
                    act.wait_ge(sem("tile_done"), d + 1)
                    if d - D_K >= 2:
                        act.wait_ge(sem("roped"), d - D_K - 1)
                    for q in range(4):
                        src = 32 * (q ^ 1)
                        ins = act.activation(two(rot[32 * q:32 * q + 32, d % 2]),
                                             ps[src:src + 32, dbank(d):dbank(d) + 2, 0:H2], ACT.Copy)
                    ins.then_inc(sem("rot_ready"), 1)

            def attention():
                rope_shift(D_K, 2)
                act.wait_ge(sem("v_done"), 1)
                act.activation(vtok[:, 0:4].rearrange("p (b t) n -> p b (t n)", b=2), ps[:, 4:6, :], ACT.Copy)
                act.activation(vtok[0:NB * TS, 4], ps[0:NB * TS, 6, 0:NKV * HD], ACT.Copy
                               ).then_inc(sem("v_ready"), 1)
                rope_shift(D_Q, NC)
                for u in range(NQB * NKV):
                    act.wait_ge(sem("pmax"), u + 1)
                    for g in range(GRP):
                        act.activation(pr[:, g], pr[:, g], ACT.Exp, bias=sm[:, 1, g:g + 1],
                                       accum_out=sm[:, 2, g:g + 1])
                    act.activation(sm[:, 3, 0:GRP], sm[:, 3, 0:GRP], ACT.Exp).then_inc(sem("pexp"), 1)
                    act.wait_ge(sem("pturn"), u + 1)
                    act.activation(prT[:, :, :].rearrange("p (b j) k -> p b (j k)", b=2), ps[:, 2:4, :],
                                   ACT.Copy).then_inc(sem("prT_ready"), 1)
                act.wait_ge(sem("smax"), 1)
                act.activation(pss[:, :, :], pss[:, :, :], ACT.Exp).then_inc(sem("sexp"), 1)
                act.activation(sm[:, 3], sm[:, 3], ACT.Exp).then_inc(sem("sexp"), 1)
                act.wait_ge(sem("sturn"), 1)
                act.activation(pssT[:, :, :].rearrange("p (b j) k -> p b (j k)", b=2), ps[:, 4:6, :], ACT.Copy)
                act.activation(pssN[:, :, :].rearrange("p (b j) k -> p b (j k)", b=2), ps[0:TS, 6:8, :],
                               ACT.Copy).then_inc(sem("pssT_ready"), 1)

            rg_lru()
            for l, d0 in ((0, D_PQ0), (1, D_PQ1)):
                if l == 1:
                    square(2)
                    attention()
                square((1, 3)[l])
                copy_queries(d0)
                topk(l)
                copy_gates(l)
                split_x(l)
                experts(l)
            square(4)

        @block.vector
        def _(dve):
            chain = Chain(dve, sem("dve_chain"))

            def norm_stats(s):
                dve.wait_ge(sem("sum_done"), s + 1)
                dve.tensor_scalar(two(rinv[:, :]), halves(4), 1.0 / D, EPS, ALU.mult, ALU.add
                                  ).then_inc(sem("ms_ready"), 1)
                dve.wait_ge(sem("rms_ready"), s + 1)
                chain.did(dve.reciprocal(rinv[:, :], rinv[:, :]))
                chain.settle()

            def norm_apply(off):
                for c in range(NC):
                    ins = dve.scalar_tensor_tensor(xn[:, c], xT[:, c], prm[:, off + c:off + c + 1],
                                                   rinv[:, :], ALU.mult, ALU.mult)
                ins.then_inc(sem("xn_ready"), 1)

            def add_residual(d0):
                for f in range(NC):
                    dve.wait_ge(sem("tile_done"), d0 + f + 1)
                    dve.tensor_tensor(two(xT[:, f]), two(xT[:, f]), halves(dbank(d0 + f)), ALU.add
                                      ).then_inc(sem("d_free"), 1)

            def rg_lru():
                dve.wait_ge(sem("consts_loaded"), 32)
                dve.wait_ge(sem("lam_exp"), 1)
                dve.tensor_scalar(sp[:, 1], sp[:, 0], 1.0, None, ALU.add).then_inc(sem("lam_one"), 1)
                dve.wait_ge(sem("lam_ln"), 1)
                chain.did(dve.tensor_scalar(sp[:, 1], sp[:, 1], -1.0, None, ALU.add))
                chain.settle()
                chain.did(dve.tensor_scalar(sp[:, 3], sp[:, 1], 0.0, None, ALU.is_equal))
                chain.settle()
                chain.did(dve.tensor_tensor(sp[:, 1], sp[:, 1], sp[:, 3], ALU.add))
                chain.did(dve.tensor_tensor(sp[:, 2], sp[:, 2], sp[:, 3], ALU.add))
                chain.settle()
                chain.did(dve.reciprocal(sp[:, 1], sp[:, 1]))
                chain.settle()
                chain.did(dve.tensor_tensor(sp[:, 2], sp[:, 2], sp[:, 0], ALU.mult))
                chain.settle()
                dve.scalar_tensor_tensor(sp[:, 3], sp[:, 2], -8.0, sp[:, 1], ALU.mult, ALU.mult
                                         ).then_inc(sem("sp_ready"), 1)
                norm_stats(0)
                norm_apply(N_RG)
                for f in range(NC):
                    dve.wait_ge(sem("pre_copied"), f + 1)
                    dve.wait_ge(sem("d_free"), D_IN + NC + f + 1)
                    outs = (xc[:, f, 0:TP], xc[:, f, TP:T].rearrange("p (b s) -> p b s", b=NB))

                    def tap(k):
                        return (xpre[:, f, k:k + TP], xpreS[:, f, :, k:k + TS])
                    for k in range(CW):
                        w = prm[:, P_CW + k * NC + f:P_CW + k * NC + f + 1]
                        for o, i in zip(outs, tap(k)):
                            if k == 0:
                                ins = dve.tensor_scalar(o, i, w, prm[:, P_CB + f:P_CB + f + 1],
                                                        ALU.mult, ALU.add)
                            else:
                                ins = dve.scalar_tensor_tensor(o, i, w, o, ALU.mult, ALU.add)
                            if k < CW - 1:
                                chain.did(ins)
                        if k < CW - 1:
                            chain.settle()
                    ins.then_inc(sem("xc_ready"), 1)
                for f in range(NC):
                    dve.wait_ge(sem("tanh_ready"), f + 1)
                    chain.did(dve.tensor_scalar(xn[:, f], rg[:, f], -1.0, 1.0, ALU.mult, ALU.add))
                    chain.did(dve.tensor_tensor(ig[:, f], ig[:, f], xc[:, f], ALU.mult))
                    chain.settle()
                    chain.did(dve.reciprocal(xn[:, f], xn[:, f]))
                    chain.settle()
                    dve.scalar_tensor_tensor(rg[:, f], rg[:, f], -2.0, xn[:, f], ALU.mult, ALU.mult
                                             ).then_inc(sem("m2_ready"), 1)
                for f in range(NC):
                    dve.wait_ge(sem("mult_ready"), f + 1)
                    chain.did(dve.tensor_tensor(ig[:, f], ig[:, f], rg[:, f], ALU.mult))
                starts = dec[:, :, TP:T].rearrange("p c (b s) -> p c b s", b=NB)[:, :, :, 0]
                bstarts = ig[:, :, TP:T].rearrange("p c (b s) -> p c b s", b=NB)[:, :, :, 0]
                dve.wait_ge(sem("dec_ready"), NC)
                chain.did(dve.tensor_tensor(ah0[:, :, :], starts,
                                            prm[:, P_H0:P_H0 + NC * NB].rearrange("p (c b) -> p c b", c=NC),
                                            ALU.mult))
                chain.settle()
                chain.did(dve.tensor_tensor(bstarts, bstarts, ah0[:, :, :], ALU.add))
                chain.did(dve.memset(starts, 0.0))
                chain.settle()
                for f in range(NC):
                    chain.did(dve.tensor_tensor_scan(rg[:, f], dec[:, f], ig[:, f], 0.0, ALU.mult, ALU.add))
                chain.settle()
                chain.did(dve.tensor_copy(hlast[:, :, 0:1], rg[:, :, TP - 1:TP]))
                dve.tensor_copy(hlast[:, :, 1:1 + NB],
                                rg[:, :, TP:T].rearrange("p c (b s) -> p c b s", b=NB)[:, :, :, TS - 1]
                                ).then_inc(sem("hlast_ready"), 1)
                for f in range(NC):
                    dve.tensor_tensor(xn[:, f], rg[:, f], gate[:, f], ALU.mult).then_inc(sem("hg_ready"), 1)
                add_residual(D_OUT)
                dve.wait_ge(sem("d_free"), D_PQ0)
                dve.wait_ge(sem("states_out"), 48)
                dve.memset(qT[:, :, T:TPAD], 0.0).then_inc(sem("x_ready"), 1)

            def topk(l):
                def tile(t):
                    dve.wait_ge(sem(f"sc_copied{l}"), t + 1)
                    for j in range(2 * PH):
                        chain.did(dve.max(sv[:, j, 0:8], sc[:, j]))
                    chain.settle()
                    for j in range(2 * PH):
                        chain.did(dve.max_index(si[:, j, 0:8], sv[:, j, 0:8], sc[:, j]))
                        chain.did(dve.match_replace(sc2[:, j], sv[:, j, 0:8], sc[:, j], BIG))
                    chain.settle()
                    for j in range(2 * PH):
                        ins = dve.max(sv[:, j, 8:16], sc2[:, j])
                        if j < 2 * PH - 1:
                            chain.did(ins)
                    ins.then_inc(sem(f"sc_read{l}"), 1)
                    chain.settle()
                    dve.wait_ge(sem(f"sc_read{l}"), t + 1)
                    for j in range(2 * PH):
                        chain.did(dve.max_index(si[:, j, 8:16], sv[:, j, 8:16], sc2[:, j]))
                    s4 = sv[:, :, :].rearrange("p (h a) k -> p h a k", a=2)
                    chain.did(dve.tensor_tensor(
                        cand[:, :, :].rearrange("p h (i j) -> p h i j", i=TOPK),
                        s4[:, :, 0].unsqueeze(3).broadcast_to([P, PH, TOPK, TOPK]),
                        s4[:, :, 1].unsqueeze(2).broadcast_to([P, PH, TOPK, TOPK]), ALU.add))
                    chain.settle()
                    chain.did(dve.tensor_copy(sif[:, :, :], si[:, :, :]))
                    for h in range(PH):
                        chain.did(dve.max(cv[:, h, 0:8], cand[:, h]))
                    chain.settle()
                    for h in range(PH):
                        chain.did(dve.max_index(ci[:, h, 0:8], cv[:, h, 0:8], cand[:, h]))
                        chain.did(dve.match_replace(cand2[:, h], cv[:, h, 0:8], cand[:, h], BIG))
                    chain.settle()
                    for h in range(PH):
                        chain.did(dve.max(cv[:, h, 8:16], cand2[:, h]))
                    chain.settle()
                    dve.tensor_tensor(ex[:, :, :], cv[:, :, :], cv[:, :, 0:1].broadcast_to([P, PH, TOPK]),
                                      ALU.subtract).then_inc(sem(f"ex_in{l}"), 1)
                    for h in range(PH):
                        chain.did(dve.max_index(ci[:, h, 8:16], cv[:, h, 8:16], cand2[:, h]))
                    chain.settle()
                    chain.did(dve.tensor_scalar(cab[:, 0], ci[:, :, :], 4, None, ALU.logical_shift_right))
                    chain.did(dve.tensor_scalar(cab[:, 1], ci[:, :, :], TOPK - 1, None, ALU.bitwise_and))
                    chain.settle()
                    chain.did(dve.tensor_copy(cabf[:, :, :, :], cab[:, :, :, :]))
                    chain.settle()
                    f4 = sif[:, :, :].rearrange("p (h a) k -> p h a k", a=2)
                    eq = [b_[:, :, :].rearrange("p h (k i) -> p h k i", k=TOPK) for b_ in (cand, cand2)]
                    for a in range(2):
                        chain.did(dve.tensor_tensor(
                            eq[a], cabf[:, a].unsqueeze(3).broadcast_to([P, PH, TOPK, TOPK]),
                            iota[:, 0:TOPK].unsqueeze(1).unsqueeze(1).broadcast_to([P, PH, TOPK, TOPK]),
                            ALU.is_equal))
                    chain.settle()
                    for a in range(2):
                        chain.did(dve.tensor_tensor(
                            eq[a], eq[a], f4[:, :, a].unsqueeze(2).broadcast_to([P, PH, TOPK, TOPK]),
                            ALU.mult))
                    chain.settle()
                    for a in range(2):
                        chain.did(dve.tensor_reduce(slot[:, a].rearrange("p (h k) -> p h k", h=PH), eq[a],
                                                    X, ALU.add))
                    dve.wait_ge(sem(f"ex_out{l}"), t + 1)
                    chain.did(dve.tensor_reduce(exs[:, 0], ex[:, :, :], X, ALU.add))
                    chain.settle()
                    chain.did(dve.reciprocal(exs[:, 1], exs[:, 0]))
                    chain.settle()
                    dve.tensor_tensor(slot[:, 2].rearrange("p (h k) -> p h k", h=PH), ex[:, :, :],
                                      exs[:, 1].unsqueeze(2).broadcast_to([P, PH, TOPK]), ALU.mult
                                      ).then_inc(sem(f"slots{l}"), 1)
                    dve.wait_ge(sem(f"turned{l}"), t + 1)

                for t in range(TT):
                    tile(t)

            def one_hots(l):
                dve.wait_ge(sem(f"slot_ready{l}"), TT)

                def batch(it, first):
                    for q in range(4):
                        if not first:
                            dve.wait_ge(sem(f"g_done{l}"), it * 4 + (q - 3))
                        for i in range(4):
                            k = 4 * q + i

                            def col(a):
                                if isinstance(it, int):
                                    return slotT[:, a, it * 16 + k:it * 16 + k + 1]
                                return slotT[:, a, bass.ds(it * 16 + k, 1)]
                            dve.tensor_scalar(hotA[:, k], iota, col(0), None, ALU.is_equal)
                            ins = dve.tensor_scalar(hotB[:, k], iota, col(1), col(2), ALU.is_equal, ALU.mult)
                        ins.then_inc(sem(f"hot{l}"), 1)

                batch(0, True)
                with dve.Fori(1, T // 16) as it:
                    batch(it, False)

            def split_x(l):
                for c in range(NC):
                    dve.wait_ge(sem(f"xh_ready{l}"), c + 1)
                    dve.tensor_tensor(xl[:, c], xn[:, c], xh[:, c].bitcast(F32), ALU.subtract
                                      ).then_inc(sem(f"xl_ready{l}"), 1)

            def experts(l):
                def lo_u(n, i):
                    dve.wait_ge(sem(f"uh_ready{l}"), n + 1)
                    dve.tensor_tensor(ul[:, i], uraw[:, i], uh[:, i].bitcast(F32), ALU.subtract
                                      ).then_inc(sem(f"u_split{l}"), 1)

                def evac(g, c):
                    dve.wait_ge(sem(f"o_full{l}"), 8 * g + (c + 1))
                    dve.tensor_tensor(two(xT[:, c]), two(xT[:, c]), halves(4 + 2 * (c % 2)), ALU.add
                                      ).then_inc(sem(f"o_free{l}"), 1)

                def step(it, j, first, last):
                    g = 2 * it + j

                    def ev(c):
                        if not (first and j == 0):
                            evac(g - 1, c)
                    for i in range(2):
                        ev(i)
                        if not last:
                            lo_u(2 * g + 2 + i, i)
                    for i in range(2):
                        n = 2 * g + i
                        ev(2 + i)
                        dve.wait_ge(sem(f"s_free{l}"), n + 1)
                        dve.wait_ge(sem(f"gt_loaded{l}_{j}"), 16 * it + 16)
                        dve.tensor_tensor(hg[:, i].rearrange("p (b t) -> p b t", b=NGB),
                                          hg[:, i].rearrange("p (b t) -> p b t", b=NGB),
                                          gt[:, j, :, i], ALU.mult).then_inc(sem(f"h_mul{l}"), 1)
                    for i in range(2):
                        n = 2 * g + i
                        ev(4 + i)
                        dve.wait_ge(sem(f"vh_ready{l}"), n + 1)
                        dve.tensor_tensor(vl[:, 2 * j + i], vraw[:, i], vh[:, 2 * j + i].bitcast(F32),
                                          ALU.subtract).then_inc(sem(f"v_split{l}"), 1)
                    for i in range(2):
                        n = 2 * g + i
                        ev(6 + i)
                        dve.wait_ge(sem(f"hh_ready{l}"), n + 1)
                        dve.tensor_tensor(hl[:, 2 * j + i], hg[:, i], hh[:, 2 * j + i].bitcast(F32),
                                          ALU.subtract).then_inc(sem(f"h_split{l}"), 1)

                for i in range(2):
                    lo_u(i, i)
                for j in range(2):
                    step(0, j, True, False)
                with dve.Fori(1, KEYS // 4 - 1) as it:
                    for j in range(2):
                        step(it, j, False, False)
                for j in range(2):
                    step(KEYS // 4 - 1, j, False, j == 1)
                for c in range(NC):
                    evac(KEYS // 2 - 1, c)
                dve.wait_ge(sem(f"o_free{l}"), KEYS // 2 * NC)
                dve.memset(sm0, 0.0).then_inc(sem("x_ready"), 1)

            sm0 = rinv[:, 0:1]

            def rope(d0, n, dst):
                for f in range(n):
                    d = d0 + f
                    r = d % 2
                    dve.wait_ge(sem("rot_ready"), d - D_K + 1)
                    chain.did(dve.tensor_tensor(rot[:, r], rot[:, r], cst[:, C_SIN:C_SIN + T], ALU.mult))
                    dve.tensor_tensor(two(rc[:, r]), halves(dbank(d)), two(cst[:, C_COS:C_COS + T]), ALU.mult
                                      ).then_inc(sem("d_free"), 1)
                    chain.settle()
                    dve.wait_ge(sem("d_free"), d + 1)
                    chain.did(dve.tensor_tensor(dst[:, 2 * f], rc[0:HD, r], rot[0:HD, r], ALU.add))
                    ins = dve.tensor_tensor(dst[:, 2 * f + 1], rc[HD:P, r], rot[HD:P, r], ALU.add)
                    ins.then_inc(sem("roped"), 1)

            def attention():
                norm_stats(2)
                norm_apply(N_KV)
                rope(D_K, 2, kR)
                dve.wait_ge(sem("roped"), 2)
                dve.wait_ge(sem("tile_done"), D_Q)
                dve.wait_ge(sem("v_done"), 1)
                dve.memset(sm0b, 0.0).then_inc(sem("k_ready"), 2)
                norm_apply(N_AT)
                rope(D_Q, NC, qR)
                dve.wait_ge(sem("roped"), 2 + NC)
                dve.tensor_copy(qS[:, :, :, :], qR[:, :, TP:T].rearrange("p h (b s) -> p b h s", b=NB)
                                ).then_inc(sem("qS_ready"), 1)
                ob = xn
                for n in range(NQB):
                    for kv in range(NKV):
                        u = n * NKV + kv
                        lo = 0 if n else WIN
                        dve.wait_ge(sem("p_scores"), u + 1)
                        if u:
                            dve.wait_ge(sem("pturn"), u)
                        elif True:
                            dve.wait_ge(sem("tile_done"), D_O)
                        w = 2 * WIN - lo
                        chain.did(dve.scalar_tensor_tensor(
                            pr[:, :, lo:], ps[:, 0:2, :].rearrange("p b (g k) -> p (b g) k", g=2)[:, :, lo:],
                            HD ** -0.5, cst[:, C_MP + lo:C_MP + 2 * WIN].unsqueeze(1).broadcast_to([P, GRP, w]),
                            ALU.mult, ALU.add))
                        if not n:
                            chain.did(dve.memset(pr[:, :, 0:WIN], BIG))
                        chain.settle()
                        chain.did(dve.tensor_reduce(sm[:, 0, 0:GRP], pr[:, :, :], X, ALU.max))
                        chain.settle()
                        sk = prm[:, P_SINK + kv * GRP:P_SINK + (kv + 1) * GRP]
                        chain.did(dve.tensor_tensor(sm[:, 0, 0:GRP], sm[:, 0, 0:GRP], sk, ALU.max))
                        chain.settle()
                        chain.did(dve.tensor_scalar(sm[:, 1, 0:GRP], sm[:, 0, 0:GRP], -1.0, None, ALU.mult))
                        dve.tensor_tensor(sm[:, 3, 0:GRP], sk, sm[:, 0, 0:GRP], ALU.subtract
                                          ).then_inc(sem("pmax"), 1)
                        dve.wait_ge(sem("pexp"), u + 1)
                        chain.did(dve.tensor_tensor(sm[:, 4, 0:GRP], sm[:, 2, 0:GRP], sm[:, 3, 0:GRP], ALU.add))
                        chain.settle()
                        chain.did(dve.reciprocal(sm[:, 5, 0:GRP], sm[:, 4, 0:GRP]))
                        chain.settle()
                        dve.tensor_tensor(pr[:, :, :], pr[:, :, :],
                                          sm[:, 5, 0:GRP].unsqueeze(2).broadcast_to([P, GRP, 2 * WIN]), ALU.mult
                                          ).then_inc(sem("p_ready"), 1)
                        dve.wait_ge(sem("p_out"), u + 1)
                        for e in range(2):
                            ins = dve.tensor_copy(
                                ob[e * HD:(e + 1) * HD, 2 * kv:2 * kv + 2, n * WIN:(n + 1) * WIN],
                                ps[0:HD, 7, :].rearrange("p (g e q) -> p g e q", g=2, e=2)[:, :, e])
                            if e == 0:
                                chain.did(ins)
                        ins.then_inc(sem("o_copied"), 1)
                dve.wait_ge(sem("s_scores"), 1)
                chain.did(dve.scalar_tensor_tensor(
                    pss[:, :, :], ps[:, 0:4, :].rearrange("p b (j k) -> p (b j) k", j=2)[:, :, 0:WIN + TS],
                    HD ** -0.5, cst[:, C_MS:C_MS + WIN + TS].unsqueeze(1).broadcast_to([P, NB, WIN + TS]),
                    ALU.mult, ALU.add))
                chain.settle()
                chain.did(dve.tensor_reduce(sm[:, 0], pss[:, :, :], X, ALU.max))
                chain.settle()
                chain.did(dve.tensor_scalar(sm[:, 0], sm[:, 0], prm[:, P_SKS:P_SKS + 1], None, ALU.max))
                chain.settle()
                chain.did(dve.tensor_scalar(sm[:, 3], sm[:, 0], -1.0, prm[:, P_SKS:P_SKS + 1], ALU.mult, ALU.add))
                chain.settle()
                dve.tensor_tensor(pss[:, :, :], pss[:, :, :],
                                  sm[:, 0].unsqueeze(2).broadcast_to([P, NB, WIN + TS]), ALU.subtract
                                  ).then_inc(sem("smax"), 1)
                dve.wait_ge(sem("sexp"), 2)
                chain.did(dve.tensor_reduce(sm[:, 4], pss[:, :, :], X, ALU.add))
                chain.settle()
                chain.did(dve.tensor_tensor(sm[:, 4], sm[:, 4], sm[:, 3], ALU.add))
                chain.settle()
                chain.did(dve.reciprocal(sm[:, 5], sm[:, 4]))
                chain.settle()
                dve.tensor_tensor(pss[:, :, :], pss[:, :, :],
                                  sm[:, 5].unsqueeze(2).broadcast_to([P, NB, WIN + TS]), ALU.mult
                                  ).then_inc(sem("s_ready"), 1)
                dve.wait_ge(sem("s_out"), 1)
                for g in range(GRP):
                    e = g % 2
                    for bb in range(2):
                        ins = dve.tensor_copy(
                            ob[e * HD:(e + 1) * HD, :, TP:T].rearrange("p (k c) (b s) -> p c b k s", k=NKV, b=NB)
                            [:, g // 2, 4 * bb:4 * bb + 4],
                            ps[0:HD, bb, :].rearrange("p (b k g s) -> p g b k s", b=4, k=NKV, g=GRP)[:, g])
                        if g < GRP - 1 or bb == 0:
                            chain.did(ins)
                ins.then_inc(sem("o_copied"), 1)
                add_residual(D_O)
                dve.wait_ge(sem("d_free"), D_PQ1)
                dve.memset(qT[:, :, T:TPAD], 0.0).then_inc(sem("x_ready"), 1)

            sm0b = rc[:, 0, 0:1]

            rg_lru()
            for l, (s, off) in enumerate(((1, N_F0), (3, N_F1))):
                if l == 1:
                    attention()
                norm_stats(s)
                norm_apply(off)
                topk(l)
                one_hots(l)
                split_x(l)
                experts(l)
            norm_stats(4)
            norm_apply(N_FIN)

        @block.tensor
        def _(pe):
            def sum_squares(s):
                if s == 0:
                    pe.wait_ge(sem("ones_ready"), 1)
                for c in range(NC):
                    pe.wait_ge(sem("sq_ready"), NC * s + c + 1)
                    for h in range(2):
                        ins = pe.matmul(ps[:, 4 + h, 0:H2], ones[:, :], xn[:, c, h * H2:(h + 1) * H2],
                                        start=(c == 0), stop=(c == NC - 1))
                ins.then_inc(sem("sum_done"), 1)

            def project(w0, d0, n, src):
                for f in range(n):
                    w, d = w0 + f, d0 + f
                    pe.wait_ge(sem(f"w_loaded{w % RING}"), 16 * (w // RING + 1))
                    if d >= 2:
                        pe.wait_ge(sem("d_free"), d - 1)
                    for c in range(NC):
                        for h in range(2):
                            ins = pe.matmul(ps[:, dbank(d) + h, 0:H2], wring[:, w % RING, c],
                                            src[:, c, h * H2:(h + 1) * H2], start=(c == 0), stop=(c == NC - 1))
                    ins.then_inc(sem("tile_done"), 1)

            def rg_gates():
                for w, d0 in ((W_A, D_A), (W_X, D_X)):
                    pe.wait_ge(sem(f"w_loaded{w % RING}"), 16 * (w // RING + 1))
                    for f in range(NC):
                        d = d0 + f
                        pe.wait_ge(sem("xc_ready"), f + 1)
                        pe.wait_ge(sem("d_free"), d - 1)
                        for h in range(2):
                            ins = pe.matmul(ps[:, dbank(d) + h, 0:H2], wring[:, w % RING, f],
                                            xc[:, f, h * H2:(h + 1) * H2], start=True, stop=True)
                        ins.then_inc(sem("tile_done"), 1)

            def topk(l):
                def scores(t):
                    if t:
                        pe.wait_ge(sem(f"sc_copied{l}"), t)
                    for j in range(2 * PH):
                        sk = P_SK + (2 * l + j % 2) * KEYS
                        ins = pe.matmul(ps[:, 4 + j // 4, (j % 4) * P:(j % 4 + 1) * P],
                                        qT[:, j, t * P:(t + 1) * P], prm[:, sk:sk + KEYS], start=True, stop=True)
                    ins.then_inc(sem(f"sc_done{l}"), 1)

                pe.wait_ge(sem("d_free"), (D_K, D_N)[l])
                scores(0)
                for t in range(TT):
                    if t + 1 < TT:
                        scores(t + 1)
                    pe.wait_ge(sem(f"slots{l}"), t + 1)
                    if t:
                        pe.wait_ge(sem(f"slot_ready{l}"), t)
                    for a in range(3):
                        ins = pe.transpose(ps[:, 0, a * P:(a + 1) * P], slot[:, a], ident)
                    ins.then_inc(sem(f"turned{l}"), 1)

            def gate_matrix(l):
                pe.wait_ge(sem(f"slot_ready{l}"), TT)

                def batch(it, first):
                    for q in range(4):
                        pe.wait_ge(sem(f"hot{l}"), it * 4 + (q + 1))
                        if not first:
                            pe.wait_ge(sem(f"g_copied{l}"), it * 4 + (q - 3))
                        for i in range(4):
                            k = 4 * q + i
                            ins = pe.matmul(ps[:, q, i * P:(i + 1) * P], hotB[:, k], hotA[:, k],
                                            start=True, stop=True)
                        ins.then_inc(sem(f"g_done{l}"), 1)

                batch(0, True)
                with pe.Fori(1, T // 16) as it:
                    batch(it, False)

            def experts(l):
                def up(g, i, first):
                    n = 2 * g + i
                    pe.wait_ge(sem(f"u_split{l}"), n + 1)
                    if not first:
                        pe.wait_ge(sem(f"s_free{l}"), n - 1)
                    for c in range(NC):
                        for k, (w, x) in enumerate(((uh, xh), (uh, xl), (ul, xh))):
                            for h in range(2):
                                ins = pe.matmul(ps[:, 2 * i + h, 0:H2], w[:, i, c], x[:, c, h * H2:(h + 1) * H2],
                                                start=(c == 0 and k == 0), stop=(c == NC - 1 and k == 2))
                    ins.then_inc(sem(f"s_full{l}"), 1)

                def down(g, j, first):
                    pe.wait_ge(sem(f"v_split{l}"), 2 * g + 2)
                    pe.wait_ge(sem(f"h_split{l}"), 2 * g + 2)
                    for c in range(NC):
                        if not (first and c < 2):
                            pe.wait_ge(sem(f"o_free{l}"), 8 * g + (c - 1))
                        for i in range(2):
                            for k, (w, x) in enumerate(((vh, hh), (vh, hl), (vl, hh))):
                                for h in range(2):
                                    ins = pe.matmul(ps[:, 4 + 2 * (c % 2) + h, 0:H2],
                                                    w[:, 2 * j + i, c * P:(c + 1) * P],
                                                    x[:, 2 * j + i, h * H2:(h + 1) * H2],
                                                    start=(i == 0 and k == 0), stop=(i == 1 and k == 2))
                        ins.then_inc(sem(f"o_full{l}"), 1)

                pe.wait_ge(sem(f"xl_ready{l}"), NC)
                pe.wait_ge(sem(f"g_copied{l}"), T // 4)
                for i in range(2):
                    up(0, i, True)
                for j in range(2):
                    for i in range(2):
                        up(1 + j, i, False)
                    down(j, j, j == 0)
                with pe.Fori(1, KEYS // 4 - 1) as it:
                    for j in range(2):
                        for i in range(2):
                            up(2 * it + (1 + j), i, False)
                        down(2 * it + j, j, False)
                g = KEYS // 2 - 2
                for i in range(2):
                    up(g + 1, i, False)
                down(g, 0, False)
                down(g + 1, 1, False)

            def attention():
                project(W_K, D_K, 2, xn)
                pe.wait_ge(sem("wv_loaded"), 16)
                for t in range(TT):
                    m = min(P, T - t * P)
                    for c in range(NC):
                        ins = pe.matmul(ps[0:m, 4 + t // 2, (t % 2) * 256:(t % 2 + 1) * 256],
                                        xn[:, c, t * P:t * P + m], wv_sb[:, c], start=(c == 0), stop=(c == NC - 1))
                ins.then_inc(sem("v_done"), 1)
                pe.wait_ge(sem("xn_ready"), 4)
                project(W_Q, D_Q, NC, xn)
                pe.wait_ge(sem("roped"), 2 + NC)
                pe.wait_ge(sem("v_ready"), 1)
                for n in range(NQB):
                    ks = max(0, n - 1) * WIN
                    lo = 0 if n else WIN
                    for kv in range(NKV):
                        u = n * NKV + kv
                        if u:
                            pe.wait_ge(sem("p_ready"), u)
                        for g in range(GRP):
                            ins = pe.matmul(ps[:, g // 2, (g % 2) * 256 + lo:(g % 2 + 1) * 256],
                                            qR[:, kv * GRP + g, n * WIN:(n + 1) * WIN],
                                            kR[:, kv, ks:(n + 1) * WIN], start=True, stop=True)
                        ins.then_inc(sem("p_scores"), 1)
                        pe.wait_ge(sem("p_ready"), u + 1)
                        if u:
                            pe.wait_ge(sem("prT_ready"), u)
                        for kb in range(2):
                            for g in range(GRP):
                                ins = pe.transpose(ps[:, 2 + kb, g * P:(g + 1) * P],
                                                   pr[:, g, kb * WIN:(kb + 1) * WIN], ident)
                        ins.then_inc(sem("pturn"), 1)
                        pe.wait_ge(sem("prT_ready"), u + 1)
                        if u:
                            pe.wait_ge(sem("o_copied"), u)
                        kbs = (0, 1) if n else (1,)
                        for kb in kbs:
                            ins = pe.matmul(ps[0:HD, 7, :], vtok[:, n - 1 + kb, kv * HD:(kv + 1) * HD],
                                            prT[:, 4 * kb:4 * kb + 4].rearrange("p g q -> p (g q)"),
                                            start=(kb == kbs[0]), stop=(kb == 1))
                        ins.then_inc(sem("p_out"), 1)
                pe.wait_ge(sem("qS_ready"), 1)
                pe.wait_ge(sem("kc_loaded"), 16)
                pe.wait_ge(sem("vc_loaded"), 16)
                pe.wait_ge(sem("vnew_loaded"), 16 * NB)
                for b in range(NB):
                    for kv in range(NKV):
                        o = ps[32 * kv:32 * kv + 32, b // 2, (b % 2) * 256:(b % 2) * 256 + WIN + TS]
                        q = qS[:, b, kv * GRP:(kv + 1) * GRP].rearrange("p g s -> p (g s)")
                        pe.matmul(o[:, 0:WIN], q, kc_sb[:, b, kv], start=True, stop=True)
                        ins = pe.matmul(o[:, WIN:], q, kR[:, kv, TP + b * TS:TP + (b + 1) * TS],
                                        start=True, stop=True)
                ins.then_inc(sem("s_scores"), 1)
                pe.wait_ge(sem("s_ready"), 1)
                pe.wait_ge(sem("o_copied"), NQB * NKV)
                for b in range(NB):
                    pe.transpose(ps[:, 4 + b // 4, (b % 4) * P:(b % 4 + 1) * P], pss[:, b, 0:WIN], ident)
                    ins = pe.transpose(ps[0:TS, 6 + b // 4, (b % 4) * P:(b % 4 + 1) * P], pss[:, b, WIN:], ident)
                ins.then_inc(sem("sturn"), 1)
                pe.wait_ge(sem("pssT_ready"), 1)
                for b in range(NB):
                    for kv in range(NKV):
                        o = ps[0:HD, b // 4, (b % 4) * P + 32 * kv:(b % 4) * P + 32 * kv + 32]
                        pe.matmul(o, vc_sb[:, b, kv * HD:(kv + 1) * HD], pssT[:, b, 32 * kv:32 * kv + 32],
                                  start=True, stop=False)
                        ins = pe.matmul(o, vnew[:, b, kv * HD:(kv + 1) * HD], pssN[:, b, 32 * kv:32 * kv + 32],
                                        start=False, stop=True)
                ins.then_inc(sem("s_out"), 1)
                pe.wait_ge(sem("o_copied"), NQB * NKV + 1)
                project(W_O, D_O, NC, xn)

            sum_squares(0)
            pe.wait_ge(sem("xn_ready"), 1)
            project(W_IN, D_IN, 2 * NC, xn)
            rg_gates()
            pe.wait_ge(sem("hg_ready"), NC)
            project(W_OUT, D_OUT, NC, xn)
            for l in range(2):
                if l == 1:
                    sum_squares(2)
                    pe.wait_ge(sem("xn_ready"), 3)
                    attention()
                sum_squares((1, 3)[l])
                pe.wait_ge(sem("xn_ready"), (2, 5)[l])
                project((W_PQ0, W_PQ1)[l], (D_PQ0, D_PQ1)[l], 2 * PH, xn)
                topk(l)
                gate_matrix(l)
                experts(l)
            sum_squares(4)


def _shape_constants():
    import numpy as np
    c = np.zeros((P, C_N), np.float32)
    c[:, C_ID:C_ID + P] = np.eye(P)
    c[:, C_IOTA:C_IOTA + P] = np.arange(P)
    half = HD // 2
    inv = np.float32(10000.0) ** (-np.arange(half, dtype=np.float32) / np.float32(half))
    pos = np.concatenate([np.arange(TP), np.tile(4096 + np.arange(TS), NB)]).astype(np.float32)
    ang = (inv[:, None] * pos[None, :]).astype(np.float32).astype(np.float64)
    cos, sin = np.cos(ang), np.sin(ang)
    c[:, C_COS:C_COS + T] = np.tile(cos, (4, 1))
    c[:, C_SIN:C_SIN + T] = np.concatenate([-sin, sin, -sin, sin])
    q = np.arange(P)[:, None]
    k = np.arange(WIN)[None, :]
    c[:, C_MP:C_MP + WIN] = np.where(k > q, 0, BIG)
    c[:, C_MP + WIN:C_MP + 2 * WIN] = np.where(k <= q, 0, BIG)
    s = q % TS
    c[:, C_MS:C_MS + WIN] = np.where(k > s, 0, BIG)
    c[:, C_MS + WIN:C_MS + WIN + TS] = np.where(np.arange(TS)[None, :] <= s, 0, BIG)
    return c


def kernel(**inputs):
    import numpy as np
    import concourse.bacc as _bacc
    from concourse import mybir as _mybir
    from concourse.bass_utils import run_bass_kernel_spmd as _run

    a = {k: np.asarray(v) for k, v in inputs.items()}

    def chunks(vec):
        return vec.reshape(-1, P).T

    def tiles(w):
        return w.reshape(NC, P, -1, P).transpose(2, 1, 0, 3)

    xin = np.concatenate([a["x_prompt"].reshape(TP, D), a["x_sample"].reshape(NB * TS, D)])
    xin = xin.T.reshape(NC, P, T).transpose(1, 0, 2)
    gains = np.concatenate([a["rg_norm"].ravel(), a["ffn_norm"][0], a["kv_norm"], a["attn_norm"].ravel(),
                            a["ffn_norm"][1], a["final_norm"]])
    h0 = a["state_h"][0].reshape(NB, NC, P).transpose(2, 1, 0).reshape(P, NC * NB)
    sinks = a["sinks"].ravel()
    subkeys = a["peer_subkeys"].transpose(3, 0, 1, 2).reshape(P, 4 * KEYS)
    params = np.concatenate([
        chunks(gains), chunks(a["rg_conv_w"].ravel()), chunks(a["rg_conv_b"].ravel()),
        chunks(a["rg_ba"].ravel()), chunks(a["rg_bx"].ravel()), chunks(a["rg_lambda"].ravel()), h0,
        np.broadcast_to(sinks, (P, NH)), np.repeat(sinks, TS).reshape(P, 1), subkeys], axis=1)
    w_kv = a["w_kv"]
    wts = np.concatenate([
        tiles(a["rg_w_in"][0]), a["rg_wa"][0].transpose(1, 0, 2)[None], a["rg_wx"][0].transpose(1, 0, 2)[None],
        tiles(a["rg_w_out"][0]), tiles(a["peer_wq"][0]), tiles(w_kv[:, :NKV * HD]), tiles(a["w_q"][0]),
        tiles(a["w_o"][0]), tiles(a["peer_wq"][1])])
    arrays = {
        "xin": xin, "consts": _shape_constants(), "params": params, "wts": wts,
        "wv": w_kv[:, NKV * HD:].reshape(NC, P, NKV * HD).transpose(1, 0, 2),
        "stconv": a["state_conv"][0].reshape(NB, CW - 1, NC, P).transpose(3, 2, 0, 1).reshape(P, NC * NB, CW - 1),
        "kcT": a["cache_k"].transpose(3, 0, 2, 1),
        "kc": a["cache_k"].reshape(NB, WIN, NKV * HD),
        "vc": a["cache_v"].reshape(NB, WIN, NKV * HD).transpose(1, 0, 2),
        "uT": a["peer_u"].reshape(2, KEYS, KEYS, NC, P).transpose(0, 1, 4, 3, 2).reshape(2, KEYS, P, D),
        "v": a["peer_v"].reshape(2, KEYS, KEYS, D),
    }
    arrays = {k: np.ascontiguousarray(x) for k, x in arrays.items()}
    outs = {
        "yT": (P, NC, T), "convP": (P, NC, CW - 1), "hOut": (P, NC, 1 + NB), "kNew": (HD, NKV, WIN + NB * TS),
        "vNewP": (P, NKV * HD), "vNewS": (NB * TS, NKV * HD), "kKeep": (NB, WIN - TS, NKV * HD),
        "vKeep": (NB, WIN - TS, NKV * HD), "convS": (P, NC * NB, CW - 1),
    }
    nc = _bacc.Bacc("TRN2", target_bir_lowering=False, num_devices=1)
    f32 = _mybir.dt.float32
    args = [nc.dram_tensor(k, x.shape, _mybir.dt.from_np(x.dtype), kind="ExternalInput").ap()
            for k, x in arrays.items()]
    args += [nc.dram_tensor(k, s, f32, kind="ExternalOutput").ap() for k, s in outs.items()]
    args.append(nc.dram_tensor("gate_dram", (2, NGB, P, KEYS * GB), f32, kind="Internal").ap())
    decoder(nc, *args)
    r = _run(nc, [arrays], core_ids=[0]).results[0]

    y = r["yT"].transpose(2, 1, 0).reshape(T, D)
    convP = r["convP"].transpose(2, 1, 0).reshape(1, 1, CW - 1, D)
    convS = r["convS"].reshape(P, NC, NB, CW - 1).transpose(2, 3, 1, 0).reshape(1, NB, CW - 1, D)
    h = r["hOut"].transpose(2, 1, 0).reshape(1 + NB, D)
    kn = r["kNew"].transpose(2, 1, 0)
    ks = np.concatenate([r["kKeep"].reshape(NB, WIN - TS, NKV, HD), kn[WIN:].reshape(NB, TS, NKV, HD)], axis=1)
    vs = np.concatenate([r["vKeep"].reshape(NB, WIN - TS, NKV, HD), r["vNewS"].reshape(NB, TS, NKV, HD)], axis=1)
    return (y[:TP].reshape(1, TP, D), y[TP:].reshape(NB, TS, D), convP, h[:1].reshape(1, 1, D),
            kn[:WIN].reshape(1, WIN, NKV, HD), r["vNewP"].reshape(1, WIN, NKV, HD), convS,
            h[1:].reshape(1, NB, D), ks, vs)
```

```python
from contextlib import ExitStack

import concourse.bass as bass
from concourse import mybir

F32 = mybir.dt.float32
F32R = mybir.dt.float32r
U32 = mybir.dt.uint32
ALU = mybir.AluOpType
ACT = mybir.ActivationFunctionType
X = mybir.AxisListType.X

P = 128
D = 1024
NC = D // P
TP, NB, TS = 512, 8, 8
T = TP + NB * TS
H2 = T // 2
TT = -(-T // P)
TLO = [min(t * P, T - P) for t in range(TT)]
CW = 4
NH, NKV, HD = 16, 4, 64
GRP = NH // NKV
WIN = 128
NQB = TP // WIN
PH, TOPK = 8, 16
NS = PH * TOPK
KEYS = 128
RING = 4
GB = 64
NGB = T // GB
UB = 8
NA1 = UB * TT
NA2 = T // 16
NA = NA1 + NA2
GA = NA // 2
NG = KEYS // 2
EPS = 1e-6
BIG = -3.0e38

C_ID, C_IOTA, C_COS = 0, P, 2 * P
C_SIN = C_COS + T
C_MP = C_SIN + T
C_MS = C_MP + 2 * WIN
C_N = C_MS + WIN + TS
(N_RG, N_F0, N_KV, N_AT, N_F1, N_FIN) = (NC * i for i in range(6))
P_CW = 6 * NC
P_CB = P_CW + CW * NC
P_BA = P_CB + NC
P_BX = P_BA + NC
P_LAM = P_BX + NC
P_H0 = P_LAM + NC
P_SINK = P_H0 + NC * NB
P_SKS = P_SINK + NH
P_SK = P_SKS + 1
P_N = P_SK + 4 * KEYS

W_IN, W_A, W_X, W_OUT, W_PQ0, W_K, W_Q, W_O, W_PQ1, W_N = 0, 16, 17, 18, 26, 42, 44, 52, 60, 76
D_IN, D_A, D_X, D_OUT, D_PQ0, D_K, D_Q, D_O, D_PQ1, D_N = 0, 16, 24, 32, 40, 56, 58, 66, 74, 90


def tiles_made(w):
    if w < W_A:
        return w + 1
    if w in (W_A, W_X):
        return D_A + NC * (w - W_A + 1)
    return w + 1 + 2 * (NC - 1)


class Chain:

    def __init__(self, eng, sem):
        self.eng, self.sem, self.n = eng, sem, 0

    def did(self, ins):
        ins.then_inc(self.sem, 1)
        self.n += 1

    def settle(self):
        self.eng.wait_ge(self.sem, self.n)


def decoder(nc, xin, consts, params, wts, wv, stconv, kcT, kc, vc, uT, v,
            yT, convP, hOut, kNew, vNewP, vNewS, kKeep, vKeep, convS, gate_dram, s_dram):
    with ExitStack() as ctx:
        def sb(name, shape, dt=F32, st=ctx):
            return st.enter_context(nc.sbuf_tensor(name, shape, dt))

        sems = {}

        def sem(name):
            if name not in sems:
                sems[name] = ctx.enter_context(nc.semaphore(name))
            return sems[name]

        ps = ctx.enter_context(nc.psum_tensor("ps", [P, 8, 512], F32))

        xT = sb("xT", [P, NC, T])
        cst = sb("cst", [P, C_N])
        prm = sb("prm", [P, P_N])
        wring = sb("wring", [P, RING, NC, P])
        rinv = sb("rinv", [P, T])
        ones = sb("ones", [P, P])
        slotT = sb("slotT", [P, 3, T])
        ident = cst[:, C_ID:C_ID + P]
        iota = cst[:, C_IOTA:C_IOTA + P]

        with ExitStack() as st:
            sc = sb("sc", [P, 2 * PH, KEYS], st=st)
            sc2 = sb("sc2", [P, 2 * PH, KEYS], st=st)
        with ExitStack() as st:
            hotA = sb("hotA", [P, 16, KEYS], st=st)
            hotB = sb("hotB", [P, 16, KEYS], st=st)
        with ExitStack() as st:
            hh = sb("hh", [P, 4, T], F32R, st=st)
            hl = sb("hl", [P, 4, T], F32R, st=st)
        xn = sb("xn", [P, NC, T])

        with ExitStack() as st:
            gate = sb("gate", [P, NC, T], st=st)
            xpre = sb("xpre", [P, NC, TP + CW - 1], st=st)
            xpreS = sb("xpreS", [P, NC, NB, TS + CW - 1], st=st)
            xc = sb("xc", [P, NC, T], st=st)
            rg = sb("rg", [P, NC, T], st=st)
            ig = sb("ig", [P, NC, T], st=st)
            dec = sb("dec", [P, NC, T], st=st)
            sp = sb("sp", [P, 4, NC], st=st)
            ah0 = sb("ah0", [P, NC, NB], st=st)
            hlast = sb("hlast", [P, NC, 1 + NB], st=st)
        with ExitStack() as peer:
            xh = sb("xh", [P, NC, T], F32R, st=peer)
            xl = sb("xl", [P, NC, T], F32R, st=peer)
            uraw = sb("uraw", [P, 2, NC, P], st=peer)
            uh = sb("uh", [P, 2, NC, P], F32R, st=peer)
            ul = sb("ul", [P, 2, NC, P], F32R, st=peer)
            hg0 = sb("hg0", [P, 2, T], st=peer)
            with ExitStack() as st:
                qT = sb("qT", [P, 2 * PH, T], st=st)
                sv = sb("sv", [P, 2 * PH, TOPK], st=st)
                si = sb("si", [P, 2 * PH, TOPK], U32, st=st)
                sif = sb("sif", [P, 2 * PH, TOPK], st=st)
                cand = sb("cand", [P, PH, TOPK * TOPK], st=st)
                cand2 = sb("cand2", [P, PH, TOPK * TOPK], st=st)
                cv = sb("cv", [P, PH, TOPK], st=st)
                ci = sb("ci", [P, PH, TOPK], U32, st=st)
                cab = sb("cab", [P, 2, PH, TOPK], U32, st=st)
                cabf = sb("cabf", [P, 2, PH, TOPK], st=st)
                ex = sb("ex", [P, PH, TOPK], st=st)
                exs = sb("exs", [P, 2, PH], st=st)
                slot = sb("slot", [P, 3, NS], st=st)
            with ExitStack() as st:
                gblk = sb("gblk", [P, 2, KEYS, GB], st=st)
            with ExitStack() as st:
                vraw = sb("vraw", [P, 2, D], st=st)
                vh = sb("vh", [P, 4, D], F32R, st=st)
                vl = sb("vl", [P, 4, D], F32R, st=st)
                gt = sb("gt", [P, 2, NGB, 2, GB], st=st)
                hg1 = sb("hg1", [P, 2, T], st=st)
            hg = (hg0, hg1)
        with ExitStack() as st:
            qR = sb("qR", [HD, NH, T], st=st)
            kR = sb("kR", [HD, NKV, T], st=st)
            qS = sb("qS", [HD, NB, NH, TS], st=st)
            rot = sb("rot", [P, 2, T], st=st)
            rc = sb("rc", [P, 2, T], st=st)
            wv_sb = sb("wv_sb", [P, NC, NKV * HD], st=st)
            vtok = sb("vtok", [P, TT, NKV * HD], st=st)
            vnew = sb("vnew", [TS, NB, NKV * HD], st=st)
            kc_sb = sb("kc_sb", [HD, NB, NKV, WIN], st=st)
            vc_sb = sb("vc_sb", [P, NB, NKV * HD], st=st)
            pr = sb("pr", [P, GRP, 2 * WIN], st=st)
            prT = sb("prT", [P, 2 * GRP, P], st=st)
            pss = sb("pss", [P, NB, WIN + TS], st=st)
            pssT = sb("pssT", [P, NB, P], st=st)
            pssN = sb("pssN", [TS, NB, P], st=st)
            sm = sb("sm", [P, 6, NB], st=st)

        def halves(lo):
            return ps[:, lo:lo + 2, 0:H2]

        def two(ap):
            return ap.rearrange("p (h t) -> p h t", h=2)

        def dbank(d):
            return 2 * (d % 2)

        def wait_stored(eng, l):
            for i in range(2):
                eng.wait_ge(sem(f"g_stored{l}_{i}"), 16 * ((NGB + 1 - i) // 2))
                eng.wait_ge(sem(f"s_stored{l}_{i}"), 16 * (NA // 2))

        block = ctx.enter_context(nc.Block())

        @block.sync
        def _(spq):
            spq.dma_start(xT[:, :, :], xin).then_inc(sem("x_loaded"), 16)
            spq.dma_start(cst[:, :], consts).then_inc(sem("consts_loaded"), 16)
            spq.dma_start(prm[:, :], params).then_inc(sem("consts_loaded"), 16)

            def load_weights(lo, hi):
                for w in range(lo, hi):
                    if w >= RING:
                        spq.wait_ge(sem("tile_done"), tiles_made(w - RING))
                    spq.dma_start(wring[:, w % RING], wts[w]).then_inc(sem(f"w_loaded{w % RING}"), 16)

            def hidden(l):
                def step(n, i):
                    spq.wait_ge(sem(f"u_split{l}"), n + 1)
                    spq.dma_start(uraw[:, i], tile_of(uT[l], n + 2)).then_inc(sem(f"u_loaded{l}_{i}"), 16)
                    spq.wait_ge(sem(f"s_free{l}"), n + 1)
                    spq.dma_start(tile_of(s_dram[l], n), hg0[:, i]).then_inc(sem(f"s_stored{l}_{i}"), 16)

                for i in range(2):
                    spq.dma_start(uraw[:, i], uT[l, i]).then_inc(sem(f"u_loaded{l}_{i}"), 16)
                with spq.Fori(0, NA1 // 2) as it:
                    for i in range(2):
                        step(it * 2 + i, i)
                for b in range(NGB):
                    with spq.Fori(0, 2) as it:
                        for i in range(2):
                            step(it * 2 + (NA1 + 4 * b + i), i)
                    spq.wait_ge(sem(f"g_copied{l}"), GB // 4 * (b + 1))
                    spq.dma_start(gate_dram[l, b], gblk[:, b % 2]).then_inc(sem(f"g_stored{l}_{b % 2}"), 16)
                wait_stored(spq, l)

            def output(l):
                def gates_and_v(g, j, fresh):
                    if not fresh:
                        spq.wait_ge(sem(f"h_mul{l}"), 2 * g - 2)
                    spq.dma_start(gt[:, j].rearrange("p b a t -> p b (a t)"),
                                  gates_of(l, g)).then_inc(sem(f"gt_loaded{l}_{j}"), 16)
                    for i in range(2):
                        if not (fresh and j == 0):
                            spq.wait_ge(sem(f"v_split{l}"), 2 * g + (i - 1))
                        spq.dma_start(vraw[:, i], tile_of(v[l], 2 * g + i)).then_inc(sem(f"v_loaded{l}_{i}"), 16)

                def stored_group(g, j, fresh):
                    for i in range(2):
                        if not fresh:
                            spq.wait_ge(sem(f"h_split{l}"), 2 * g + (i - 3))
                        spq.dma_start(hg[j][:, i], tile_of(s_dram[l], 2 * g + i)
                                      ).then_inc(sem(f"h_loaded{l}_{j}{i}"), 16)
                    gates_and_v(g, j, fresh)

                def new_group(g, j, last):
                    if not last:
                        for i in range(2):
                            spq.wait_ge(sem(f"u_split{l}"), 2 * g + (i + 1))
                            spq.dma_start(uraw[:, i], tile_of(uT[l], 2 * g + (i + 2))
                                          ).then_inc(sem(f"u_loaded{l}_{i}"), 16)
                    gates_and_v(g, j, False)

                for j in range(2):
                    stored_group(j, j, True)
                with spq.Fori(1, GA // 2) as it:
                    for j in range(2):
                        stored_group(it * 2 + j, j, False)
                with spq.Fori(GA // 2, NG // 2 - 1) as it:
                    for j in range(2):
                        new_group(it * 2 + j, j, False)
                for j in range(2):
                    new_group(NG - 2 + j, j, j == 1)

            def tile_of(ap, n):
                if isinstance(n, int):
                    return ap[n]
                return ap[bass.ds(n, 1)].rearrange("o p n -> (o p) n")

            def gates_of(l, g):
                src = gate_dram[l].rearrange("b p (g n) -> p b g n", n=2 * GB)
                if isinstance(g, int):
                    return src[:, :, g]
                return src[:, :, bass.ds(g, 1)].rearrange("p b o n -> p b (o n)")

            load_weights(0, W_PQ0)
            spq.wait_ge(sem("pre_copied"), NC)
            spq.wait_ge(sem("d_free"), D_A)
            spq.dma_start(convP, xpre[:, :, TP:TP + CW - 1]).then_inc(sem("states_out"), 16)
            spq.dma_start(convS, xpreS[:, :, :, TS:TS + CW - 1].rearrange("p c b k -> p (c b) k")
                          ).then_inc(sem("states_out"), 16)
            spq.wait_ge(sem("hlast_ready"), 1)
            spq.dma_start(hOut, hlast[:, :, :]).then_inc(sem("states_out"), 16)
            load_weights(W_PQ0, W_K)
            hidden(0)
            output(0)
            spq.wait_ge(sem("x_ready"), 2)
            spq.dma_start(wv_sb[:, :, :], wv).then_inc(sem("wv_loaded"), 16)
            spq.dma_start(kc_sb[:, :, :, :], kcT).then_inc(sem("kc_loaded"), 16)
            spq.dma_start(vc_sb[:, :, :], vc).then_inc(sem("vc_loaded"), 16)
            load_weights(W_K, W_Q)
            spq.wait_ge(sem("v_ready"), 1)
            spq.dma_start(vNewP, vtok[:, NQB - 1]).then_inc(sem("out_done"), 16)
            spq.dma_start(vNewS, vtok[0:NB * TS, NQB]).then_inc(sem("out_done"), 16)
            for b in range(NB):
                spq.dma_start(vnew[:, b], vtok[b * TS:(b + 1) * TS, NQB]).then_inc(sem("vnew_loaded"), 16)
            spq.wait_ge(sem("k_ready"), 2)
            spq.dma_start(kNew, kR[:, :, TP - WIN:T]).then_inc(sem("out_done"), 16)
            load_weights(W_Q, W_N)
            hidden(1)
            output(1)
            spq.wait_ge(sem("xn_ready"), 6)
            spq.dma_start(yT, xn[:, :, :]).then_inc(sem("out_done"), 16)
            spq.wait_ge(sem("states_out"), 48)
            spq.wait_ge(sem("out_done"), 16 * 4)

        @block.gpsimd
        def _(pool):
            pool.memset(ones[:, :], 1.0).then_inc(sem("ones_ready"), 1)
            pool.memset(xpre[:, :, 0:CW - 1], 0.0).then_inc(sem("pad_ready"), 1)
            pool.dma_start(xpreS[:, :, :, 0:CW - 1].rearrange("p c b k -> p (c b) k"), stconv
                           ).then_inc(sem("st_loaded"), 16)
            pool.dma_start(kKeep, kc[:, TS:WIN]).then_inc(sem("kept"), 16)
            pool.dma_start(vKeep, vc.rearrange("p b n -> b p n")[:, TS:WIN]).then_inc(sem("kept"), 16)
            for l in range(2):
                with pool.Fori(0, KEYS // 2) as it:
                    for i in range(2):
                        pool.wait_ge(sem(f"uh_ready{l}"), it * 2 + (i + 1))
                        pool.tensor_tensor(ul[:, i], uraw[:, i], uh[:, i].bitcast(F32), ALU.subtract
                                           ).then_inc(sem(f"u_split{l}"), 1)
            pool.wait_ge(sem("kept"), 32)

        @block.scalar
        def _(act):
            chain = Chain(act, sem("act_chain"))

            def square(s):
                act.wait_ge(sem("x_ready" if s else "x_loaded"), s if s else 16)
                if s:
                    act.wait_ge(sem("tile_done"), (0, D_PQ0, D_K, D_PQ1, D_N)[s])
                for c in range(NC):
                    act.activation(xn[:, c], xT[:, c], ACT.Square).then_inc(sem("sq_ready"), 1)
                act.wait_ge(sem("ms_ready"), s + 1)
                act.activation(rinv[:, :], rinv[:, :], ACT.Sqrt).then_inc(sem("rms_ready"), 1)

            def split_x(l):
                act.wait_ge(sem("xn_ready"), (2, 5)[l])
                for c in range(NC):
                    act.activation(xh[:, c], xn[:, c], ACT.Copy).then_inc(sem(f"xh_ready{l}"), 1)

            def rg_lru():
                act.wait_ge(sem("consts_loaded"), 32)
                act.activation(sp[:, 0], prm[:, P_LAM:P_LAM + NC], ACT.Exp, scale=-1.0
                               ).then_inc(sem("lam_exp"), 1)
                act.wait_ge(sem("lam_one"), 1)
                act.activation(sp[:, 2], sp[:, 1], ACT.Ln).then_inc(sem("lam_ln"), 1)
                square(0)
                for f in range(NC):
                    act.wait_ge(sem("tile_done"), D_IN + f + 1)
                    act.activation(two(gate[:, f]), halves(dbank(f)), ACT.Gelu_apprx_tanh
                                   ).then_inc(sem("d_free"), 1)
                act.wait_ge(sem("pad_ready"), 1)
                act.wait_ge(sem("st_loaded"), 16)
                for f in range(NC):
                    d = D_IN + NC + f
                    b = dbank(d)
                    act.wait_ge(sem("tile_done"), d + 1)
                    act.activation(xpre[:, f, CW - 1:CW - 1 + H2], ps[:, b, 0:H2], ACT.Copy)
                    act.activation(xpre[:, f, CW - 1 + H2:CW - 1 + TP], ps[:, b + 1, 0:TP - H2], ACT.Copy
                                   ).then_inc(sem("pre_copied"), 1)
                    act.activation(xpreS[:, f, :, CW - 1:],
                                   ps[:, b + 1, TP - H2:H2].rearrange("p (b s) -> p b s", b=NB),
                                   ACT.Copy).then_inc(sem("d_free"), 1)
                for k, (d0, dst, bias) in enumerate(((D_A, rg, P_BA), (D_X, ig, P_BX))):
                    for f in range(NC):
                        act.wait_ge(sem("tile_done"), d0 + f + 1)
                        act.activation(two(dst[:, f]), halves(dbank(d0 + f)), ACT.Sigmoid,
                                       bias=prm[:, bias + f:bias + f + 1]).then_inc(sem("d_free"), 1)
                act.wait_ge(sem("d_free"), D_OUT)
                act.wait_ge(sem("sp_ready"), 1)
                for f in range(NC):
                    act.activation(dec[:, f], rg[:, f], ACT.Exp, scale=sp[:, 3, f:f + 1]
                                   ).then_inc(sem("dec_ready"), 1)
                act.wait_ge(sem("dec_ready"), NC)
                for f in range(NC):
                    act.activation(rg[:, f], rg[:, f], ACT.Tanh, scale=sp[:, 3, f:f + 1]
                                   ).then_inc(sem("tanh_ready"), 1)
                for f in range(NC):
                    act.wait_ge(sem("m2_ready"), f + 1)
                    act.activation(rg[:, f], rg[:, f], ACT.Sqrt).then_inc(sem("mult_ready"), 1)

            def copy_queries(d0):
                for f in range(2 * PH):
                    act.wait_ge(sem("tile_done"), d0 + f + 1)
                    act.activation(two(qT[:, f]), halves(dbank(d0 + f)), ACT.Copy
                                   ).then_inc(sem("d_free"), 1)

            def hidden(l):
                def split_u(n, i, fresh):
                    act.wait_ge(sem(f"u_loaded{l}_{i}"), (n - i) * 8 + 16)
                    if not fresh:
                        act.wait_ge(sem(f"s_full{l}"), n - 1)
                    act.activation(uh[:, i], uraw[:, i], ACT.Copy).then_inc(sem(f"uh_ready{l}"), 1)

                def step(n, i, fresh):
                    split_u(n + 1, 1 - i, fresh and i == 0)
                    act.wait_ge(sem(f"s_full{l}"), n + 1)
                    if not fresh:
                        act.wait_ge(sem(f"s_stored{l}_{i}"), (n - i) * 8)
                    act.activation(two(hg0[:, i]), halves(2 * i), ACT.Gelu).then_inc(sem(f"s_free{l}"), 1)

                def copy_scores(t):
                    act.wait_ge(sem(f"sc_done{l}"), t + 1)
                    if t:
                        act.wait_ge(sem(f"sc_read{l}"), t)
                    act.activation(sc[:, :, :].rearrange("p (b j) k -> p b (j k)", b=4), ps[:, 4:8, :],
                                   ACT.Copy).then_inc(sem(f"sc_copied{l}"), 1)

                def copy_gates(n, b, k):
                    for q in range(4):
                        act.wait_ge(sem(f"g_done{l}"), (n - NA1) * 4 + (q + 1))
                        act.activation(gblk[:, b % 2, :, bass.ds(k + 4 * q, 4)],
                                       ps[:, 4 + q, :].rearrange("p (t k) -> p k t", t=4),
                                       ACT.Copy).then_inc(sem(f"g_copied{l}"), 1)

                copy_scores(0)
                split_u(0, 0, True)
                for t in range(TT):
                    if t == 0:
                        for i in range(2):
                            step(i, i, True)
                    with act.Fori(1 if t == 0 else UB // 2 * t, UB // 2 * t + UB // 2 - 1) as it:
                        for i in range(2):
                            step(it * 2 + i, i, False)
                    if t + 1 < TT:
                        copy_scores(t + 1)
                    for i in range(2):
                        step(UB * (t + 1) - 2 + i, i, False)
                    act.wait_ge(sem(f"ex_in{l}"), t + 1)
                    act.activation(ex[:, :, :], ex[:, :, :], ACT.Exp).then_inc(sem(f"ex_out{l}"), 1)
                    act.wait_ge(sem(f"turned{l}"), t + 1)
                    act.activation(slotT[:, :, TLO[t]:TLO[t] + P], ps[:, 4, 0:3 * P].rearrange("p (a t) -> p a t", a=3),
                                   ACT.Copy).then_inc(sem(f"slot_ready{l}"), 1)
                for b in range(NGB):
                    if b >= 2:
                        act.wait_ge(sem(f"g_stored{l}_{b % 2}"), 16 * (b // 2))
                    with act.Fori(0, 2) as it:
                        for i in range(2):
                            n = it * 2 + (NA1 + 4 * b + i)
                            step(n, i, False)
                            copy_gates(n, b, it * 32 + 16 * i)
                split_u(NA + 1, 1, False)

            def output(l):
                def split_v_h(g, j, fresh):
                    for i in range(2):
                        act.wait_ge(sem(f"v_loaded{l}_{i}"), g * 16 + 16)
                        if not fresh:
                            act.wait_ge(sem(f"o_full{l}"), g * 8 - 8)
                        act.activation(vh[:, 2 * j + i], vraw[:, i], ACT.Copy).then_inc(sem(f"vh_ready{l}"), 1)
                    for i in range(2):
                        act.wait_ge(sem(f"h_mul{l}"), 2 * g + (i + 1))
                        act.activation(hh[:, 2 * j + i], hg[j][:, i], ACT.Copy).then_inc(sem(f"hh_ready{l}"), 1)

                def new_group(g, j, last):
                    if not last:
                        for i in range(2):
                            act.wait_ge(sem(f"u_loaded{l}_{i}"), g * 16 + 32)
                            act.wait_ge(sem(f"s_full{l}"), 2 * g + (i + 1))
                            act.activation(uh[:, i], uraw[:, i], ACT.Copy).then_inc(sem(f"uh_ready{l}"), 1)
                    for i in range(2):
                        act.wait_ge(sem(f"s_full{l}"), 2 * g + (i + 1))
                        act.wait_ge(sem(f"h_split{l}"), 2 * g + (i - 3))
                        act.activation(two(hg[j][:, i]), halves(2 * i), ACT.Gelu).then_inc(sem(f"s_free{l}"), 1)
                    split_v_h(g, j, False)

                wait_stored(act, l)
                for j in range(2):
                    split_v_h(j, j, True)
                with act.Fori(1, GA // 2) as it:
                    for j in range(2):
                        split_v_h(it * 2 + j, j, False)
                with act.Fori(GA // 2, NG // 2 - 1) as it:
                    for j in range(2):
                        new_group(it * 2 + j, j, False)
                for j in range(2):
                    new_group(NG - 2 + j, j, j == 1)

            def rope_shift(first_tile, n):
                for f in range(n):
                    d = first_tile + f
                    act.wait_ge(sem("tile_done"), d + 1)
                    if d - D_K >= 2:
                        act.wait_ge(sem("roped"), d - D_K - 1)
                    for q in range(4):
                        src = 32 * (q ^ 1)
                        ins = act.activation(two(rot[32 * q:32 * q + 32, d % 2]),
                                             ps[src:src + 32, dbank(d):dbank(d) + 2, 0:H2], ACT.Copy)
                    ins.then_inc(sem("rot_ready"), 1)

            def attention():
                rope_shift(D_K, 2)
                act.wait_ge(sem("v_done"), 1)
                act.activation(vtok[:, 0:4].rearrange("p (b t) n -> p b (t n)", b=2), ps[:, 4:6, :], ACT.Copy)
                act.activation(vtok[0:NB * TS, 4], ps[0:NB * TS, 6, 0:NKV * HD], ACT.Copy
                               ).then_inc(sem("v_ready"), 1)
                rope_shift(D_Q, NC)
                for u in range(NQB * NKV):
                    act.wait_ge(sem("pmax"), u + 1)
                    for g in range(GRP):
                        act.activation(pr[:, g], pr[:, g], ACT.Exp, bias=sm[:, 1, g:g + 1],
                                       accum_out=sm[:, 2, g:g + 1])
                    act.activation(sm[:, 3, 0:GRP], sm[:, 3, 0:GRP], ACT.Exp).then_inc(sem("pexp"), 1)
                    act.wait_ge(sem("pturn"), u + 1)
                    act.activation(prT[:, :, :].rearrange("p (b j) k -> p b (j k)", b=2), ps[:, 2:4, :],
                                   ACT.Copy).then_inc(sem("prT_ready"), 1)
                act.wait_ge(sem("smax"), 1)
                act.activation(pss[:, :, :], pss[:, :, :], ACT.Exp).then_inc(sem("sexp"), 1)
                act.activation(sm[:, 3], sm[:, 3], ACT.Exp).then_inc(sem("sexp"), 1)
                act.wait_ge(sem("sturn"), 1)
                act.activation(pssT[:, :, :].rearrange("p (b j) k -> p b (j k)", b=2), ps[:, 4:6, :], ACT.Copy)
                act.activation(pssN[:, :, :].rearrange("p (b j) k -> p b (j k)", b=2), ps[0:TS, 6:8, :],
                               ACT.Copy).then_inc(sem("pssT_ready"), 1)

            rg_lru()
            for l, d0 in ((0, D_PQ0), (1, D_PQ1)):
                if l == 1:
                    square(2)
                    attention()
                square((1, 3)[l])
                split_x(l)
                copy_queries(d0)
                hidden(l)
                output(l)
            square(4)

        @block.vector
        def _(dve):
            chain = Chain(dve, sem("dve_chain"))

            def norm_stats(s):
                dve.wait_ge(sem("sum_done"), s + 1)
                dve.tensor_scalar(two(rinv[:, :]), halves(4), 1.0 / D, EPS, ALU.mult, ALU.add
                                  ).then_inc(sem("ms_ready"), 1)
                dve.wait_ge(sem("rms_ready"), s + 1)
                chain.did(dve.reciprocal(rinv[:, :], rinv[:, :]))
                chain.settle()

            def norm_apply(off):
                for c in range(NC):
                    ins = dve.scalar_tensor_tensor(xn[:, c], xT[:, c], prm[:, off + c:off + c + 1],
                                                   rinv[:, :], ALU.mult, ALU.mult)
                ins.then_inc(sem("xn_ready"), 1)

            def add_residual(d0):
                for f in range(NC):
                    dve.wait_ge(sem("tile_done"), d0 + f + 1)
                    dve.tensor_tensor(two(xT[:, f]), two(xT[:, f]), halves(dbank(d0 + f)), ALU.add
                                      ).then_inc(sem("d_free"), 1)

            def rg_lru():
                dve.wait_ge(sem("consts_loaded"), 32)
                dve.wait_ge(sem("lam_exp"), 1)
                dve.tensor_scalar(sp[:, 1], sp[:, 0], 1.0, None, ALU.add).then_inc(sem("lam_one"), 1)
                dve.wait_ge(sem("lam_ln"), 1)
                chain.did(dve.tensor_scalar(sp[:, 1], sp[:, 1], -1.0, None, ALU.add))
                chain.settle()
                chain.did(dve.tensor_scalar(sp[:, 3], sp[:, 1], 0.0, None, ALU.is_equal))
                chain.settle()
                chain.did(dve.tensor_tensor(sp[:, 1], sp[:, 1], sp[:, 3], ALU.add))
                chain.did(dve.tensor_tensor(sp[:, 2], sp[:, 2], sp[:, 3], ALU.add))
                chain.settle()
                chain.did(dve.reciprocal(sp[:, 1], sp[:, 1]))
                chain.settle()
                chain.did(dve.tensor_tensor(sp[:, 2], sp[:, 2], sp[:, 0], ALU.mult))
                chain.settle()
                dve.scalar_tensor_tensor(sp[:, 3], sp[:, 2], -8.0, sp[:, 1], ALU.mult, ALU.mult
                                         ).then_inc(sem("sp_ready"), 1)
                norm_stats(0)
                norm_apply(N_RG)
                for f in range(NC):
                    dve.wait_ge(sem("pre_copied"), f + 1)
                    dve.wait_ge(sem("d_free"), D_IN + NC + f + 1)
                    outs = (xc[:, f, 0:TP], xc[:, f, TP:T].rearrange("p (b s) -> p b s", b=NB))

                    def tap(k):
                        return (xpre[:, f, k:k + TP], xpreS[:, f, :, k:k + TS])
                    for k in range(CW):
                        w = prm[:, P_CW + k * NC + f:P_CW + k * NC + f + 1]
                        for o, i in zip(outs, tap(k)):
                            if k == 0:
                                ins = dve.tensor_scalar(o, i, w, prm[:, P_CB + f:P_CB + f + 1],
                                                        ALU.mult, ALU.add)
                            else:
                                ins = dve.scalar_tensor_tensor(o, i, w, o, ALU.mult, ALU.add)
                            if k < CW - 1:
                                chain.did(ins)
                        if k < CW - 1:
                            chain.settle()
                    ins.then_inc(sem("xc_ready"), 1)
                for f in range(NC):
                    dve.wait_ge(sem("tanh_ready"), f + 1)
                    chain.did(dve.tensor_scalar(xn[:, f], rg[:, f], -1.0, 1.0, ALU.mult, ALU.add))
                    chain.did(dve.tensor_tensor(ig[:, f], ig[:, f], xc[:, f], ALU.mult))
                    chain.settle()
                    chain.did(dve.reciprocal(xn[:, f], xn[:, f]))
                    chain.settle()
                    dve.scalar_tensor_tensor(rg[:, f], rg[:, f], -2.0, xn[:, f], ALU.mult, ALU.mult
                                             ).then_inc(sem("m2_ready"), 1)
                for f in range(NC):
                    dve.wait_ge(sem("mult_ready"), f + 1)
                    chain.did(dve.tensor_tensor(ig[:, f], ig[:, f], rg[:, f], ALU.mult))
                starts = dec[:, :, TP:T].rearrange("p c (b s) -> p c b s", b=NB)[:, :, :, 0]
                bstarts = ig[:, :, TP:T].rearrange("p c (b s) -> p c b s", b=NB)[:, :, :, 0]
                dve.wait_ge(sem("dec_ready"), NC)
                chain.did(dve.tensor_tensor(ah0[:, :, :], starts,
                                            prm[:, P_H0:P_H0 + NC * NB].rearrange("p (c b) -> p c b", c=NC),
                                            ALU.mult))
                chain.settle()
                chain.did(dve.tensor_tensor(bstarts, bstarts, ah0[:, :, :], ALU.add))
                chain.did(dve.memset(starts, 0.0))
                chain.settle()
                for f in range(NC):
                    chain.did(dve.tensor_tensor_scan(rg[:, f], dec[:, f], ig[:, f], 0.0, ALU.mult, ALU.add))
                chain.settle()
                chain.did(dve.tensor_copy(hlast[:, :, 0:1], rg[:, :, TP - 1:TP]))
                dve.tensor_copy(hlast[:, :, 1:1 + NB],
                                rg[:, :, TP:T].rearrange("p c (b s) -> p c b s", b=NB)[:, :, :, TS - 1]
                                ).then_inc(sem("hlast_ready"), 1)
                for f in range(NC):
                    dve.tensor_tensor(xn[:, f], rg[:, f], gate[:, f], ALU.mult).then_inc(sem("hg_ready"), 1)
                add_residual(D_OUT)
                dve.wait_ge(sem("d_free"), D_PQ0)
                dve.wait_ge(sem("states_out"), 48)
                dve.memset(rinv[:, 0:1], 0.0).then_inc(sem("x_ready"), 1)

            def topk(l):
                def tile(t):
                    dve.wait_ge(sem(f"sc_copied{l}"), t + 1)
                    for j in range(2 * PH):
                        chain.did(dve.max(sv[:, j, 0:8], sc[:, j]))
                    chain.settle()
                    for j in range(2 * PH):
                        chain.did(dve.max_index(si[:, j, 0:8], sv[:, j, 0:8], sc[:, j]))
                        chain.did(dve.match_replace(sc2[:, j], sv[:, j, 0:8], sc[:, j], BIG))
                    chain.settle()
                    for j in range(2 * PH):
                        ins = dve.max(sv[:, j, 8:16], sc2[:, j])
                        if j < 2 * PH - 1:
                            chain.did(ins)
                    ins.then_inc(sem(f"sc_read{l}"), 1)
                    chain.settle()
                    dve.wait_ge(sem(f"sc_read{l}"), t + 1)
                    for j in range(2 * PH):
                        chain.did(dve.max_index(si[:, j, 8:16], sv[:, j, 8:16], sc2[:, j]))
                    s4 = sv[:, :, :].rearrange("p (h a) k -> p h a k", a=2)
                    chain.did(dve.tensor_tensor(
                        cand[:, :, :].rearrange("p h (i j) -> p h i j", i=TOPK),
                        s4[:, :, 0].unsqueeze(3).broadcast_to([P, PH, TOPK, TOPK]),
                        s4[:, :, 1].unsqueeze(2).broadcast_to([P, PH, TOPK, TOPK]), ALU.add))
                    chain.settle()
                    chain.did(dve.tensor_copy(sif[:, :, :], si[:, :, :]))
                    for h in range(PH):
                        chain.did(dve.max(cv[:, h, 0:8], cand[:, h]))
                    chain.settle()
                    for h in range(PH):
                        chain.did(dve.max_index(ci[:, h, 0:8], cv[:, h, 0:8], cand[:, h]))
                        chain.did(dve.match_replace(cand2[:, h], cv[:, h, 0:8], cand[:, h], BIG))
                    chain.settle()
                    for h in range(PH):
                        chain.did(dve.max(cv[:, h, 8:16], cand2[:, h]))
                    chain.settle()
                    dve.tensor_tensor(ex[:, :, :], cv[:, :, :], cv[:, :, 0:1].broadcast_to([P, PH, TOPK]),
                                      ALU.subtract).then_inc(sem(f"ex_in{l}"), 1)
                    for h in range(PH):
                        chain.did(dve.max_index(ci[:, h, 8:16], cv[:, h, 8:16], cand2[:, h]))
                    chain.settle()
                    chain.did(dve.tensor_scalar(cab[:, 0], ci[:, :, :], 4, None, ALU.logical_shift_right))
                    chain.did(dve.tensor_scalar(cab[:, 1], ci[:, :, :], TOPK - 1, None, ALU.bitwise_and))
                    chain.settle()
                    chain.did(dve.tensor_copy(cabf[:, :, :, :], cab[:, :, :, :]))
                    chain.settle()
                    f4 = sif[:, :, :].rearrange("p (h a) k -> p h a k", a=2)
                    eq = [b_[:, :, :].rearrange("p h (k i) -> p h k i", k=TOPK) for b_ in (cand, cand2)]
                    for a in range(2):
                        chain.did(dve.tensor_tensor(
                            eq[a], cabf[:, a].unsqueeze(3).broadcast_to([P, PH, TOPK, TOPK]),
                            iota[:, 0:TOPK].unsqueeze(1).unsqueeze(1).broadcast_to([P, PH, TOPK, TOPK]),
                            ALU.is_equal))
                    chain.settle()
                    for a in range(2):
                        chain.did(dve.tensor_tensor(
                            eq[a], eq[a], f4[:, :, a].unsqueeze(2).broadcast_to([P, PH, TOPK, TOPK]),
                            ALU.mult))
                    chain.settle()
                    if t:
                        dve.wait_ge(sem(f"turned{l}"), t)
                    for a in range(2):
                        chain.did(dve.tensor_reduce(slot[:, a].rearrange("p (h k) -> p h k", h=PH), eq[a],
                                                    X, ALU.add))
                    dve.wait_ge(sem(f"ex_out{l}"), t + 1)
                    chain.did(dve.tensor_reduce(exs[:, 0], ex[:, :, :], X, ALU.add))
                    chain.settle()
                    chain.did(dve.reciprocal(exs[:, 1], exs[:, 0]))
                    chain.settle()
                    dve.tensor_tensor(slot[:, 2].rearrange("p (h k) -> p h k", h=PH), ex[:, :, :],
                                      exs[:, 1].unsqueeze(2).broadcast_to([P, PH, TOPK]), ALU.mult
                                      ).then_inc(sem(f"slots{l}"), 1)
                for t in range(TT):
                    tile(t)

            def one_hots(l):
                dve.wait_ge(sem(f"slot_ready{l}"), TT)

                def batch(it, first):
                    for q in range(4):
                        if not first:
                            dve.wait_ge(sem(f"g_done{l}"), it * 4 + (q - 3))
                        for i in range(4):
                            k = 4 * q + i

                            def col(a):
                                if isinstance(it, int):
                                    return slotT[:, a, it * 16 + k:it * 16 + k + 1]
                                return slotT[:, a, bass.ds(it * 16 + k, 1)]
                            dve.tensor_scalar(hotA[:, k], iota, col(0), None, ALU.is_equal)
                            ins = dve.tensor_scalar(hotB[:, k], iota, col(1), col(2), ALU.is_equal, ALU.mult)
                        ins.then_inc(sem(f"hot{l}"), 1)

                batch(0, True)
                with dve.Fori(1, T // 16) as it:
                    batch(it, False)

            def split_x(l):
                for c in range(NC):
                    dve.wait_ge(sem(f"xh_ready{l}"), c + 1)
                    dve.tensor_tensor(xl[:, c], xn[:, c], xh[:, c].bitcast(F32), ALU.subtract
                                      ).then_inc(sem(f"xl_ready{l}"), 1)

            def output(l):
                def evac(g, c):
                    dve.wait_ge(sem(f"o_full{l}"), g * 8 + (c + 1))
                    dve.tensor_tensor(two(xT[:, c]), two(xT[:, c]), halves(4 + 2 * (c % 2)), ALU.add
                                      ).then_inc(sem(f"o_free{l}"), 1)

                def step(g, j, first, stored):
                    def ev(c):
                        if not (first and j == 0):
                            evac(g - 1, c)
                    for i in range(2):
                        ev(i)
                        if stored:
                            dve.wait_ge(sem(f"h_loaded{l}_{j}{i}"), (g - j) * 8 + 16)
                        else:
                            dve.wait_ge(sem(f"s_free{l}"), 2 * g + (i + 1))
                        dve.wait_ge(sem(f"gt_loaded{l}_{j}"), (g - j) * 8 + 16)
                        hb = hg[j][:, i].rearrange("p (b t) -> p b t", b=NGB)
                        dve.tensor_tensor(hb, hb, gt[:, j, :, i], ALU.mult).then_inc(sem(f"h_mul{l}"), 1)
                    for i in range(2):
                        ev(2 + i)
                        dve.wait_ge(sem(f"vh_ready{l}"), 2 * g + (i + 1))
                        dve.tensor_tensor(vl[:, 2 * j + i], vraw[:, i], vh[:, 2 * j + i].bitcast(F32),
                                          ALU.subtract).then_inc(sem(f"v_split{l}"), 1)
                    for i in range(2):
                        ev(4 + i)
                        dve.wait_ge(sem(f"hh_ready{l}"), 2 * g + (i + 1))
                        dve.tensor_tensor(hl[:, 2 * j + i], hg[j][:, i], hh[:, 2 * j + i].bitcast(F32),
                                          ALU.subtract).then_inc(sem(f"h_split{l}"), 1)
                    for i in range(2):
                        ev(6 + i)

                for j in range(2):
                    step(j, j, True, True)
                with dve.Fori(1, GA // 2) as it:
                    for j in range(2):
                        step(it * 2 + j, j, False, True)
                with dve.Fori(GA // 2, NG // 2) as it:
                    for j in range(2):
                        step(it * 2 + j, j, False, False)
                for c in range(NC):
                    evac(NG - 1, c)
                dve.wait_ge(sem(f"o_free{l}"), NG * NC)
                dve.memset(sm0, 0.0).then_inc(sem("x_ready"), 1)

            sm0 = rinv[:, 0:1]

            def rope(d0, n, dst):
                for f in range(n):
                    d = d0 + f
                    r = d % 2
                    dve.wait_ge(sem("rot_ready"), d - D_K + 1)
                    chain.did(dve.tensor_tensor(rot[:, r], rot[:, r], cst[:, C_SIN:C_SIN + T], ALU.mult))
                    dve.tensor_tensor(two(rc[:, r]), halves(dbank(d)), two(cst[:, C_COS:C_COS + T]), ALU.mult
                                      ).then_inc(sem("d_free"), 1)
                    chain.settle()
                    dve.wait_ge(sem("d_free"), d + 1)
                    chain.did(dve.tensor_tensor(dst[:, 2 * f], rc[0:HD, r], rot[0:HD, r], ALU.add))
                    ins = dve.tensor_tensor(dst[:, 2 * f + 1], rc[HD:P, r], rot[HD:P, r], ALU.add)
                    ins.then_inc(sem("roped"), 1)

            def attention():
                norm_stats(2)
                norm_apply(N_KV)
                rope(D_K, 2, kR)
                dve.wait_ge(sem("roped"), 2)
                dve.wait_ge(sem("tile_done"), D_Q)
                dve.wait_ge(sem("v_done"), 1)
                dve.memset(sm0b, 0.0).then_inc(sem("k_ready"), 2)
                norm_apply(N_AT)
                rope(D_Q, NC, qR)
                dve.wait_ge(sem("roped"), 2 + NC)
                dve.tensor_copy(qS[:, :, :, :], qR[:, :, TP:T].rearrange("p h (b s) -> p b h s", b=NB)
                                ).then_inc(sem("qS_ready"), 1)
                ob = xn
                for n in range(NQB):
                    for kv in range(NKV):
                        u = n * NKV + kv
                        lo = 0 if n else WIN
                        dve.wait_ge(sem("p_scores"), u + 1)
                        if u:
                            dve.wait_ge(sem("pturn"), u)
                        elif True:
                            dve.wait_ge(sem("tile_done"), D_O)
                        w = 2 * WIN - lo
                        chain.did(dve.scalar_tensor_tensor(
                            pr[:, :, lo:], ps[:, 0:2, :].rearrange("p b (g k) -> p (b g) k", g=2)[:, :, lo:],
                            HD ** -0.5, cst[:, C_MP + lo:C_MP + 2 * WIN].unsqueeze(1).broadcast_to([P, GRP, w]),
                            ALU.mult, ALU.add))
                        if not n:
                            chain.did(dve.memset(pr[:, :, 0:WIN], BIG))
                        chain.settle()
                        chain.did(dve.tensor_reduce(sm[:, 0, 0:GRP], pr[:, :, :], X, ALU.max))
                        chain.settle()
                        sk = prm[:, P_SINK + kv * GRP:P_SINK + (kv + 1) * GRP]
                        chain.did(dve.tensor_tensor(sm[:, 0, 0:GRP], sm[:, 0, 0:GRP], sk, ALU.max))
                        chain.settle()
                        chain.did(dve.tensor_scalar(sm[:, 1, 0:GRP], sm[:, 0, 0:GRP], -1.0, None, ALU.mult))
                        dve.tensor_tensor(sm[:, 3, 0:GRP], sk, sm[:, 0, 0:GRP], ALU.subtract
                                          ).then_inc(sem("pmax"), 1)
                        dve.wait_ge(sem("pexp"), u + 1)
                        chain.did(dve.tensor_tensor(sm[:, 4, 0:GRP], sm[:, 2, 0:GRP], sm[:, 3, 0:GRP], ALU.add))
                        chain.settle()
                        chain.did(dve.reciprocal(sm[:, 5, 0:GRP], sm[:, 4, 0:GRP]))
                        chain.settle()
                        dve.tensor_tensor(pr[:, :, :], pr[:, :, :],
                                          sm[:, 5, 0:GRP].unsqueeze(2).broadcast_to([P, GRP, 2 * WIN]), ALU.mult
                                          ).then_inc(sem("p_ready"), 1)
                        dve.wait_ge(sem("p_out"), u + 1)
                        for e in range(2):
                            ins = dve.tensor_copy(
                                ob[e * HD:(e + 1) * HD, 2 * kv:2 * kv + 2, n * WIN:(n + 1) * WIN],
                                ps[0:HD, 7, :].rearrange("p (g e q) -> p g e q", g=2, e=2)[:, :, e])
                            if e == 0:
                                chain.did(ins)
                        ins.then_inc(sem("o_copied"), 1)
                dve.wait_ge(sem("s_scores"), 1)
                chain.did(dve.scalar_tensor_tensor(
                    pss[:, :, :], ps[:, 0:4, :].rearrange("p b (j k) -> p (b j) k", j=2)[:, :, 0:WIN + TS],
                    HD ** -0.5, cst[:, C_MS:C_MS + WIN + TS].unsqueeze(1).broadcast_to([P, NB, WIN + TS]),
                    ALU.mult, ALU.add))
                chain.settle()
                chain.did(dve.tensor_reduce(sm[:, 0], pss[:, :, :], X, ALU.max))
                chain.settle()
                chain.did(dve.tensor_scalar(sm[:, 0], sm[:, 0], prm[:, P_SKS:P_SKS + 1], None, ALU.max))
                chain.settle()
                chain.did(dve.tensor_scalar(sm[:, 3], sm[:, 0], -1.0, prm[:, P_SKS:P_SKS + 1], ALU.mult, ALU.add))
                chain.settle()
                dve.tensor_tensor(pss[:, :, :], pss[:, :, :],
                                  sm[:, 0].unsqueeze(2).broadcast_to([P, NB, WIN + TS]), ALU.subtract
                                  ).then_inc(sem("smax"), 1)
                dve.wait_ge(sem("sexp"), 2)
                chain.did(dve.tensor_reduce(sm[:, 4], pss[:, :, :], X, ALU.add))
                chain.settle()
                chain.did(dve.tensor_tensor(sm[:, 4], sm[:, 4], sm[:, 3], ALU.add))
                chain.settle()
                chain.did(dve.reciprocal(sm[:, 5], sm[:, 4]))
                chain.settle()
                dve.tensor_tensor(pss[:, :, :], pss[:, :, :],
                                  sm[:, 5].unsqueeze(2).broadcast_to([P, NB, WIN + TS]), ALU.mult
                                  ).then_inc(sem("s_ready"), 1)
                dve.wait_ge(sem("s_out"), 1)
                for g in range(GRP):
                    e = g % 2
                    for bb in range(2):
                        ins = dve.tensor_copy(
                            ob[e * HD:(e + 1) * HD, :, TP:T].rearrange("p (k c) (b s) -> p c b k s", k=NKV, b=NB)
                            [:, g // 2, 4 * bb:4 * bb + 4],
                            ps[0:HD, bb, :].rearrange("p (b k g s) -> p g b k s", b=4, k=NKV, g=GRP)[:, g])
                        if g < GRP - 1 or bb == 0:
                            chain.did(ins)
                ins.then_inc(sem("o_copied"), 1)
                add_residual(D_O)
                dve.wait_ge(sem("d_free"), D_PQ1)
                dve.memset(rinv[:, 0:1], 0.0).then_inc(sem("x_ready"), 1)

            sm0b = rc[:, 0, 0:1]

            rg_lru()
            for l, (s, off) in enumerate(((1, N_F0), (3, N_F1))):
                if l == 1:
                    attention()
                norm_stats(s)
                norm_apply(off)
                split_x(l)
                topk(l)
                one_hots(l)
                output(l)
            norm_stats(4)
            norm_apply(N_FIN)

        @block.tensor
        def _(pe):
            def sum_squares(s):
                if s == 0:
                    pe.wait_ge(sem("ones_ready"), 1)
                for c in range(NC):
                    pe.wait_ge(sem("sq_ready"), NC * s + c + 1)
                    for h in range(2):
                        ins = pe.matmul(ps[:, 4 + h, 0:H2], ones[:, :], xn[:, c, h * H2:(h + 1) * H2],
                                        start=(c == 0), stop=(c == NC - 1))
                ins.then_inc(sem("sum_done"), 1)

            def project(w0, d0, n, src):
                for f in range(n):
                    w, d = w0 + f, d0 + f
                    pe.wait_ge(sem(f"w_loaded{w % RING}"), 16 * (w // RING + 1))
                    if d >= 2:
                        pe.wait_ge(sem("d_free"), d - 1)
                    for c in range(NC):
                        for h in range(2):
                            ins = pe.matmul(ps[:, dbank(d) + h, 0:H2], wring[:, w % RING, c],
                                            src[:, c, h * H2:(h + 1) * H2], start=(c == 0), stop=(c == NC - 1))
                    ins.then_inc(sem("tile_done"), 1)

            def rg_gates():
                for w, d0 in ((W_A, D_A), (W_X, D_X)):
                    pe.wait_ge(sem(f"w_loaded{w % RING}"), 16 * (w // RING + 1))
                    for f in range(NC):
                        d = d0 + f
                        pe.wait_ge(sem("xc_ready"), f + 1)
                        pe.wait_ge(sem("d_free"), d - 1)
                        for h in range(2):
                            ins = pe.matmul(ps[:, dbank(d) + h, 0:H2], wring[:, w % RING, f],
                                            xc[:, f, h * H2:(h + 1) * H2], start=True, stop=True)
                        ins.then_inc(sem("tile_done"), 1)

            def up(l, n, i, fresh):
                pe.wait_ge(sem(f"u_split{l}"), n + 1)
                if not fresh:
                    pe.wait_ge(sem(f"s_free{l}"), n - 1)
                for c in range(NC):
                    for k, (w, x) in enumerate(((uh, xh), (uh, xl), (ul, xh))):
                        for h in range(2):
                            ins = pe.matmul(ps[:, 2 * i + h, 0:H2], w[:, i, c], x[:, c, h * H2:(h + 1) * H2],
                                            start=(c == 0 and k == 0), stop=(c == NC - 1 and k == 2))
                ins.then_inc(sem(f"s_full{l}"), 1)

            def hidden(l):
                def scores(t):
                    if t:
                        pe.wait_ge(sem(f"sc_copied{l}"), t)
                    if t > 1:
                        pe.wait_ge(sem(f"slot_ready{l}"), t - 1)
                    for j in range(2 * PH):
                        sk = P_SK + (2 * l + j % 2) * KEYS
                        ins = pe.matmul(ps[:, 4 + j // 4, (j % 4) * P:(j % 4 + 1) * P],
                                        qT[:, j, TLO[t]:TLO[t] + P], prm[:, sk:sk + KEYS], start=True, stop=True)
                    ins.then_inc(sem(f"sc_done{l}"), 1)

                def gates(n, first):
                    for q in range(4):
                        pe.wait_ge(sem(f"hot{l}"), (n - NA1) * 4 + (q + 1))
                        if not first:
                            pe.wait_ge(sem(f"g_copied{l}"), (n - NA1) * 4 + (q - 3))
                        elif q == 0:
                            pe.wait_ge(sem(f"slot_ready{l}"), TT)
                        for i in range(4):
                            k = 4 * q + i
                            ins = pe.matmul(ps[:, 4 + q, i * P:(i + 1) * P], hotB[:, k], hotA[:, k],
                                            start=True, stop=True)
                        ins.then_inc(sem(f"g_done{l}"), 1)

                pe.wait_ge(sem("d_free"), (D_K, D_N)[l])
                pe.wait_ge(sem(f"xl_ready{l}"), NC)
                scores(0)
                for t in range(TT):
                    if t + 1 < TT:
                        scores(t + 1)
                    if t == 0:
                        for i in range(2):
                            up(l, i, i, True)
                    with pe.Fori(1 if t == 0 else UB // 2 * t, UB // 2 * (t + 1)) as it:
                        for i in range(2):
                            up(l, it * 2 + i, i, False)
                    pe.wait_ge(sem(f"slots{l}"), t + 1)
                    pe.wait_ge(sem(f"sc_copied{l}"), min(t + 2, TT))
                    for a in range(3):
                        ins = pe.transpose(ps[:, 4, a * P:(a + 1) * P], slot[:, a], ident)
                    ins.then_inc(sem(f"turned{l}"), 1)
                for i in range(4):
                    up(l, NA1 + i, i % 2, False)
                    gates(NA1 + i, i == 0)
                with pe.Fori((NA1 + 4) // 2, NA // 2) as it:
                    for i in range(2):
                        n = it * 2 + i
                        up(l, n, i, False)
                        gates(n, False)

            def output(l):
                def down(g, j, first):
                    pe.wait_ge(sem(f"v_split{l}"), 2 * g + 2)
                    pe.wait_ge(sem(f"h_split{l}"), 2 * g + 2)
                    for c in range(NC):
                        if not (first and c < 2):
                            pe.wait_ge(sem(f"o_free{l}"), g * 8 + (c - 1))
                        for i in range(2):
                            for k, (w, x) in enumerate(((vh, hh), (vh, hl), (vl, hh))):
                                for h in range(2):
                                    ins = pe.matmul(ps[:, 4 + 2 * (c % 2) + h, 0:H2],
                                                    w[:, 2 * j + i, c * P:(c + 1) * P],
                                                    x[:, 2 * j + i, h * H2:(h + 1) * H2],
                                                    start=(i == 0 and k == 0), stop=(i == 1 and k == 2))
                        ins.then_inc(sem(f"o_full{l}"), 1)

                def up_group(g):
                    for i in range(2):
                        up(l, 2 * g + i, i, False)

                pe.wait_ge(sem(f"g_copied{l}"), T // 4)
                for j in range(2):
                    down(j, j, j == 0)
                with pe.Fori(1, GA // 2 - 1) as it:
                    for j in range(2):
                        down(it * 2 + j, j, False)
                down(GA - 2, 0, False)
                up_group(GA)
                down(GA - 1, 1, False)
                with pe.Fori(GA // 2, NG // 2 - 1) as it:
                    for j in range(2):
                        up_group(it * 2 + (j + 1))
                        down(it * 2 + j, j, False)
                up_group(NG - 1)
                down(NG - 2, 0, False)
                down(NG - 1, 1, False)

            def attention():
                project(W_K, D_K, 2, xn)
                pe.wait_ge(sem("wv_loaded"), 16)
                for t in range(TT):
                    m = min(P, T - t * P)
                    for c in range(NC):
                        ins = pe.matmul(ps[0:m, 4 + t // 2, (t % 2) * 256:(t % 2 + 1) * 256],
                                        xn[:, c, t * P:t * P + m], wv_sb[:, c], start=(c == 0), stop=(c == NC - 1))
                ins.then_inc(sem("v_done"), 1)
                pe.wait_ge(sem("xn_ready"), 4)
                project(W_Q, D_Q, NC, xn)
                pe.wait_ge(sem("roped"), 2 + NC)
                pe.wait_ge(sem("v_ready"), 1)
                for n in range(NQB):
                    ks = max(0, n - 1) * WIN
                    lo = 0 if n else WIN
                    for kv in range(NKV):
                        u = n * NKV + kv
                        if u:
                            pe.wait_ge(sem("p_ready"), u)
                        for g in range(GRP):
                            ins = pe.matmul(ps[:, g // 2, (g % 2) * 256 + lo:(g % 2 + 1) * 256],
                                            qR[:, kv * GRP + g, n * WIN:(n + 1) * WIN],
                                            kR[:, kv, ks:(n + 1) * WIN], start=True, stop=True)
                        ins.then_inc(sem("p_scores"), 1)
                        pe.wait_ge(sem("p_ready"), u + 1)
                        if u:
                            pe.wait_ge(sem("prT_ready"), u)
                        for kb in range(2):
                            for g in range(GRP):
                                ins = pe.transpose(ps[:, 2 + kb, g * P:(g + 1) * P],
                                                   pr[:, g, kb * WIN:(kb + 1) * WIN], ident)
                        ins.then_inc(sem("pturn"), 1)
                        pe.wait_ge(sem("prT_ready"), u + 1)
                        if u:
                            pe.wait_ge(sem("o_copied"), u)
                        kbs = (0, 1) if n else (1,)
                        for kb in kbs:
                            ins = pe.matmul(ps[0:HD, 7, :], vtok[:, n - 1 + kb, kv * HD:(kv + 1) * HD],
                                            prT[:, 4 * kb:4 * kb + 4].rearrange("p g q -> p (g q)"),
                                            start=(kb == kbs[0]), stop=(kb == 1))
                        ins.then_inc(sem("p_out"), 1)
                pe.wait_ge(sem("qS_ready"), 1)
                pe.wait_ge(sem("kc_loaded"), 16)
                pe.wait_ge(sem("vc_loaded"), 16)
                pe.wait_ge(sem("vnew_loaded"), 16 * NB)
                for b in range(NB):
                    for kv in range(NKV):
                        o = ps[32 * kv:32 * kv + 32, b // 2, (b % 2) * 256:(b % 2) * 256 + WIN + TS]
                        q = qS[:, b, kv * GRP:(kv + 1) * GRP].rearrange("p g s -> p (g s)")
                        pe.matmul(o[:, 0:WIN], q, kc_sb[:, b, kv], start=True, stop=True)
                        ins = pe.matmul(o[:, WIN:], q, kR[:, kv, TP + b * TS:TP + (b + 1) * TS],
                                        start=True, stop=True)
                ins.then_inc(sem("s_scores"), 1)
                pe.wait_ge(sem("s_ready"), 1)
                pe.wait_ge(sem("o_copied"), NQB * NKV)
                for b in range(NB):
                    pe.transpose(ps[:, 4 + b // 4, (b % 4) * P:(b % 4 + 1) * P], pss[:, b, 0:WIN], ident)
                    ins = pe.transpose(ps[0:TS, 6 + b // 4, (b % 4) * P:(b % 4 + 1) * P], pss[:, b, WIN:], ident)
                ins.then_inc(sem("sturn"), 1)
                pe.wait_ge(sem("pssT_ready"), 1)
                for b in range(NB):
                    for kv in range(NKV):
                        o = ps[0:HD, b // 4, (b % 4) * P + 32 * kv:(b % 4) * P + 32 * kv + 32]
                        pe.matmul(o, vc_sb[:, b, kv * HD:(kv + 1) * HD], pssT[:, b, 32 * kv:32 * kv + 32],
                                  start=True, stop=False)
                        ins = pe.matmul(o, vnew[:, b, kv * HD:(kv + 1) * HD], pssN[:, b, 32 * kv:32 * kv + 32],
                                        start=False, stop=True)
                ins.then_inc(sem("s_out"), 1)
                pe.wait_ge(sem("o_copied"), NQB * NKV + 1)
                project(W_O, D_O, NC, xn)

            sum_squares(0)
            pe.wait_ge(sem("xn_ready"), 1)
            project(W_IN, D_IN, 2 * NC, xn)
            rg_gates()
            pe.wait_ge(sem("hg_ready"), NC)
            project(W_OUT, D_OUT, NC, xn)
            for l in range(2):
                if l == 1:
                    sum_squares(2)
                    pe.wait_ge(sem("xn_ready"), 3)
                    attention()
                sum_squares((1, 3)[l])
                pe.wait_ge(sem("xn_ready"), (2, 5)[l])
                project((W_PQ0, W_PQ1)[l], (D_PQ0, D_PQ1)[l], 2 * PH, xn)
                hidden(l)
                output(l)
            sum_squares(4)


def _shape_constants():
    import numpy as np
    c = np.zeros((P, C_N), np.float32)
    c[:, C_ID:C_ID + P] = np.eye(P)
    c[:, C_IOTA:C_IOTA + P] = np.arange(P)
    half = HD // 2
    inv = np.float32(10000.0) ** (-np.arange(half, dtype=np.float32) / np.float32(half))
    pos = np.concatenate([np.arange(TP), np.tile(4096 + np.arange(TS), NB)]).astype(np.float32)
    ang = (inv[:, None] * pos[None, :]).astype(np.float32).astype(np.float64)
    cos, sin = np.cos(ang), np.sin(ang)
    c[:, C_COS:C_COS + T] = np.tile(cos, (4, 1))
    c[:, C_SIN:C_SIN + T] = np.concatenate([-sin, sin, -sin, sin])
    q = np.arange(P)[:, None]
    k = np.arange(WIN)[None, :]
    c[:, C_MP:C_MP + WIN] = np.where(k > q, 0, BIG)
    c[:, C_MP + WIN:C_MP + 2 * WIN] = np.where(k <= q, 0, BIG)
    s = q % TS
    c[:, C_MS:C_MS + WIN] = np.where(k > s, 0, BIG)
    c[:, C_MS + WIN:C_MS + WIN + TS] = np.where(np.arange(TS)[None, :] <= s, 0, BIG)
    return c


def kernel(**inputs):
    import numpy as np
    import concourse.bacc as _bacc
    from concourse import mybir as _mybir
    from concourse.bass_utils import run_bass_kernel_spmd as _run

    a = {k: np.asarray(v) for k, v in inputs.items()}

    def chunks(vec):
        return vec.reshape(-1, P).T

    def tiles(w):
        return w.reshape(NC, P, -1, P).transpose(2, 1, 0, 3)

    xin = np.concatenate([a["x_prompt"].reshape(TP, D), a["x_sample"].reshape(NB * TS, D)])
    xin = xin.T.reshape(NC, P, T).transpose(1, 0, 2)
    gains = np.concatenate([a["rg_norm"].ravel(), a["ffn_norm"][0], a["kv_norm"], a["attn_norm"].ravel(),
                            a["ffn_norm"][1], a["final_norm"]])
    h0 = a["state_h"][0].reshape(NB, NC, P).transpose(2, 1, 0).reshape(P, NC * NB)
    sinks = a["sinks"].ravel()
    subkeys = a["peer_subkeys"].transpose(3, 0, 1, 2).reshape(P, 4 * KEYS)
    params = np.concatenate([
        chunks(gains), chunks(a["rg_conv_w"].ravel()), chunks(a["rg_conv_b"].ravel()),
        chunks(a["rg_ba"].ravel()), chunks(a["rg_bx"].ravel()), chunks(a["rg_lambda"].ravel()), h0,
        np.broadcast_to(sinks, (P, NH)), np.repeat(sinks, TS).reshape(P, 1), subkeys], axis=1)
    w_kv = a["w_kv"]
    wts = np.concatenate([
        tiles(a["rg_w_in"][0]), a["rg_wa"][0].transpose(1, 0, 2)[None], a["rg_wx"][0].transpose(1, 0, 2)[None],
        tiles(a["rg_w_out"][0]), tiles(a["peer_wq"][0]), tiles(w_kv[:, :NKV * HD]), tiles(a["w_q"][0]),
        tiles(a["w_o"][0]), tiles(a["peer_wq"][1])])
    arrays = {
        "xin": xin, "consts": _shape_constants(), "params": params, "wts": wts,
        "wv": w_kv[:, NKV * HD:].reshape(NC, P, NKV * HD).transpose(1, 0, 2),
        "stconv": a["state_conv"][0].reshape(NB, CW - 1, NC, P).transpose(3, 2, 0, 1).reshape(P, NC * NB, CW - 1),
        "kcT": a["cache_k"].transpose(3, 0, 2, 1),
        "kc": a["cache_k"].reshape(NB, WIN, NKV * HD),
        "vc": a["cache_v"].reshape(NB, WIN, NKV * HD).transpose(1, 0, 2),
        "uT": a["peer_u"].reshape(2, KEYS, KEYS, NC, P).transpose(0, 1, 4, 3, 2).reshape(2, KEYS, P, D),
        "v": a["peer_v"].reshape(2, KEYS, KEYS, D),
    }
    arrays = {k: np.ascontiguousarray(x) for k, x in arrays.items()}
    outs = {
        "yT": (P, NC, T), "convP": (P, NC, CW - 1), "hOut": (P, NC, 1 + NB), "kNew": (HD, NKV, WIN + NB * TS),
        "vNewP": (P, NKV * HD), "vNewS": (NB * TS, NKV * HD), "kKeep": (NB, WIN - TS, NKV * HD),
        "vKeep": (NB, WIN - TS, NKV * HD), "convS": (P, NC * NB, CW - 1),
    }
    nc = _bacc.Bacc("TRN2", target_bir_lowering=False, num_devices=1)
    f32 = _mybir.dt.float32
    args = [nc.dram_tensor(k, x.shape, _mybir.dt.from_np(x.dtype), kind="ExternalInput").ap()
            for k, x in arrays.items()]
    args += [nc.dram_tensor(k, s, f32, kind="ExternalOutput").ap() for k, s in outs.items()]
    args.append(nc.dram_tensor("gate_dram", (2, NGB, P, KEYS * GB), f32, kind="Internal").ap())
    args.append(nc.dram_tensor("s_dram", (2, NA, P, T), f32, kind="Internal").ap())
    decoder(nc, *args)
    r = _run(nc, [arrays], core_ids=[0]).results[0]

    y = r["yT"].transpose(2, 1, 0).reshape(T, D)
    convP = r["convP"].transpose(2, 1, 0).reshape(1, 1, CW - 1, D)
    convS = r["convS"].reshape(P, NC, NB, CW - 1).transpose(2, 3, 1, 0).reshape(1, NB, CW - 1, D)
    h = r["hOut"].transpose(2, 1, 0).reshape(1 + NB, D)
    kn = r["kNew"].transpose(2, 1, 0)
    ks = np.concatenate([r["kKeep"].reshape(NB, WIN - TS, NKV, HD), kn[WIN:].reshape(NB, TS, NKV, HD)], axis=1)
    vs = np.concatenate([r["vKeep"].reshape(NB, WIN - TS, NKV, HD), r["vNewS"].reshape(NB, TS, NKV, HD)], axis=1)
    return (y[:TP].reshape(1, TP, D), y[TP:].reshape(NB, TS, D), convP, h[:1].reshape(1, 1, D),
            kn[:WIN].reshape(1, WIN, NKV, HD), r["vNewP"].reshape(1, WIN, NKV, HD), convS,
            h[1:].reshape(1, NB, D), ks, vs)
```

```python
from contextlib import ExitStack

import concourse.bass as bass
from concourse import mybir

F32 = mybir.dt.float32
F32R = mybir.dt.float32r
U32 = mybir.dt.uint32
ALU = mybir.AluOpType
ACT = mybir.ActivationFunctionType
X = mybir.AxisListType.X

P = 128
D = 1024
NC = D // P
TP, NB, TS = 512, 8, 8
T = TP + NB * TS
H2 = T // 2
TT = -(-T // P)
CW = 4
NH, NKV, HD = 16, 4, 64
GRP = NH // NKV
WIN = 128
NQB = TP // WIN
PH, TOPK = 8, 16
NS = PH * TOPK
KEYS = 128
GB = 64
NGB = TP // GB
UB = (8, 10, 8, 10, 8)
NA1 = sum(UB)
NA2 = TP // 16
NA3 = 4
NA = NA1 + NA2 + NA3
GA = NA // 2
NU = TT - 1
SMP = NB * TS
ROWS = 8
PICK = 8
GATHERS = NS // 2
NG = KEYS // 2
EPS = 1e-6
BIG = -3.0e38

C_ID, C_IOTA, C_COS = 0, P, 2 * P
C_SIN = C_COS + T
C_MP = C_SIN + T
C_MS = C_MP + 2 * WIN
C_FOLD = C_MS + WIN + TS
C_N = C_FOLD + NB * TS
(N_RG, N_F0, N_KV, N_AT, N_F1, N_FIN) = (NC * i for i in range(6))
P_CW = 6 * NC
P_CB = P_CW + CW * NC
P_BA = P_CB + NC
P_BX = P_BA + NC
P_LAM = P_BX + NC
P_H0 = P_LAM + NC
P_SINK = P_H0 + NC * NB
P_SKS = P_SINK + NH
P_SK = P_SKS + 1
P_N = P_SK + 4 * KEYS

W_IN, W_A, W_X, W_OUT, W_PQ0, W_K, W_Q, W_O, W_PQ1, W_N = 0, 16, 17, 18, 26, 42, 44, 52, 60, 76
D_IN, D_A, D_X, D_OUT, D_PQ0, D_K, D_Q, D_O, D_PQ1, D_N = 0, 16, 24, 32, 40, 56, 58, 66, 74, 90


def tiles_made(w):
    if w < W_A:
        return w + 1
    if w in (W_A, W_X):
        return D_A + NC * (w - W_A + 1)
    return w + 1 + 2 * (NC - 1)


def splits_made(w):
    return w + 1 if w < W_A else w - 1


(X_IN, X_OUT, X_F0, X_KV, X_AT, X_O, X_F1) = range(7)


class Chain:

    def __init__(self, eng, sem):
        self.eng, self.sem, self.n = eng, sem, 0

    def did(self, ins):
        ins.then_inc(self.sem, 1)
        self.n += 1

    def settle(self):
        self.eng.wait_ge(self.sem, self.n)


def decoder(nc, xin, consts, params, wts, wv, stconv, kcT, kc, vc, uT, u, v,
            yT, convP, hOut, kNew, vNewP, vNewS, kKeep, vKeep, convS, gate_dram, s_dram):
    with ExitStack() as ctx:
        def sb(name, shape, dt=F32, st=ctx):
            return st.enter_context(nc.sbuf_tensor(name, shape, dt))

        sems = {}

        def sem(name):
            if name not in sems:
                sems[name] = ctx.enter_context(nc.semaphore(name))
            return sems[name]

        ps = ctx.enter_context(nc.psum_tensor("ps", [P, 8, 512], F32))

        xT = sb("xT", [P, NC, T])
        cst = sb("cst", [P, C_N])
        prm = sb("prm", [P, P_N])
        uraw = sb("uraw", [P, 2, NC, P])
        uh = sb("uh", [P, 2, NC, P], F32R)
        ul = sb("ul", [P, 2, NC, P], F32R)
        rinv = sb("rinv", [P, T])
        ones = sb("ones", [P, P])
        mark = sb("mark", [P, 1])
        with ExitStack() as st:
            accS = sb("accS", [P, D], st=st)
        slotT = sb("slotT", [P, 3, TP])
        ident = cst[:, C_ID:C_ID + P]
        iota = cst[:, C_IOTA:C_IOTA + P]

        with ExitStack() as st:
            sc = sb("sc", [P, 2 * PH, KEYS], st=st)
            sc2 = sb("sc2", [P, 2 * PH, KEYS], st=st)
        with ExitStack() as st:
            hotA = sb("hotA", [P, 16, KEYS], st=st)
            hotB = sb("hotB", [P, 16, KEYS], st=st)
        with ExitStack() as st:
            hh = sb("hh", [P, 4, TP], F32R, st=st)
            hl = sb("hl", [P, 4, TP], F32R, st=st)
        xn = sb("xn", [P, NC, T])

        with ExitStack() as st:
            ig = sb("ig", [P, NC, T], st=st)
            dec = sb("dec", [P, NC, T], st=st)
        with ExitStack() as st:
            vnew = sb("vnew", [TS, NB, NKV * HD], st=st)
            kc_sb = sb("kc_sb", [HD, NB, NKV, WIN], st=st)
            vc_sb = sb("vc_sb", [P, NB, NKV * HD], st=st)
        xh = sb("xh", [P, NC, T], F32R)
        xl = sb("xl", [P, NC, T], F32R)

        with ExitStack() as st:
            gate = sb("gate", [P, NC, T], st=st)
            xpre = sb("xpre", [P, NC, TP + CW - 1], st=st)
            xpreS = sb("xpreS", [P, NC, NB, TS + CW - 1], st=st)
            xc = sb("xc", [P, NC, T], st=st)
            rg = sb("rg", [P, NC, T], st=st)
            sp = sb("sp", [P, 4, NC], st=st)
            ah0 = sb("ah0", [P, NC, NB], st=st)
            hlast = sb("hlast", [P, NC, 1 + NB], st=st)
        with ExitStack() as peer:
            hg0 = sb("hg0", [P, 2, TP], st=peer)
            xs = sb("xs", [P, D], st=peer)
            pick = sb("pick", [P, GATHERS], U32, st=peer)
            pgate = sb("pgate", [P, GATHERS], st=peer)
            phid = sb("phid", [P, GATHERS], st=peer)
            with ExitStack() as st:
                qT = sb("qT", [P, 2 * PH, T], st=st)
                sv = sb("sv", [P, 2 * PH, TOPK], st=st)
                si = sb("si", [P, 2 * PH, TOPK], U32, st=st)
                sif = sb("sif", [P, 2 * PH, TOPK], st=st)
                cand = sb("cand", [P, PH, TOPK * TOPK], st=st)
                cand2 = sb("cand2", [P, PH, TOPK * TOPK], st=st)
                cv = sb("cv", [P, PH, TOPK], st=st)
                ci = sb("ci", [P, PH, TOPK], U32, st=st)
                cab = sb("cab", [P, 2, PH, TOPK], U32, st=st)
                cabf = sb("cabf", [P, 2, PH, TOPK], st=st)
                ex = sb("ex", [P, PH, TOPK], st=st)
                exs = sb("exs", [P, 2, PH], st=st)
                slot = sb("slot", [P, 3, NS], st=st)
            with ExitStack() as st:
                gblk = sb("gblk", [P, 2, KEYS, GB], st=st)
            with ExitStack() as st:
                vraw = sb("vraw", [P, 2, D], st=st)
                vh = sb("vh", [P, 4, D], F32R, st=st)
                gt = sb("gt", [P, 2, NGB, 2, GB], st=st)
                rows = sb("rows", [P, ROWS, D], st=st)
                vl = sb("vl", [P, 4, D], F32R, st=st)
                hg1 = sb("hg1", [P, 2, TP], st=st)
            hg = (hg1, hg0)
        with ExitStack() as st:
            qR = sb("qR", [HD, NH, T], st=st)
            kR = sb("kR", [HD, NKV, T], st=st)
            qS = sb("qS", [HD, NB, NH, TS], st=st)
            vtok = sb("vtok", [P, TT, NKV * HD], st=st)
            with ExitStack() as st2:
                rot = sb("rot", [P, 2, T], st=st2)
                rc = sb("rc", [P, 2, T], st=st2)
            pss = sb("pss", [P, NB, WIN + TS], st=st)
            pssT = sb("pssT", [P, NB, P], st=st)
            with ExitStack() as st2:
                past_rope = sb("past_rope", [P, 4 * T - 2 * NB * P - NB * TS], st=st2)
                wv_sb = sb("wv_sb", [P, NC, NKV * HD], st=st2)
            pssN = sb("pssN", [TS, NB, P], st=st)
            prT = sb("prT", [P, 2, 2 * GRP, P], st=st)
            pr = sb("pr", [P, 2, GRP, 2 * WIN], st=st)
            sm = sb("sm", [P, 2, 6, NB], st=st)

        def halves(lo):
            return ps[:, lo:lo + 2, 0:H2]

        def two(ap):
            return ap.rearrange("p (h t) -> p h t", h=2)

        def sbank(u):
            return ps[:, 4 * (u % 2):4 * (u % 2) + 2, :]

        def dbank(d):
            return 2 * (d % 2)

        v_tiles = v.rearrange("(l a b) d -> l a b d", l=2, b=KEYS)

        def wait_gates(eng, l, i):
            eng.wait_ge(sem(f"g_stored{l}_{i}"), 16 * ((NGB + 1 - i) // 2))

        def wait_hidden(eng, l):
            for i in range(2):
                eng.wait_ge(sem(f"s_stored{l}_{i}"), 16 * (NA // 2))

        GU = GA + GATHERS // PICK
        GV = GU + GATHERS // PICK

        block = ctx.enter_context(nc.Block())

        @block.sync
        def _(spq):
            for h in range(2):
                spq.dma_start(xT[:, 4 * h:4 * h + 4], xin[:, 4 * h:4 * h + 4]).then_inc(sem(f"x_loaded{h}"), 16)
            spq.dma_start(prm[:, :], params).then_inc(sem("params_loaded"), 16)

            def load_weights(lo, hi):
                for w in range(lo, hi):
                    if w - 2 in (W_A, W_X):
                        spq.wait_ge(sem("tile_done"), tiles_made(w - 2))
                    elif w >= 2:
                        spq.wait_ge(sem("w_split"), splits_made(w - 2))
                    spq.dma_start(uraw[:, w % 2], wts[w]).then_inc(sem(f"w_loaded{w % 2}"), 16)

            def hidden(l):
                def step(n, i, full=None):
                    spq.wait_ge(sem(f"u_split{l}"), n + 1)
                    spq.dma_start(uraw[:, i], tile_of(uT[l], n + 2)).then_inc(sem(f"u_loaded{l}_{i}"), 16)
                    if full is not None:
                        spq.wait_ge(sem(f"g_copied{l}"), GB // 4 * (full + 1))
                        spq.dma_start(gate_dram[l, full], gblk[:, full % 2]
                                      ).then_inc(sem(f"g_stored{l}_{full % 2}"), 16)
                    spq.wait_ge(sem(f"s_free{l}"), n + 1)
                    spq.dma_start(tile_of(s_dram[l], n), hg0[:, i]).then_inc(sem(f"s_stored{l}_{i}"), 16)

                for i in range(2):
                    spq.wait_ge(sem("w_split"), splits_made((W_K, W_N)[l] + i - 2))
                    spq.dma_start(uraw[:, i], uT[l, i]).then_inc(sem(f"u_loaded{l}_{i}"), 16)
                with spq.Fori(0, NA1 // 2) as it:
                    for i in range(2):
                        step(it * 2 + i, i)
                for b in range(NGB):
                    step(NA1 + 4 * b, 0, b - 1 if b else None)
                    for i in range(1, 4):
                        step(NA1 + 4 * b + i, i % 2)
                step(NA - 4, 0, NGB - 1)
                step(NA - 3, 1)
                wait_gates(spq, l, 0)
                for i in range(2):
                    spq.dma_start(vraw[:, i], v_tiles[l, i]).then_inc(sem(f"v_loaded{l}_{i}"), 16)
                step(NA - 2, 0)
                wait_gates(spq, l, 1)
                load_h(l, 0, 0)
                load_gates(l, 0, 0)
                step(NA - 1, 1)
                wait_hidden(spq, l)

            def load_h(l, g, j):
                for i in range(2):
                    spq.dma_start(hg[j][:, i], tile_of(s_dram[l], 2 * g + i)
                                  ).then_inc(sem(f"h_loaded{l}_{j}{i}"), 16)

            def load_gates(l, g, j):
                spq.dma_start(gt[:, j].rearrange("p b a t -> p b (a t)"),
                              gates_of(l, g)).then_inc(sem(f"gt_loaded{l}_{j}"), 16)

            def output(l):
                def gates_and_v(g, j, fresh):
                    if not fresh:
                        spq.wait_ge(sem(f"h_mul{l}"), 2 * g - 2)
                    load_gates(l, g, j)
                    for i in range(2):
                        spq.wait_ge(sem(f"v_split{l}"), 2 * g + (i - 1))
                        spq.dma_start(vraw[:, i], tile_of(v_tiles[l], 2 * g + i)).then_inc(sem(f"v_loaded{l}_{i}"), 16)

                def stored_group(g, j, fresh):
                    for i in range(2):
                        if not fresh:
                            spq.wait_ge(sem(f"h_split{l}"), 2 * g + (i - 3))
                        spq.dma_start(hg[j][:, i], tile_of(s_dram[l], 2 * g + i)
                                      ).then_inc(sem(f"h_loaded{l}_{j}{i}"), 16)
                    gates_and_v(g, j, fresh)

                def new_group(g, j, last):
                    if not last:
                        for i in range(2):
                            spq.wait_ge(sem(f"u_split{l}"), 2 * g + (i + 1))
                            spq.dma_start(uraw[:, i], tile_of(uT[l], 2 * g + (i + 2))
                                          ).then_inc(sem(f"u_loaded{l}_{i}"), 16)
                    gates_and_v(g, j, False)

                stored_group(1, 1, True)
                with spq.Fori(1, GA // 2) as it:
                    for j in range(2):
                        stored_group(it * 2 + j, j, False)
                with spq.Fori(GA // 2, NG // 2 - 1) as it:
                    for j in range(2):
                        new_group(it * 2 + j, j, False)
                for j in range(2):
                    new_group(NG - 2 + j, j, j == 1)

            def tile_of(ap, n):
                if isinstance(n, int):
                    return ap[n]
                return ap[bass.ds(n, 1)].rearrange("o p n -> (o p) n")

            def gates_of(l, g):
                src = gate_dram[l].rearrange("b p (g n) -> p b g n", n=2 * GB)
                if isinstance(g, int):
                    return src[:, :, g]
                return src[:, :, bass.ds(g, 1)].rearrange("p b o n -> p b (o n)")

            load_weights(0, 3)
            spq.dma_start(cst[:, :], consts).then_inc(sem("consts_loaded"), 16)
            load_weights(3, W_PQ0)
            spq.wait_ge(sem("pre_copied"), NC)
            spq.wait_ge(sem("d_free"), D_A)
            spq.dma_start(convP, xpre[:, :, TP:TP + CW - 1]).then_inc(sem("states_out"), 16)
            spq.dma_start(convS, xpreS[:, :, :, TS:TS + CW - 1].rearrange("p c b k -> p (c b) k")
                          ).then_inc(sem("states_out"), 16)
            spq.wait_ge(sem("hlast_ready"), 1)
            spq.dma_start(hOut, hlast[:, :, :]).then_inc(sem("states_out"), 16)
            load_weights(W_PQ0, W_K)
            hidden(0)
            output(0)
            spq.wait_ge(sem("x_ready"), 2)
            spq.dma_start(wv_sb[:, :, :], wv).then_inc(sem("wv_loaded"), 16)
            load_weights(W_K, W_Q + 2)
            spq.wait_ge(sem("v_ready"), 1)
            spq.dma_start(vNewP, vtok[:, NQB - 1]).then_inc(sem("out_done"), 16)
            spq.dma_start(vNewS, vtok[0:NB * TS, NQB]).then_inc(sem("out_done"), 16)
            spq.wait_ge(sem("k_ready"), 2)
            spq.dma_start(kNew, kR[:, :, TP - WIN:T]).then_inc(sem("out_done"), 16)
            load_weights(W_Q + 2, W_O + 2)
            spq.wait_ge(sem("tile_done"), D_O)
            for b in range(NB):
                spq.dma_start(vnew[:, b], vtok[b * TS:(b + 1) * TS, NQB]).then_inc(sem("vnew_loaded"), 16)
            spq.dma_start(kc_sb[:, :, :, :], kcT).then_inc(sem("kc_loaded"), 16)
            spq.dma_start(vc_sb[:, :, :], vc).then_inc(sem("vc_loaded"), 16)
            load_weights(W_O + 2, W_N)
            hidden(1)
            output(1)
            spq.wait_ge(sem("y_ready"), NC)
            spq.dma_start(yT, xn[:, :, :]).then_inc(sem("out_done"), 16)
            spq.wait_ge(sem("states_out"), 48)
            spq.wait_ge(sem("out_done"), 16 * 4)

        @block.gpsimd
        def _(pool):
            pool.memset(ones[:, :], 1.0).then_inc(sem("ones_ready"), 1)
            pool.memset(xpre[:, :, 0:CW - 1], 0.0).then_inc(sem("pad_ready"), 1)
            pool.dma_start(xpreS[:, :, :, 0:CW - 1].rearrange("p c b k -> p (c b) k"), stconv
                           ).then_inc(sem("st_loaded"), 16)
            def split_weights(lo, hi):
                for w in range(lo, hi):
                    if w in (W_A, W_X):
                        continue
                    if w == W_OUT:
                        pool.dma_start(kKeep, kc[:, TS:WIN]).then_inc(sem("kept"), 16)
                        pool.dma_start(vKeep, vc.rearrange("p b n -> b p n")[:, TS:WIN]).then_inc(sem("kept"), 16)
                    if w == W_OUT + 2:
                        for f in range(NC):
                            pool.wait_ge(sem("scanned"), f + 1)
                            pool.tensor_tensor(xn[:, f], rg[:, f], gate[:, f], ALU.mult
                                               ).then_inc(sem("x_whole"), 1)
                    n = splits_made(w) - 1
                    pool.wait_ge(sem(f"w_loaded{w % 2}"), 16 * (w // 2 + 1))
                    if W_PQ0 <= w < W_K or w >= W_PQ1:
                        pool.wait_ge(sem("qh_ready"), w + 1 - (W_PQ0 if w < W_K else W_PQ1 - 2 * PH))
                        pool.tensor_tensor(ul[:, w % 2], uraw[:, w % 2], uh[:, w % 2].bitcast(F32), ALU.subtract
                                           ).then_inc(sem("w_split"), 1)
                        continue
                    if n >= 2:
                        pool.wait_ge(sem("tile_done"), tiles_made(w - 2 if w - 2 not in (W_A, W_X) else w - 4))
                    pool.tensor_copy(uh[:, w % 2], uraw[:, w % 2]).then_inc(sem("wh_ready"), 1)
                    pool.wait_ge(sem("wh_ready"), n + 1 - (2 * PH if w >= W_K else 0))
                    pool.tensor_tensor(ul[:, w % 2], uraw[:, w % 2], uh[:, w % 2].bitcast(F32), ALU.subtract
                                       ).then_inc(sem("w_split"), 1)

            for l, (lo, hi) in enumerate(((0, W_K), (W_K, W_N))):
                split_weights(lo, hi)

                def low_u(n, i):
                    pool.wait_ge(sem(f"uh_ready{l}"), n + 1)
                    pool.tensor_tensor(ul[:, i], uraw[:, i], uh[:, i].bitcast(F32), ALU.subtract
                                       ).then_inc(sem(f"u_split{l}"), 1)

                def low_v(g, j):
                    for i in range(2):
                        pool.wait_ge(sem(f"vh_ready{l}"), g * 2 + (i + 1))
                        pool.tensor_tensor(vl[:, 2 * j + i], vraw[:, i], vh[:, 2 * j + i].bitcast(F32),
                                           ALU.subtract).then_inc(sem(f"v_split{l}"), 1)

                with pool.Fori(0, NA // 2) as it:
                    for i in range(2):
                        low_u(it * 2 + i, i)
                low_v(0, 0)
                for i in range(2):
                    low_u(NA + i, i)
                low_v(1, 1)
                with pool.Fori(1, GA // 2) as it:
                    for j in range(2):
                        low_v(it * 2 + j, j)

                def gather_rows(g):
                    for k in range((g - GA) * PICK, min((g - GA + 1) * PICK, 2 * GATHERS)):
                        if k == 0:
                            pool.wait_ge(sem(f"picked{l}"), 2)
                        if k >= ROWS:
                            pool.wait_ge(sem(f"row_used{l}"), k - ROWS + 1)
                        pool.indirect_dma_start(
                            out=rows[:, k % ROWS], out_offset=None, in_=u if k < GATHERS else v,
                            in_offset=bass.IndirectOffsetOnAxis(ap=pick[:, k % GATHERS:k % GATHERS + 1], axis=0)
                        ).then_inc(sem(f"row_loaded{k % ROWS}"), 16)

                gather_rows(GA)
                for g in range(GA, NG):
                    if g + 1 < NG:
                        for i in range(2):
                            low_u(2 * g + 2 + i, i)
                    low_v(g, g % 2)
                    gather_rows(g + 1)
            pool.wait_ge(sem("kept"), 32)

        @block.scalar
        def _(act):
            chain = Chain(act, sem("act_chain"))

            def square(s):
                if s:
                    act.wait_ge(sem("x_ready"), s)
                    act.wait_ge(sem("tile_done"), (0, D_PQ0, D_K, D_PQ1, D_N)[s])
                for c in range(NC):
                    if not s and c % 4 == 0:
                        act.wait_ge(sem(f"x_loaded{c // 4}"), 16)
                    act.activation(xn[:, c], xT[:, c], ACT.Square).then_inc(sem("sq_ready"), 1)
                act.wait_ge(sem("ms_ready"), s + 1)
                act.activation(rinv[:, :], rinv[:, :], ACT.Sqrt).then_inc(sem("rms_ready"), 1)

            def split_x(k):
                for c in range(NC):
                    act.wait_ge(sem("x_whole"), k * NC + c + 1)
                    act.activation(xh[:, c], xn[:, c], ACT.Copy).then_inc(sem("xh_ready"), 1)

            def rg_lru():
                square(0)
                act.activation(sp[:, 0], prm[:, P_LAM:P_LAM + NC], ACT.Exp, scale=-1.0
                               ).then_inc(sem("softplus_step"), 1)
                split_x(X_IN)
                act.wait_ge(sem("softplus_step"), 2)
                act.activation(sp[:, 2], sp[:, 1], ACT.Ln).then_inc(sem("softplus_step"), 1)
                for f in range(NC):
                    act.wait_ge(sem("tile_done"), D_IN + f + 1)
                    act.activation(two(gate[:, f]), halves(dbank(f)), ACT.Gelu_apprx_tanh
                                   ).then_inc(sem("d_free"), 1)
                act.wait_ge(sem("pad_ready"), 1)
                act.wait_ge(sem("st_loaded"), 16)
                for f in range(NC):
                    d = D_IN + NC + f
                    b = dbank(d)
                    act.wait_ge(sem("tile_done"), d + 1)
                    act.activation(xpre[:, f, CW - 1:CW - 1 + H2], ps[:, b, 0:H2], ACT.Copy)
                    act.activation(xpre[:, f, CW - 1 + H2:CW - 1 + TP], ps[:, b + 1, 0:TP - H2], ACT.Copy
                                   ).then_inc(sem("pre_copied"), 1)
                    act.activation(xpreS[:, f, :, CW - 1:],
                                   ps[:, b + 1, TP - H2:H2].rearrange("p (b s) -> p b s", b=NB),
                                   ACT.Copy).then_inc(sem("d_free"), 1)
                for k, (d0, dst, bias) in enumerate(((D_A, rg, P_BA), (D_X, ig, P_BX))):
                    for f in range(NC):
                        act.wait_ge(sem("tile_done"), d0 + f + 1)
                        act.activation(two(dst[:, f]), halves(dbank(d0 + f)), ACT.Sigmoid,
                                       bias=prm[:, bias + f:bias + f + 1]).then_inc(sem("d_free"), 1)
                act.wait_ge(sem("d_free"), D_OUT)
                act.wait_ge(sem("softplus_step"), 4)
                for f in range(NC):
                    act.activation(dec[:, f], rg[:, f], ACT.Exp, scale=sp[:, 3, f:f + 1]
                                   ).then_inc(sem("dec_ready"), 1)
                act.wait_ge(sem("dec_ready"), NC)
                for f in range(NC):
                    act.activation(rg[:, f], rg[:, f], ACT.Tanh, scale=sp[:, 3, f:f + 1]
                                   ).then_inc(sem("tanh_ready"), 1)
                for f in range(NC):
                    act.wait_ge(sem("m2_ready"), f + 1)
                    act.activation(rg[:, f], rg[:, f], ACT.Sqrt, scale=-1.0).then_inc(sem("mult_ready"), 1)
                split_x(X_OUT)

            def copy_queries(d0):
                for f in range(2 * PH):
                    act.wait_ge(sem("tile_done"), d0 + f + 1)
                    act.activation(two(qT[:, f]), halves(dbank(d0 + f)), ACT.Copy
                                   ).then_inc(sem("d_free"), 1)

            def hidden(l):
                def split_u(n, i, fresh):
                    act.wait_ge(sem(f"u_loaded{l}_{i}"), (n - i) * 8 + 16)
                    if not fresh:
                        act.wait_ge(sem(f"s_full{l}"), n - 1)
                    else:
                        act.wait_ge(sem("tile_done"), (D_K, D_N)[l])
                    act.activation(uh[:, i], uraw[:, i], ACT.Copy).then_inc(sem(f"uh_ready{l}"), 1)

                def step(n, i, fresh):
                    split_u(n + 1, 1 - i, fresh and i == 0)
                    act.wait_ge(sem(f"s_full{l}"), n + 1)
                    if not fresh:
                        act.wait_ge(sem(f"s_stored{l}_{i}"), (n - i) * 8)
                    act.activation(hg0[:, i], ps[:, i, :], ACT.Gelu).then_inc(sem(f"s_free{l}"), 1)

                def copy_scores(t):
                    act.wait_ge(sem(f"sc_done{l}"), t + 1)
                    if t:
                        act.wait_ge(sem(f"sc_read{l}"), t)
                    act.activation(sc[:, :, :].rearrange("p (b j) k -> p b (j k)", b=4), ps[:, 4:8, :],
                                   ACT.Copy).then_inc(sem(f"sc_copied{l}"), 1)

                def copy_slots(t):
                    act.wait_ge(sem(f"turned{l}"), t)
                    act.activation(slotT[:, :, (t - 1) * P:t * P],
                                   ps[:, 2 + t % 2, 0:3 * P].rearrange("p (a t) -> p a t", a=3),
                                   ACT.Copy).then_inc(sem(f"slot_ready{l}"), 1)

                def copy_gates(n, b, k):
                    for q in range(4):
                        act.wait_ge(sem(f"g_done{l}"), (n - NA1) * 4 + (q + 1))
                        act.activation(gblk[:, b % 2, :, bass.ds(k + 4 * q, 4)],
                                       ps[:, 4 + q, :].rearrange("p (t k) -> p k t", t=4),
                                       ACT.Copy).then_inc(sem(f"g_copied{l}"), 1)

                act.wait_ge(sem(f"xs_done{l}"), 1)
                act.activation(xs.rearrange("p (b n) -> p b n", b=2), ps[:, 2:4, :], ACT.Copy
                               ).then_inc(sem(f"xs_ready{l}"), 1)
                copy_scores(0)
                split_u(0, 0, True)
                n0 = 0
                for t in range(TT):
                    n1 = n0 + UB[t]
                    if t == 0:
                        for i in range(2):
                            step(i, i, True)
                    with act.Fori(1 if t == 0 else n0 // 2, n1 // 2 - 1) as it:
                        for i in range(2):
                            step(it * 2 + i, i, False)
                    if t > 1:
                        copy_slots(t - 1)
                    if t + 1 < TT:
                        copy_scores(t + 1)
                    for i in range(2):
                        step(n1 - 2 + i, i, False)
                    n0 = n1
                    act.wait_ge(sem(f"ex_in{l}"), t + 1)
                    act.activation(ex[:, :, :], ex[:, :, :], ACT.Exp).then_inc(sem(f"ex_out{l}"), 1)
                copy_slots(TT - 1)
                for b in range(NGB):
                    if b >= 2:
                        act.wait_ge(sem(f"g_stored{l}_{b % 2}"), 16 * (b // 2))
                    with act.Fori(0, 2) as it:
                        for i in range(2):
                            n = it * 2 + (NA1 + 4 * b + i)
                            step(n, i, False)
                            copy_gates(n, b, it * 32 + 16 * i)
                with act.Fori((NA1 + NA2) // 2, NA // 2 - 1) as it:
                    for i in range(2):
                        step(it * 2 + i, i, False)
                step(NA - 2, 0, False)
                wait_gates(act, l, 0)
                split_v_h(l, 0, 0, True)
                step(NA - 1, 1, False)
                split_u(NA + 1, 1, False)
                wait_hidden(act, l)
                split_v_h(l, 1, 1, True)

            def split_v_h(l, g, j, fresh):
                for i in range(2):
                    act.wait_ge(sem(f"v_loaded{l}_{i}"), g * 16 + 16)
                    if not fresh:
                        act.wait_ge(sem(f"o_full{l}"), g * 8 - 8)
                    act.activation(vh[:, 2 * j + i], vraw[:, i], ACT.Copy).then_inc(sem(f"vh_ready{l}"), 1)
                for i in range(2):
                    act.wait_ge(sem(f"h_mul{l}"), 2 * g + (i + 1))
                    act.activation(hh[:, 2 * j + i], hg[j][:, i], ACT.Copy).then_inc(sem(f"hh_ready{l}"), 1)

            def output(l):
                def new_group(g, j, last):
                    if not last:
                        for i in range(2):
                            act.wait_ge(sem(f"u_loaded{l}_{i}"), g * 16 + 32)
                            act.wait_ge(sem(f"s_full{l}"), 2 * g + (i + 1))
                            act.activation(uh[:, i], uraw[:, i], ACT.Copy).then_inc(sem(f"uh_ready{l}"), 1)
                    for i in range(2):
                        act.wait_ge(sem(f"s_full{l}"), 2 * g + (i + 1))
                        act.wait_ge(sem(f"h_split{l}"), 2 * g + (i - 3))
                        act.activation(hg[j][:, i], ps[:, i, :], ACT.Gelu).then_inc(sem(f"s_free{l}"), 1)
                    split_v_h(l, g, j, False)

                with act.Fori(1, GA // 2) as it:
                    for j in range(2):
                        split_v_h(l, it * 2 + j, j, False)
                with act.Fori(GA // 2, GU // 2) as it:
                    for j in range(2):
                        new_group(it * 2 + j, j, False)
                act.wait_ge(sem(f"row_used{l}"), GATHERS)
                act.activation(phid[:, :], phid[:, :], ACT.Gelu).then_inc(sem(f"phid_ready{l}"), 1)
                with act.Fori(GU // 2, NG // 2 - 1) as it:
                    for j in range(2):
                        new_group(it * 2 + j, j, False)
                for j in range(2):
                    new_group(NG - 2 + j, j, j == 1)

            def rope_shift(first_tile, n):
                for f in range(n):
                    d = first_tile + f
                    act.wait_ge(sem("tile_done"), d + 1)
                    if d - D_K >= 2:
                        act.wait_ge(sem("roped"), d - D_K - 1)
                    for q in range(4):
                        src = 32 * (q ^ 1)
                        ins = act.activation(two(rot[32 * q:32 * q + 32, d % 2]),
                                             ps[src:src + 32, dbank(d):dbank(d) + 2, 0:H2], ACT.Copy)
                    ins.then_inc(sem("rot_ready"), 1)

            def attention():
                split_x(X_KV)
                rope_shift(D_K, 2)
                act.wait_ge(sem("v_done"), 1)
                act.activation(vtok[:, 0:4].rearrange("p (b t) n -> p b (t n)", b=2), ps[:, 4:6, :], ACT.Copy)
                act.activation(vtok[0:NB * TS, 4], ps[0:NB * TS, 6, 0:NKV * HD], ACT.Copy
                               ).then_inc(sem("v_ready"), 1)
                act.wait_ge(sem("tile_done"), D_Q)
                split_x(X_AT)
                rope_shift(D_Q, NC)

                def exps(u):
                    p, m = pr[:, u % 2], sm[:, u % 2]
                    act.wait_ge(sem("pmax"), u + 1)
                    for g in range(GRP):
                        act.activation(p[:, g], p[:, g], ACT.Exp, bias=m[:, 1, g:g + 1],
                                       accum_out=m[:, 2, g:g + 1])
                    act.activation(m[:, 3, 0:GRP], m[:, 3, 0:GRP], ACT.Exp).then_inc(sem("pexp"), 1)

                exps(0)
                exps(1)
                for u in range(NQB * NKV):
                    act.wait_ge(sem("pturn"), u + 1)
                    if u >= 2:
                        act.wait_ge(sem("p_out"), u - 1)
                    act.activation(prT[:, u % 2].rearrange("p (b j) k -> p b (j k)", b=2), ps[:, 2:4, :],
                                   ACT.Copy).then_inc(sem("prT_ready"), 1)
                    if u + 2 < NQB * NKV:
                        exps(u + 2)
                act.wait_ge(sem("smax"), 1)
                act.activation(pss[:, :, :], pss[:, :, :], ACT.Exp).then_inc(sem("sexp"), 1)
                act.activation(sm[:, 0, 3], sm[:, 0, 3], ACT.Exp).then_inc(sem("sexp"), 1)
                act.wait_ge(sem("sturn"), 1)
                act.activation(pssT[:, :, :].rearrange("p (b j) k -> p b (j k)", b=2), ps[:, 4:6, :], ACT.Copy)
                act.activation(pssN[:, :, :].rearrange("p (b j) k -> p b (j k)", b=2), ps[0:TS, 6:8, :],
                               ACT.Copy).then_inc(sem("pssT_ready"), 1)
                act.wait_ge(sem("s_out"), 1)
                split_x(X_O)

            rg_lru()
            for l, d0 in ((0, D_PQ0), (1, D_PQ1)):
                if l == 1:
                    square(2)
                    attention()
                square((1, 3)[l])
                split_x((X_F0, X_F1)[l])
                copy_queries(d0)
                hidden(l)
                output(l)
            square(4)

        @block.vector
        def _(dve):
            chain = Chain(dve, sem("dve_chain"))

            def norm_stats(s):
                for c in range(2, NC):
                    dve.wait_ge(sem("sq_ready"), NC * s + c + 1)
                    if c > 3:
                        dve.wait_ge(sem("sq_added"), (NC - 2) * s + c - 3)
                    dve.tensor_tensor(xn[:, c % 2], xn[:, c % 2], xn[:, c], ALU.add
                                      ).then_inc(sem("sq_added"), 1)
                dve.wait_ge(sem("sum_done"), s + 1)
                dve.tensor_scalar(two(rinv[:, :]), halves(4), 1.0 / D, EPS, ALU.mult, ALU.add
                                  ).then_inc(sem("ms_ready"), 1)
                dve.wait_ge(sem("rms_ready"), s + 1)
                chain.did(dve.reciprocal(rinv[:, :], rinv[:, :]))
                chain.settle()

            def low_half(k, c):
                dve.wait_ge(sem("xh_ready"), k * NC + c + 1)
                dve.tensor_tensor(xl[:, c], xn[:, c], xh[:, c].bitcast(F32), ALU.subtract
                                  ).then_inc(sem("xl_ready"), 1)

            def high_queries(l, lo, hi):
                for f in range(lo, hi):
                    w = (W_PQ0, W_PQ1)[l] + f
                    dve.wait_ge(sem(f"w_loaded{w % 2}"), 16 * (w // 2 + 1))
                    dve.wait_ge(sem("tile_done"), tiles_made(w - 2))
                    dve.tensor_copy(uh[:, w % 2], uraw[:, w % 2]).then_inc(sem("qh_ready"), 1)

            def norm_apply(off, k, lag=2):
                for c in range(NC + lag):
                    if c < NC:
                        dve.scalar_tensor_tensor(xn[:, c], xT[:, c], prm[:, off + c:off + c + 1],
                                                 rinv[:, :], ALU.mult, ALU.mult
                                                 ).then_inc(sem("x_whole" if k is not None else "y_ready"), 1)
                    if k is not None and c >= lag:
                        low_half(k, c - lag)

            def add_residual(d0):
                for f in range(NC):
                    dve.wait_ge(sem("tile_done"), d0 + f + 1)
                    dve.tensor_tensor(two(xT[:, f]), two(xT[:, f]), halves(dbank(d0 + f)), ALU.add
                                      ).then_inc(sem("d_free"), 1)

            def rg_lru():
                dve.wait_ge(sem("params_loaded"), 16)
                norm_stats(0)
                norm_apply(N_RG, X_IN)
                dve.wait_ge(sem("softplus_step"), 1)
                dve.tensor_scalar(sp[:, 1], sp[:, 0], 1.0, None, ALU.add).then_inc(sem("softplus_step"), 1)
                dve.wait_ge(sem("softplus_step"), 3)
                chain.did(dve.tensor_scalar(sp[:, 1], sp[:, 1], -1.0, None, ALU.add))
                chain.settle()
                chain.did(dve.tensor_scalar(sp[:, 3], sp[:, 1], 0.0, None, ALU.is_equal))
                chain.settle()
                chain.did(dve.tensor_tensor(sp[:, 1], sp[:, 1], sp[:, 3], ALU.add))
                chain.did(dve.tensor_tensor(sp[:, 2], sp[:, 2], sp[:, 3], ALU.add))
                chain.settle()
                chain.did(dve.reciprocal(sp[:, 1], sp[:, 1]))
                chain.settle()
                chain.did(dve.tensor_tensor(sp[:, 2], sp[:, 2], sp[:, 0], ALU.mult))
                chain.settle()
                dve.scalar_tensor_tensor(sp[:, 3], sp[:, 2], -8.0, sp[:, 1], ALU.mult, ALU.mult
                                         ).then_inc(sem("softplus_step"), 1)
                for f in range(NC):
                    dve.wait_ge(sem("pre_copied"), f + 1)
                    dve.wait_ge(sem("d_free"), D_IN + NC + f + 1)
                    outs = (xc[:, f, 0:TP], xc[:, f, TP:T].rearrange("p (b s) -> p b s", b=NB))

                    def tap(k):
                        return (xpre[:, f, k:k + TP], xpreS[:, f, :, k:k + TS])
                    for k in range(CW):
                        w = prm[:, P_CW + k * NC + f:P_CW + k * NC + f + 1]
                        for o, i in zip(outs, tap(k)):
                            if k == 0:
                                ins = dve.tensor_scalar(o, i, w, prm[:, P_CB + f:P_CB + f + 1],
                                                        ALU.mult, ALU.add)
                            else:
                                ins = dve.scalar_tensor_tensor(o, i, w, o, ALU.mult, ALU.add)
                            if k < CW - 1:
                                chain.did(ins)
                        if k < CW - 1:
                            chain.settle()
                    ins.then_inc(sem("xc_ready"), 1)
                for f in range(NC):
                    dve.wait_ge(sem("d_free"), D_X + f + 1)
                    chain.did(dve.tensor_tensor(ig[:, f], ig[:, f], xc[:, f], ALU.mult))
                for f in range(NC):
                    dve.wait_ge(sem("dec_ready"), f + 1)
                    chain.did(dve.tensor_tensor(xn[:, f], dec[:, f], dec[:, f], ALU.mult))
                chain.settle()
                starts = dec[:, :, TP:T].rearrange("p c (b s) -> p c b s", b=NB)[:, :, :, 0]
                bstarts = ig[:, :, TP:T].rearrange("p c (b s) -> p c b s", b=NB)[:, :, :, 0]
                chain.did(dve.tensor_tensor(ah0[:, :, :], starts,
                                            prm[:, P_H0:P_H0 + NC * NB].rearrange("p (c b) -> p c b", c=NC),
                                            ALU.mult))
                chain.settle()
                chain.did(dve.memset(starts, 0.0))
                for f in range(NC):
                    dve.wait_ge(sem("tanh_ready"), f + 1)
                    dve.scalar_tensor_tensor(rg[:, f], xn[:, f], 1.0, rg[:, f], ALU.add, ALU.mult
                                             ).then_inc(sem("m2_ready"), 1)

                lag = 4
                for f in range(NC + lag):
                    if f < NC:
                        dve.wait_ge(sem("mult_ready"), f + 1)
                        chain.did(dve.tensor_tensor(ig[:, f], ig[:, f], rg[:, f], ALU.mult))
                    if f >= lag:
                        low_half(X_OUT, f - lag)
                    if f < NC:
                        chain.settle()
                        chain.did(dve.tensor_tensor(bstarts[:, f], bstarts[:, f], ah0[:, f], ALU.add))
                        chain.settle()
                        dve.tensor_tensor_scan(rg[:, f], dec[:, f], ig[:, f], 0.0, ALU.mult, ALU.add
                                               ).then_inc(sem("scanned"), 1)
                dve.wait_ge(sem("scanned"), NC)
                chain.did(dve.tensor_copy(hlast[:, :, 0:1], rg[:, :, TP - 1:TP]))
                dve.tensor_copy(hlast[:, :, 1:1 + NB],
                                rg[:, :, TP:T].rearrange("p c (b s) -> p c b s", b=NB)[:, :, :, TS - 1]
                                ).then_inc(sem("hlast_ready"), 1)
                add_residual(D_OUT)
                dve.wait_ge(sem("d_free"), D_PQ0)
                dve.wait_ge(sem("states_out"), 48)
                dve.memset(mark[:, :], 0.0).then_inc(sem("x_ready"), 1)

            def topk(l):
                def tile(t):
                    dve.wait_ge(sem(f"sc_copied{l}"), t + 1)
                    for j in range(2 * PH):
                        chain.did(dve.max(sv[:, j, 0:8], sc[:, j]))
                    if t:
                        finish(t - 1)
                    chain.settle()
                    for j in range(2 * PH):
                        chain.did(dve.max_index(si[:, j, 0:8], sv[:, j, 0:8], sc[:, j]))
                        chain.did(dve.match_replace(sc2[:, j], sv[:, j, 0:8], sc[:, j], BIG))
                    chain.settle()
                    for j in range(2 * PH):
                        ins = dve.max(sv[:, j, 8:16], sc2[:, j])
                        if j < 2 * PH - 1:
                            chain.did(ins)
                    ins.then_inc(sem(f"sc_read{l}"), 1)
                    chain.settle()
                    dve.wait_ge(sem(f"sc_read{l}"), t + 1)
                    for j in range(2 * PH):
                        chain.did(dve.max_index(si[:, j, 8:16], sv[:, j, 8:16], sc2[:, j]))
                    s4 = sv[:, :, :].rearrange("p (h a) k -> p h a k", a=2)
                    chain.did(dve.tensor_tensor(
                        cand[:, :, :].rearrange("p h (i j) -> p h i j", i=TOPK),
                        s4[:, :, 0].unsqueeze(3).broadcast_to([P, PH, TOPK, TOPK]),
                        s4[:, :, 1].unsqueeze(2).broadcast_to([P, PH, TOPK, TOPK]), ALU.add))
                    chain.settle()
                    chain.did(dve.tensor_copy(sif[:, :, :], si[:, :, :]))
                    for h in range(PH):
                        chain.did(dve.max(cv[:, h, 0:8], cand[:, h]))
                    chain.settle()
                    for h in range(PH):
                        chain.did(dve.max_index(ci[:, h, 0:8], cv[:, h, 0:8], cand[:, h]))
                        chain.did(dve.match_replace(cand2[:, h], cv[:, h, 0:8], cand[:, h], BIG))
                    chain.settle()
                    for h in range(PH):
                        chain.did(dve.max(cv[:, h, 8:16], cand2[:, h]))
                    chain.settle()
                    dve.tensor_tensor(ex[:, :, :], cv[:, :, :], cv[:, :, 0:1].broadcast_to([P, PH, TOPK]),
                                      ALU.subtract).then_inc(sem(f"ex_in{l}"), 1)
                    for h in range(PH):
                        chain.did(dve.max_index(ci[:, h, 8:16], cv[:, h, 8:16], cand2[:, h]))
                    chain.settle()
                    chain.did(dve.tensor_scalar(cab[:, 0], ci[:, :, :], 4, None, ALU.logical_shift_right))
                    chain.did(dve.tensor_scalar(cab[:, 1], ci[:, :, :], TOPK - 1, None, ALU.bitwise_and))
                    chain.settle()
                    chain.did(dve.tensor_copy(cabf[:, :, :, :], cab[:, :, :, :]))
                    chain.settle()
                    f4 = sif[:, :, :].rearrange("p (h a) k -> p h a k", a=2)
                    eq = [b_[:, :, :].rearrange("p h (k i) -> p h k i", k=TOPK) for b_ in (cand, cand2)]
                    for a in range(2):
                        chain.did(dve.tensor_tensor(
                            eq[a], cabf[:, a].unsqueeze(3).broadcast_to([P, PH, TOPK, TOPK]),
                            iota[:, 0:TOPK].unsqueeze(1).unsqueeze(1).broadcast_to([P, PH, TOPK, TOPK]),
                            ALU.is_equal))
                    chain.settle()
                    for a in range(2):
                        chain.did(dve.tensor_tensor(
                            eq[a], eq[a], f4[:, :, a].unsqueeze(2).broadcast_to([P, PH, TOPK, TOPK]),
                            ALU.mult))
                    chain.settle()
                    if t > 1:
                        dve.wait_ge(sem(f"turned{l}"), t - 1)
                    for a in range(2):
                        chain.did(dve.tensor_reduce(slot[:, a].rearrange("p (h k) -> p h k", h=PH), eq[a],
                                                    X, ALU.add))

                def finish(t):
                    dve.wait_ge(sem(f"ex_out{l}"), t + 1)
                    chain.did(dve.tensor_reduce(exs[:, 0], ex[:, :, :], X, ALU.add))
                    chain.settle()
                    chain.did(dve.reciprocal(exs[:, 1], exs[:, 0]))
                    chain.settle()
                    ins = dve.tensor_tensor(slot[:, 2].rearrange("p (h k) -> p h k", h=PH), ex[:, :, :],
                                            exs[:, 1].unsqueeze(2).broadcast_to([P, PH, TOPK]), ALU.mult)
                    if t:
                        ins.then_inc(sem(f"slots{l}"), 1)
                        return
                    chain.did(ins)
                    chain.settle()
                    for e in range(2):
                        lanes, cols = slice(e * SMP, (e + 1) * SMP), slice(e * GATHERS, (e + 1) * GATHERS)
                        chain.did(dve.tensor_copy(pgate[lanes, :], slot[lanes, 2, cols]))
                        chain.did(dve.tensor_scalar(slot[lanes, 0, cols], slot[lanes, 0, cols], float(KEYS),
                                                    float(l * KEYS * KEYS), ALU.mult, ALU.add))
                    chain.settle()
                    for e in range(2):
                        lanes, cols = slice(e * SMP, (e + 1) * SMP), slice(e * GATHERS, (e + 1) * GATHERS)
                        dve.tensor_tensor(pick[lanes, :], slot[lanes, 0, cols], slot[lanes, 1, cols], ALU.add
                                          ).then_inc(sem(f"picked{l}"), 1)
                    dve.wait_ge(sem(f"picked{l}"), 2)

                for t in range(TT):
                    tile(t)
                finish(TT - 1)

            def one_hots(l):
                dve.wait_ge(sem(f"slot_ready{l}"), NU)

                def batch(it, first):
                    for q in range(4):
                        if not first:
                            dve.wait_ge(sem(f"g_done{l}"), it * 4 + (q - 3))
                        for i in range(4):
                            k = 4 * q + i

                            def col(a):
                                if isinstance(it, int):
                                    return slotT[:, a, it * 16 + k:it * 16 + k + 1]
                                return slotT[:, a, bass.ds(it * 16 + k, 1)]
                            dve.tensor_scalar(hotA[:, k], iota, col(0), None, ALU.is_equal)
                            ins = dve.tensor_scalar(hotB[:, k], iota, col(1), col(2), ALU.is_equal, ALU.mult)
                        ins.then_inc(sem(f"hot{l}"), 1)

                batch(0, True)
                with dve.Fori(1, TP // 16) as it:
                    batch(it, False)

            def output(l):
                def evac(g, c):
                    dve.wait_ge(sem(f"o_full{l}"), g * 8 + (c + 1))
                    dve.tensor_tensor(xT[:, c, 0:TP], xT[:, c, 0:TP], ps[:, 4 + c % 4, :], ALU.add
                                      ).then_inc(sem(f"o_free{l}"), 1)

                def row(g, j, c, phase):
                    k0 = (g - j - GA) * PICK
                    kk = j * PICK + c
                    r = kk % ROWS
                    before = 2 * GATHERS // ROWS * l
                    dve.wait_ge(sem(f"row_loaded{r}"),
                                (g - j - GA) * (16 * PICK // ROWS) + 16 * (before + kk // ROWS + 1))
                    if phase == "u":
                        dve.scalar_tensor_tensor(rows[:, r], rows[:, r], 1.0, xs[:, :], ALU.mult, ALU.mult,
                                                 accum_out=phid[:, bass.ds(k0 + kk, 1)]
                                                 ).then_inc(sem(f"row_used{l}"), 1)
                    else:
                        dve.wait_ge(sem(f"row_used{l}"), k0 + kk)
                        dve.scalar_tensor_tensor(accS[:, :], rows[:, r],
                                                 phid[:, bass.ds(k0 + (kk - GATHERS), 1)], accS[:, :],
                                                 ALU.mult, ALU.add).then_inc(sem(f"row_used{l}"), 1)

                def step(g, j, first, stored, phase=None):
                    def ev(c):
                        if not (first and j == 0):
                            evac(g - 1, c)
                        if phase:
                            row(g, j, c, phase)
                    for i in range(2):
                        ev(i)
                        if stored:
                            dve.wait_ge(sem(f"h_loaded{l}_{j}{i}"), (g - j) * 8 + 16)
                        else:
                            dve.wait_ge(sem(f"s_free{l}"), 2 * g + (i + 1))
                        dve.wait_ge(sem(f"gt_loaded{l}_{j}"), (g - j) * 8 + 16)
                        hb = hg[j][:, i].rearrange("p (b t) -> p b t", b=NGB)
                        dve.tensor_tensor(hb, hb, gt[:, j, :, i], ALU.mult).then_inc(sem(f"h_mul{l}"), 1)
                    for i in range(2):
                        ev(2 + i)
                    for i in range(2):
                        ev(4 + i)
                        dve.wait_ge(sem(f"hh_ready{l}"), 2 * g + (i + 1))
                        dve.tensor_tensor(hl[:, 2 * j + i], hg[j][:, i], hh[:, 2 * j + i].bitcast(F32),
                                          ALU.subtract).then_inc(sem(f"h_split{l}"), 1)
                    for i in range(2):
                        ev(6 + i)

                dve.wait_ge(sem(f"g_done{l}"), TP // 4)
                for j in range(2):
                    step(j, j, True, True)
                with dve.Fori(1, GA // 2) as it:
                    for j in range(2):
                        step(it * 2 + j, j, False, True)
                chain.did(dve.memset(accS[:, :], 0.0))
                chain.settle()
                dve.wait_ge(sem(f"xs_ready{l}"), 1)
                with dve.Fori(GA // 2, GU // 2) as it:
                    for j in range(2):
                        step(it * 2 + j, j, False, False, "u")
                dve.wait_ge(sem(f"phid_ready{l}"), 1)
                chain.did(dve.tensor_tensor(phid[:, :], phid[:, :], pgate[:, :], ALU.mult))
                chain.settle()
                with dve.Fori(GU // 2, GV // 2) as it:
                    for j in range(2):
                        step(it * 2 + j, j, False, False, "v")
                with dve.Fori(GV // 2, NG // 2) as it:
                    for j in range(2):
                        step(it * 2 + j, j, False, False)
                for c in range(NC):
                    evac(NG - 1, c)
                dve.wait_ge(sem("fold_done"), l + 1)
                dve.tensor_tensor(xT[:, :, TP:T], xT[:, :, TP:T], ps[:, 2, :].rearrange("p (c t) -> p c t", c=NC),
                                  ALU.add).then_inc(sem(f"o_free{l}"), 1)
                dve.wait_ge(sem(f"o_free{l}"), NG * NC + 1)
                dve.memset(mark[:, :], 0.0).then_inc(sem("x_ready"), 1)

            def rope(d0, n, dst):
                for f in range(n):
                    d = d0 + f
                    r = d % 2
                    dve.wait_ge(sem("rot_ready"), d - D_K + 1)
                    chain.did(dve.tensor_tensor(rot[:, r], rot[:, r], cst[:, C_SIN:C_SIN + T], ALU.mult))
                    dve.tensor_tensor(two(rc[:, r]), halves(dbank(d)), two(cst[:, C_COS:C_COS + T]), ALU.mult
                                      ).then_inc(sem("d_free"), 1)
                    chain.settle()
                    dve.wait_ge(sem("d_free"), d + 1)
                    chain.did(dve.tensor_tensor(dst[:, 2 * f], rc[0:HD, r], rot[0:HD, r], ALU.add))
                    ins = dve.tensor_tensor(dst[:, 2 * f + 1], rc[HD:P, r], rot[HD:P, r], ALU.add)
                    ins.then_inc(sem("roped"), 1)

            def attention():
                norm_stats(2)
                norm_apply(N_KV, X_KV)
                rope(D_K, 2, kR)
                dve.wait_ge(sem("roped"), 2)
                dve.wait_ge(sem("tile_done"), D_Q)
                dve.wait_ge(sem("v_done"), 1)
                dve.memset(mark[:, :], 0.0).then_inc(sem("k_ready"), 2)
                norm_apply(N_AT, X_AT)
                rope(D_Q, NC, qR)
                dve.wait_ge(sem("roped"), 2 + NC)
                dve.tensor_copy(qS[:, :, :, :], qR[:, :, TP:T].rearrange("p h (b s) -> p b h s", b=NB)
                                ).then_inc(sem("qS_ready"), 1)
                ob = xn
                dve.wait_ge(sem("tile_done"), D_O)
                U = NQB * NKV

                def scale_max(u):
                    n, kv = divmod(u, NKV)
                    p, m = pr[:, u % 2], sm[:, u % 2]
                    lo = 0 if n else WIN
                    w = 2 * WIN - lo
                    dve.wait_ge(sem("p_scores"), u + 1)
                    if u >= 2:
                        dve.wait_ge(sem("pturn"), u - 1)
                    chain.did(dve.scalar_tensor_tensor(
                        p[:, :, lo:], sbank(u).rearrange("p b (g k) -> p (b g) k", g=2)[:, :, lo:],
                        HD ** -0.5, cst[:, C_MP + lo:C_MP + 2 * WIN].unsqueeze(1).broadcast_to([P, GRP, w]),
                        ALU.mult, ALU.add))
                    if not n:
                        chain.did(dve.memset(p[:, :, 0:WIN], BIG))
                    chain.settle()
                    chain.did(dve.tensor_reduce(m[:, 0, 0:GRP], p, X, ALU.max))
                    chain.settle()
                    sk = prm[:, P_SINK + kv * GRP:P_SINK + (kv + 1) * GRP]
                    chain.did(dve.tensor_tensor(m[:, 0, 0:GRP], m[:, 0, 0:GRP], sk, ALU.max))
                    chain.settle()
                    chain.did(dve.tensor_scalar(m[:, 1, 0:GRP], m[:, 0, 0:GRP], -1.0, None, ALU.mult))
                    chain.settle()
                    dve.tensor_tensor(m[:, 3, 0:GRP], sk, m[:, 0, 0:GRP], ALU.subtract
                                      ).then_inc(sem("pmax"), 1)

                def normalise(u):
                    p, m = pr[:, u % 2], sm[:, u % 2]
                    dve.wait_ge(sem("pexp"), u + 1)
                    chain.did(dve.tensor_tensor(m[:, 4, 0:GRP], m[:, 2, 0:GRP], m[:, 3, 0:GRP], ALU.add))
                    chain.settle()
                    chain.did(dve.reciprocal(m[:, 5, 0:GRP], m[:, 4, 0:GRP]))
                    chain.settle()
                    dve.tensor_tensor(p, p, m[:, 5, 0:GRP].unsqueeze(2).broadcast_to([P, GRP, 2 * WIN]),
                                      ALU.mult).then_inc(sem("p_ready"), 1)

                def keep(u):
                    n, kv = divmod(u, NKV)
                    dve.wait_ge(sem("p_out"), u + 1)
                    for e in range(2):
                        ins = dve.tensor_copy(
                            ob[e * HD:(e + 1) * HD, 2 * kv:2 * kv + 2, n * WIN:(n + 1) * WIN],
                            ps[0:HD, 6 + u % 2, :].rearrange("p (g e q) -> p g e q", g=2, e=2)[:, :, e])
                        if e == 0:
                            chain.did(ins)
                    ins.then_inc(sem("o_copied"), 1)

                def sample_max():
                    dve.wait_ge(sem("s_scores"), 1)
                    for h in range(2):
                        chain.did(dve.scalar_tensor_tensor(
                            pss[:, 4 * h:4 * h + 4],
                            sbank(h).rearrange("p b (j k) -> p (b j) k", j=2)[:, :, 0:WIN + TS], HD ** -0.5,
                            cst[:, C_MS:C_MS + WIN + TS].unsqueeze(1).broadcast_to([P, NB // 2, WIN + TS]),
                            ALU.mult, ALU.add))
                    chain.settle()
                    chain.did(dve.tensor_reduce(sm[:, 0, 0], pss[:, :, :], X, ALU.max))
                    chain.settle()
                    chain.did(dve.tensor_scalar(sm[:, 0, 0], sm[:, 0, 0], prm[:, P_SKS:P_SKS + 1], None, ALU.max))
                    chain.settle()
                    chain.did(dve.tensor_scalar(sm[:, 0, 3], sm[:, 0, 0], -1.0, prm[:, P_SKS:P_SKS + 1], ALU.mult, ALU.add))
                    chain.settle()
                    dve.tensor_tensor(pss[:, :, :], pss[:, :, :],
                                      sm[:, 0, 0].unsqueeze(2).broadcast_to([P, NB, WIN + TS]), ALU.subtract
                                      ).then_inc(sem("smax"), 1)

                scale_max(0)
                scale_max(1)
                for u in range(U):
                    normalise(u)
                    if u + 2 < U:
                        scale_max(u + 2)
                    if u == U - 1:
                        sample_max()
                    if u:
                        keep(u - 1)
                keep(U - 1)
                dve.wait_ge(sem("sexp"), 2)
                chain.did(dve.tensor_reduce(sm[:, 0, 4], pss[:, :, :], X, ALU.add))
                chain.settle()
                chain.did(dve.tensor_tensor(sm[:, 0, 4], sm[:, 0, 4], sm[:, 0, 3], ALU.add))
                chain.settle()
                chain.did(dve.reciprocal(sm[:, 0, 5], sm[:, 0, 4]))
                chain.settle()
                dve.tensor_tensor(pss[:, :, :], pss[:, :, :],
                                  sm[:, 0, 5].unsqueeze(2).broadcast_to([P, NB, WIN + TS]), ALU.mult
                                  ).then_inc(sem("s_ready"), 1)
                dve.wait_ge(sem("s_out"), 1)
                for g in range(GRP):
                    e = g % 2
                    for bb in range(2):
                        ins = dve.tensor_copy(
                            ob[e * HD:(e + 1) * HD, :, TP:T].rearrange("p (k c) (b s) -> p c b k s", k=NKV, b=NB)
                            [:, g // 2, 4 * bb:4 * bb + 4],
                            ps[0:HD, bb, :].rearrange("p (b k g s) -> p g b k s", b=4, k=NKV, g=GRP)[:, g])
                        if g < GRP - 1 or bb == 0:
                            chain.did(ins)
                chain.did(ins)
                chain.settle()
                dve.memset(mark[:, :], 0.0).then_inc(sem("x_whole"), NC)
                for c in range(NC):
                    low_half(X_O, c)
                add_residual(D_O)
                dve.wait_ge(sem("d_free"), D_PQ1)
                dve.memset(mark[:, :], 0.0).then_inc(sem("x_ready"), 1)

            rg_lru()
            for l, (s, off) in enumerate(((1, N_F0), (3, N_F1))):
                if l == 1:
                    attention()
                high_queries(l, 0, 2)
                norm_stats(s)
                norm_apply(off, (X_F0, X_F1)[l])
                high_queries(l, 2, 2 * PH)
                topk(l)
                one_hots(l)
                output(l)
            norm_stats(4)
            norm_apply(N_FIN, None)

        @block.tensor
        def _(pe):
            def sum_squares(s):
                if s == 0:
                    pe.wait_ge(sem("ones_ready"), 1)
                pe.wait_ge(sem("sq_added"), NC - 2 + (NC - 2) * s)
                for c in range(2):
                    for h in range(2):
                        ins = pe.matmul(ps[:, 4 + h, 0:H2], ones[:, :], xn[:, c, h * H2:(h + 1) * H2],
                                        start=(c == 0), stop=(c == 1))
                ins.then_inc(sem("sum_done"), 1)

            def project(w0, d0, n, k):
                def tile(f, i, first):
                    w, d = w0 + f, d0 + f
                    pe.wait_ge(sem("w_split"), f + splits_made(w0))
                    if not (first and d0 + i < 2):
                        pe.wait_ge(sem("d_free"), d - 1)
                    for c in range(NC):
                        if first and i == 0:
                            pe.wait_ge(sem("xl_ready"), k * NC + c + 1)
                        for j, (a, x) in enumerate(((uh, xh), (uh, xl), (ul, xh))):
                            for h in range(2):
                                ins = pe.matmul(ps[:, 2 * i + h, 0:H2], a[:, i, c], x[:, c, h * H2:(h + 1) * H2],
                                                start=(c == 0 and j == 0), stop=(c == NC - 1 and j == 2))
                    ins.then_inc(sem("tile_done"), 1)

                for i in range(2):
                    tile(i, i, True)
                if n > 2:
                    with pe.Fori(1, n // 2) as it:
                        for i in range(2):
                            tile(it * 2 + i, i, False)

            def rg_gates():
                for w, d0 in ((W_A, D_A), (W_X, D_X)):
                    pe.wait_ge(sem(f"w_loaded{w % 2}"), 16 * (w // 2 + 1))
                    for f in range(NC):
                        d = d0 + f
                        pe.wait_ge(sem("xc_ready"), f + 1)
                        pe.wait_ge(sem("d_free"), d - 1)
                        for h in range(2):
                            ins = pe.matmul(ps[:, dbank(d) + h, 0:H2], uraw[:, w % 2, f],
                                            xc[:, f, h * H2:(h + 1) * H2], start=True, stop=True)
                        ins.then_inc(sem("tile_done"), 1)

            def up(l, n, i, fresh):
                pe.wait_ge(sem(f"u_split{l}"), n + 1)
                if not fresh:
                    pe.wait_ge(sem(f"s_free{l}"), n - 1)
                for c in range(NC):
                    for k, (w, x) in enumerate(((uh, xh), (uh, xl), (ul, xh))):
                        ins = pe.matmul(ps[:, i, :], w[:, i, c], x[:, c, 0:TP],
                                        start=(c == 0 and k == 0), stop=(c == NC - 1 and k == 2))
                ins.then_inc(sem(f"s_full{l}"), 1)

            def hidden(l):
                def scores(t):
                    if t:
                        pe.wait_ge(sem(f"sc_copied{l}"), t)
                    for j in range(2 * PH):
                        sk = prm[:, P_SK + (2 * l + j % 2) * KEYS:P_SK + (2 * l + j % 2 + 1) * KEYS]
                        o = ps[:, 4 + j // 4, (j % 4) * P:(j % 4 + 1) * P]
                        if t:
                            ins = pe.matmul(o, qT[:, j, (t - 1) * P:t * P], sk, start=True, stop=True)
                        else:
                            for e in range(2):
                                ins = pe.matmul(o[e * SMP:(e + 1) * SMP], qT[:, j, TP:T], sk,
                                                start=True, stop=True)
                    ins.then_inc(sem(f"sc_done{l}"), 1)

                def gates(n, first):
                    for q in range(4):
                        pe.wait_ge(sem(f"hot{l}"), (n - NA1) * 4 + (q + 1))
                        if not first:
                            pe.wait_ge(sem(f"g_copied{l}"), (n - NA1) * 4 + (q - 3))
                        elif q == 0:
                            pe.wait_ge(sem(f"slot_ready{l}"), NU)
                        for i in range(4):
                            k = 4 * q + i
                            ins = pe.matmul(ps[:, 4 + q, i * P:(i + 1) * P], hotB[:, k], hotA[:, k],
                                            start=True, stop=True)
                        ins.then_inc(sem(f"g_done{l}"), 1)

                def turn(t):
                    pe.wait_ge(sem(f"slots{l}"), t)
                    if t > 2:
                        pe.wait_ge(sem(f"slot_ready{l}"), t - 2)
                    elif t == 2:
                        pe.wait_ge(sem(f"xs_ready{l}"), 1)
                    for a in range(3):
                        ins = pe.transpose(ps[:, 2 + t % 2, a * P:(a + 1) * P], slot[:, a], ident)
                    ins.then_inc(sem(f"turned{l}"), 1)

                pe.wait_ge(sem("d_free"), (D_K, D_N)[l])
                for e in range(2):
                    for c in range(NC):
                        ins = pe.matmul(ps[e * SMP:(e + 1) * SMP, 2 + c // 4, (c % 4) * P:(c % 4 + 1) * P],
                                        xn[:, c, TP:T], ident, start=True, stop=True)
                ins.then_inc(sem(f"xs_done{l}"), 1)
                scores(0)
                n0 = 0
                for t in range(TT):
                    if t + 1 < TT:
                        scores(t + 1)
                    if t == 0:
                        for i in range(2):
                            up(l, i, i, True)
                    n1 = n0 + UB[t]
                    turn_at = n0 + 4
                    with pe.Fori(1 if t == 0 else n0 // 2, turn_at // 2) as it:
                        for i in range(2):
                            up(l, it * 2 + i, i, False)
                    if t > 1:
                        turn(t - 1)
                    with pe.Fori(turn_at // 2, n1 // 2) as it:
                        for i in range(2):
                            up(l, it * 2 + i, i, False)
                    n0 = n1
                turn(TT - 1)
                for i in range(4):
                    up(l, NA1 + i, i % 2, False)
                    gates(NA1 + i, i == 0)
                with pe.Fori((NA1 + 4) // 2, (NA1 + NA2) // 2) as it:
                    for i in range(2):
                        n = it * 2 + i
                        up(l, n, i, False)
                        gates(n, False)
                with pe.Fori((NA1 + NA2) // 2, NA // 2) as it:
                    for i in range(2):
                        up(l, it * 2 + i, i, False)

            def output(l):
                def down(g, j, first):
                    pe.wait_ge(sem(f"v_split{l}"), 2 * g + 2)
                    pe.wait_ge(sem(f"h_split{l}"), 2 * g + 2)
                    for c in range(NC):
                        if not (first and c < 4):
                            pe.wait_ge(sem(f"o_free{l}"), g * 8 + (c - 3))
                        for i in range(2):
                            for k, (w, x) in enumerate(((vh, hh), (vh, hl), (vl, hh))):
                                ins = pe.matmul(ps[:, 4 + c % 4, :], w[:, 2 * j + i, c * P:(c + 1) * P],
                                                x[:, 2 * j + i], start=(i == 0 and k == 0),
                                                stop=(i == 1 and k == 2))
                        ins.then_inc(sem(f"o_full{l}"), 1)

                def up_group(g):
                    for i in range(2):
                        up(l, 2 * g + i, i, False)

                pe.wait_ge(sem(f"g_copied{l}"), TP // 4)
                for j in range(2):
                    down(j, j, j == 0)
                with pe.Fori(1, GA // 2 - 1) as it:
                    for j in range(2):
                        down(it * 2 + j, j, False)
                down(GA - 2, 0, False)
                up_group(GA)
                down(GA - 1, 1, False)
                for lo, hi in ((GA // 2, GV // 2), (GV // 2, NG // 2 - 1)):
                    with pe.Fori(lo, hi) as it:
                        for j in range(2):
                            up_group(it * 2 + (j + 1))
                            down(it * 2 + j, j, False)
                    if lo == GA // 2:
                        pe.wait_ge(sem(f"row_used{l}"), 2 * GATHERS)
                        for c in range(NC):
                            ins = pe.matmul(ps[:, 2, c * SMP:(c + 1) * SMP], accS[:, c * P:(c + 1) * P],
                                            cst[:, C_FOLD:C_FOLD + SMP], start=True, stop=True)
                        ins.then_inc(sem("fold_done"), 1)
                up_group(NG - 1)
                down(NG - 2, 0, False)
                down(NG - 1, 1, False)

            def attention():
                project(W_K, D_K, 2, X_KV)
                pe.wait_ge(sem("wv_loaded"), 16)
                for t in range(TT):
                    m = min(P, T - t * P)
                    for c in range(NC):
                        ins = pe.matmul(ps[0:m, 4 + t // 2, (t % 2) * 256:(t % 2 + 1) * 256],
                                        xn[:, c, t * P:t * P + m], wv_sb[:, c], start=(c == 0), stop=(c == NC - 1))
                ins.then_inc(sem("v_done"), 1)
                project(W_Q, D_Q, NC, X_AT)
                pe.wait_ge(sem("roped"), 2 + NC)
                pe.wait_ge(sem("v_ready"), 1)
                U = NQB * NKV

                def scores(u):
                    n, kv = divmod(u, NKV)
                    ks = max(0, n - 1) * WIN
                    lo = 0 if n else WIN
                    if u >= 2:
                        pe.wait_ge(sem("pmax"), u - 1)
                    for g in range(GRP):
                        ins = pe.matmul(sbank(u)[:, g // 2, (g % 2) * 256 + lo:(g % 2 + 1) * 256],
                                        qR[:, kv * GRP + g, n * WIN:(n + 1) * WIN],
                                        kR[:, kv, ks:(n + 1) * WIN], start=True, stop=True)
                    ins.then_inc(sem("p_scores"), 1)

                def turn(u):
                    pe.wait_ge(sem("p_ready"), u + 1)
                    if u:
                        pe.wait_ge(sem("prT_ready"), u)
                    for kb in range(2):
                        for g in range(GRP):
                            ins = pe.transpose(ps[:, 2 + kb, g * P:(g + 1) * P],
                                               pr[:, u % 2, g, kb * WIN:(kb + 1) * WIN], ident)
                    ins.then_inc(sem("pturn"), 1)

                def mix(u):
                    n, kv = divmod(u, NKV)
                    pe.wait_ge(sem("prT_ready"), u + 1)
                    if u >= 2:
                        pe.wait_ge(sem("o_copied"), u - 1)
                    kbs = (0, 1) if n else (1,)
                    for kb in kbs:
                        ins = pe.matmul(ps[0:HD, 6 + u % 2, :], vtok[:, n - 1 + kb, kv * HD:(kv + 1) * HD],
                                        prT[:, u % 2, 4 * kb:4 * kb + 4].rearrange("p g q -> p (g q)"),
                                        start=(kb == kbs[0]), stop=(kb == 1))
                    ins.then_inc(sem("p_out"), 1)

                def sample_scores():
                    pe.wait_ge(sem("pmax"), U)
                    pe.wait_ge(sem("qS_ready"), 1)
                    pe.wait_ge(sem("kc_loaded"), 16)
                    pe.wait_ge(sem("vc_loaded"), 16)
                    pe.wait_ge(sem("vnew_loaded"), 16 * NB)
                    for b in range(NB):
                        for kv in range(NKV):
                            o = sbank(b // 4)[32 * kv:32 * kv + 32, b // 2 % 2, (b % 2) * 256:(b % 2) * 256 + WIN + TS]
                            q = qS[:, b, kv * GRP:(kv + 1) * GRP].rearrange("p g s -> p (g s)")
                            pe.matmul(o[:, 0:WIN], q, kc_sb[:, b, kv], start=True, stop=True)
                            ins = pe.matmul(o[:, WIN:], q, kR[:, kv, TP + b * TS:TP + (b + 1) * TS],
                                            start=True, stop=True)
                    ins.then_inc(sem("s_scores"), 1)

                scores(0)
                scores(1)
                for u in range(U):
                    if u + 2 < U:
                        scores(u + 2)
                    if u == U - 1:
                        sample_scores()
                    turn(u)
                    if u:
                        mix(u - 1)
                mix(U - 1)
                pe.wait_ge(sem("s_ready"), 1)
                pe.wait_ge(sem("o_copied"), NQB * NKV)
                for b in range(NB):
                    pe.transpose(ps[:, 4 + b // 4, (b % 4) * P:(b % 4 + 1) * P], pss[:, b, 0:WIN], ident)
                    ins = pe.transpose(ps[0:TS, 6 + b // 4, (b % 4) * P:(b % 4 + 1) * P], pss[:, b, WIN:], ident)
                ins.then_inc(sem("sturn"), 1)
                pe.wait_ge(sem("pssT_ready"), 1)
                for b in range(NB):
                    for kv in range(NKV):
                        o = ps[0:HD, b // 4, (b % 4) * P + 32 * kv:(b % 4) * P + 32 * kv + 32]
                        pe.matmul(o, vc_sb[:, b, kv * HD:(kv + 1) * HD], pssT[:, b, 32 * kv:32 * kv + 32],
                                  start=True, stop=False)
                        ins = pe.matmul(o, vnew[:, b, kv * HD:(kv + 1) * HD], pssN[:, b, 32 * kv:32 * kv + 32],
                                        start=False, stop=True)
                ins.then_inc(sem("s_out"), 1)
                project(W_O, D_O, NC, X_O)

            sum_squares(0)
            project(W_IN, D_IN, 2 * NC, X_IN)
            rg_gates()
            project(W_OUT, D_OUT, NC, X_OUT)
            for l in range(2):
                if l == 1:
                    sum_squares(2)
                    attention()
                sum_squares((1, 3)[l])
                project((W_PQ0, W_PQ1)[l], (D_PQ0, D_PQ1)[l], 2 * PH, (X_F0, X_F1)[l])
                hidden(l)
                output(l)
            sum_squares(4)


def _shape_constants():
    import numpy as np
    c = np.zeros((P, C_N), np.float32)
    c[:, C_ID:C_ID + P] = np.eye(P)
    c[:, C_IOTA:C_IOTA + P] = np.arange(P)
    half = HD // 2
    inv = np.float32(10000.0) ** (-np.arange(half, dtype=np.float32) / np.float32(half))
    pos = np.concatenate([np.arange(TP), np.tile(4096 + np.arange(TS), NB)]).astype(np.float32)
    ang = (inv[:, None] * pos[None, :]).astype(np.float32).astype(np.float64)
    cos, sin = np.cos(ang), np.sin(ang)
    c[:, C_COS:C_COS + T] = np.tile(cos, (4, 1))
    c[:, C_SIN:C_SIN + T] = np.concatenate([-sin, sin, -sin, sin])
    q = np.arange(P)[:, None]
    k = np.arange(WIN)[None, :]
    c[:, C_MP:C_MP + WIN] = np.where(k > q, 0, BIG)
    c[:, C_MP + WIN:C_MP + 2 * WIN] = np.where(k <= q, 0, BIG)
    s = q % TS
    c[:, C_MS:C_MS + WIN] = np.where(k > s, 0, BIG)
    c[:, C_MS + WIN:C_MS + WIN + TS] = np.where(np.arange(TS)[None, :] <= s, 0, BIG)
    c[:, C_FOLD:C_FOLD + SMP] = np.tile(np.eye(SMP), (2, 1))
    return c


def kernel(**inputs):
    import numpy as np
    import concourse.bacc as _bacc
    from concourse import mybir as _mybir
    from concourse.bass_utils import run_bass_kernel_spmd as _run

    a = {k: np.asarray(v) for k, v in inputs.items()}

    def chunks(vec):
        return vec.reshape(-1, P).T

    def tiles(w):
        return w.reshape(NC, P, -1, P).transpose(2, 1, 0, 3)

    xin = np.concatenate([a["x_prompt"].reshape(TP, D), a["x_sample"].reshape(NB * TS, D)])
    xin = xin.T.reshape(NC, P, T).transpose(1, 0, 2)
    gains = np.concatenate([a["rg_norm"].ravel(), a["ffn_norm"][0], a["kv_norm"], a["attn_norm"].ravel(),
                            a["ffn_norm"][1], a["final_norm"]])
    h0 = a["state_h"][0].reshape(NB, NC, P).transpose(2, 1, 0).reshape(P, NC * NB)
    sinks = a["sinks"].ravel()
    subkeys = a["peer_subkeys"].transpose(3, 0, 1, 2).reshape(P, 4 * KEYS)
    params = np.concatenate([
        chunks(gains), chunks(a["rg_conv_w"].ravel()), chunks(a["rg_conv_b"].ravel()),
        chunks(a["rg_ba"].ravel()), chunks(a["rg_bx"].ravel()), chunks(a["rg_lambda"].ravel()), h0,
        np.broadcast_to(sinks, (P, NH)), np.repeat(sinks, TS).reshape(P, 1), subkeys], axis=1)
    w_kv = a["w_kv"]
    wts = np.concatenate([
        tiles(a["rg_w_in"][0]), a["rg_wa"][0].transpose(1, 0, 2)[None], a["rg_wx"][0].transpose(1, 0, 2)[None],
        tiles(a["rg_w_out"][0]), tiles(a["peer_wq"][0]), tiles(w_kv[:, :NKV * HD]), tiles(a["w_q"][0]),
        tiles(a["w_o"][0]), tiles(a["peer_wq"][1])])
    arrays = {
        "xin": xin, "consts": _shape_constants(), "params": params, "wts": wts,
        "wv": w_kv[:, NKV * HD:].reshape(NC, P, NKV * HD).transpose(1, 0, 2),
        "stconv": a["state_conv"][0].reshape(NB, CW - 1, NC, P).transpose(3, 2, 0, 1).reshape(P, NC * NB, CW - 1),
        "kcT": a["cache_k"].transpose(3, 0, 2, 1),
        "kc": a["cache_k"].reshape(NB, WIN, NKV * HD),
        "vc": a["cache_v"].reshape(NB, WIN, NKV * HD).transpose(1, 0, 2),
        "uT": a["peer_u"].reshape(2, KEYS, KEYS, NC, P).transpose(0, 1, 4, 3, 2).reshape(2, KEYS, P, D),
        "u": a["peer_u"].reshape(2 * KEYS * KEYS, D),
        "v": a["peer_v"].reshape(2 * KEYS * KEYS, D),
    }
    arrays = {k: np.ascontiguousarray(x) for k, x in arrays.items()}
    outs = {
        "yT": (P, NC, T), "convP": (P, NC, CW - 1), "hOut": (P, NC, 1 + NB), "kNew": (HD, NKV, WIN + NB * TS),
        "vNewP": (P, NKV * HD), "vNewS": (NB * TS, NKV * HD), "kKeep": (NB, WIN - TS, NKV * HD),
        "vKeep": (NB, WIN - TS, NKV * HD), "convS": (P, NC * NB, CW - 1),
    }
    nc = _bacc.Bacc("TRN2", target_bir_lowering=False, num_devices=1)
    f32 = _mybir.dt.float32
    args = [nc.dram_tensor(k, x.shape, _mybir.dt.from_np(x.dtype), kind="ExternalInput").ap()
            for k, x in arrays.items()]
    args += [nc.dram_tensor(k, s, f32, kind="ExternalOutput").ap() for k, s in outs.items()]
    args.append(nc.dram_tensor("gate_dram", (2, NGB, P, KEYS * GB), f32, kind="Internal").ap())
    args.append(nc.dram_tensor("s_dram", (2, NA, P, TP), f32, kind="Internal").ap())
    decoder(nc, *args)
    r = _run(nc, [arrays], core_ids=[0]).results[0]

    y = r["yT"].transpose(2, 1, 0).reshape(T, D)
    convP = r["convP"].transpose(2, 1, 0).reshape(1, 1, CW - 1, D)
    convS = r["convS"].reshape(P, NC, NB, CW - 1).transpose(2, 3, 1, 0).reshape(1, NB, CW - 1, D)
    h = r["hOut"].transpose(2, 1, 0).reshape(1 + NB, D)
    kn = r["kNew"].transpose(2, 1, 0)
    ks = np.concatenate([r["kKeep"].reshape(NB, WIN - TS, NKV, HD), kn[WIN:].reshape(NB, TS, NKV, HD)], axis=1)
    vs = np.concatenate([r["vKeep"].reshape(NB, WIN - TS, NKV, HD), r["vNewS"].reshape(NB, TS, NKV, HD)], axis=1)
    return (y[:TP].reshape(1, TP, D), y[TP:].reshape(NB, TS, D), convP, h[:1].reshape(1, 1, D),
            kn[:WIN].reshape(1, WIN, NKV, HD), r["vNewP"].reshape(1, WIN, NKV, HD), convS,
            h[1:].reshape(1, NB, D), ks, vs)
```
